# Optimizing a Trainium2 kernel written in Bass

```python
import math
import jax, jax.numpy as jnp
from jax import lax
import numpy as np

D_MODEL = 2048
BATCH = 1
SEQ = 256
DEPTH = 1
DEC_BATCH = 1
DEC_SEQ = 256
PAST_LEN = 128

RET_HEADS = 8
RET_DK = 128
RET_DV = 128
RET_QK = RET_HEADS * RET_DK
RET_WIDTH = RET_HEADS * RET_DV
CHUNK = 128
DIFF_HEADS = 8
DIFF_DQK = 64
DIFF_DV = 128
DIFF_QK = DIFF_HEADS * 2 * DIFF_DQK
DIFF_WIDTH = DIFF_HEADS * DIFF_DV
Q_BLOCK = 128
MIX_WIDTH = RET_WIDTH + DIFF_WIDTH
P_IN = 2 * RET_QK + 2 * RET_WIDTH + 2 * DIFF_QK + DIFF_WIDTH
PEER_HEADS = 8
PEER_NKEYS = 128
PEER_N = PEER_NKEYS * PEER_NKEYS
PEER_QDIM = 256
PEER_TOPK = 16
TOKEN_BLOCK = 128
EPS = 1e-6

kernel_name = "hybrid_retention_diffattn_peer_encoder"

def _rmsnorm(x, w):
    xf = x.astype(jnp.float32)
    y = xf * lax.rsqrt(jnp.mean(xf * xf, axis=-1, keepdims=True) + EPS)
    return (y * w.astype(jnp.float32)).astype(x.dtype)

def _modulate(h, shift, scale):
    return h * (1 + scale[:, None, :]) + shift[:, None, :]

def _retention_direction(q, k, v, log_gamma, strict):
    b, nh, t, dk = q.shape
    dv = v.shape[-1]
    nc = t // CHUNK
    dt = q.dtype
    qc = q.reshape(b, nh, nc, CHUNK, dk)
    kc = k.reshape(b, nh, nc, CHUNK, dk)
    vc = v.reshape(b, nh, nc, CHUNK, dv)
    lg = log_gamma.astype(jnp.float32)[:, None]
    pos = jnp.arange(CHUNK, dtype=jnp.float32)
    rel = pos[:, None] - pos[None, :]
    mask = (rel > 0) if strict else (rel >= 0)
    intra_decay = jnp.where(mask[None], jnp.exp(lg[:, :, None] * jnp.maximum(rel, 0.0)[None]), 0.0).astype(dt)
    scores = jnp.einsum("bhncd,bhnsd->bhncs", qc, kc) * intra_decay[None, :, None]
    intra = jnp.einsum("bhncs,bhnsv->bhncv", scores, vc)
    k_decay = jnp.exp(lg * (CHUNK - pos)[None]).astype(dt)
    chunk_kv = jnp.einsum("bhnsd,hs,bhnsv->nbhdv", kc, k_decay, vc)
    chunk_decay = jnp.exp(lg[:, 0] * CHUNK).astype(dt)[None, :, None, None]

    def step(state, kv_c):
        return state * chunk_decay + kv_c, state

    _, prev = lax.scan(step, jnp.zeros((b, nh, dk, dv), dt), chunk_kv)
    q_decay = jnp.exp(lg * pos[None]).astype(dt)
    cross = jnp.einsum("bhncd,hc,nbhdv->bhncv", qc, q_decay, prev)
    return (intra + cross).reshape(b, nh, t, dv)

def _hybrid_mixer(h, w_in, w_out, ret_decay_fwd, ret_decay_bwd, ret_gn_w,
                  lam_q1, lam_k1, lam_q2, lam_k2, diff_subln_w, layer_idx):
    b, t, _ = h.shape
    f32 = jnp.float32
    proj = h @ w_in
    sizes = (RET_QK, RET_QK, RET_WIDTH, RET_WIDTH, DIFF_QK, DIFF_QK, DIFF_WIDTH)
    points = [int(p) for p in np.cumsum(sizes)[:-1]]
    rq, rk, rv, rg, dq, dk, dv = jnp.split(proj, points, axis=-1)

    def heads(z, nh, d):
        return z.reshape(b, t, nh, d).transpose(0, 2, 1, 3)

    q = heads(rq, RET_HEADS, RET_DK)
    k = heads(rk, RET_HEADS, RET_DK) * (RET_DK ** -0.5)
    v = heads(rv, RET_HEADS, RET_DV)
    lg_f = jax.nn.log_sigmoid(ret_decay_fwd.astype(f32))
    lg_b = jax.nn.log_sigmoid(ret_decay_bwd.astype(f32))
    o_f = _retention_direction(q, k, v, lg_f, False)
    o_b = jnp.flip(_retention_direction(jnp.flip(q, 2), jnp.flip(k, 2), jnp.flip(v, 2), lg_b, True), 2)
    o = (o_f + o_b).astype(f32)
    mu = jnp.mean(o, axis=-1, keepdims=True)
    var = jnp.mean(jnp.square(o - mu), axis=-1, keepdims=True)
    o = (o - mu) * lax.rsqrt(var + EPS)
    o = o.transpose(0, 2, 1, 3).reshape(b, t, RET_WIDTH) * ret_gn_w.astype(f32)
    ret_out = (jax.nn.silu(rg.astype(f32)) * o).astype(h.dtype)

    lam_init = 0.8 - 0.6 * math.exp(-0.3 * layer_idx)
    lam = (jnp.exp(jnp.sum(lam_q1.astype(f32) * lam_k1.astype(f32)))
           - jnp.exp(jnp.sum(lam_q2.astype(f32) * lam_k2.astype(f32))) + lam_init)
    qd = dq.reshape(b, t, DIFF_HEADS, 2, DIFF_DQK).transpose(0, 2, 3, 1, 4)
    kd = dk.reshape(b, t, DIFF_HEADS, 2, DIFF_DQK).transpose(0, 2, 3, 1, 4)
    vd = heads(dv, DIFF_HEADS, DIFF_DV)
    nq = t // Q_BLOCK
    qb = jnp.moveaxis(qd.reshape(b, DIFF_HEADS, 2, nq, Q_BLOCK, DIFF_DQK), 3, 0)
    slopes = 2.0 ** (-8.0 * jnp.arange(1, DIFF_HEADS + 1, dtype=f32) / DIFF_HEADS)
    kpos = jnp.arange(t, dtype=f32)

    def attend(args):
        qi, start = args
        s = jnp.einsum("bhmqd,bhmkd->bhmqk", qi, kd).astype(f32) * (DIFF_DQK ** -0.5)
        qpos = start.astype(f32) + jnp.arange(Q_BLOCK, dtype=f32)
        dist = jnp.abs(qpos[:, None] - kpos[None, :])
        s = s - slopes[None, :, None, None, None] * dist[None, None, None]
        p = jax.nn.softmax(s, axis=-1)
        a = p[:, :, 0] - lam * p[:, :, 1]
        return jnp.einsum("bhqk,bhkv->bhqv", a.astype(vd.dtype), vd)

    od = lax.map(attend, (qb, jnp.arange(nq, dtype=jnp.int32) * Q_BLOCK))
    od = jnp.moveaxis(od, 0, 2).reshape(b, DIFF_HEADS, t, DIFF_DV).astype(f32)
    od = od * lax.rsqrt(jnp.mean(od * od, axis=-1, keepdims=True) + EPS) * diff_subln_w.astype(f32) * (1.0 - lam_init)
    diff_out = od.transpose(0, 2, 1, 3).reshape(b, t, DIFF_WIDTH).astype(h.dtype)

    return jnp.concatenate([ret_out, diff_out], axis=-1) @ w_out

def _peer(h, w_query, sub_keys, u_tab, v_tab):
    b, t, d = h.shape
    xf = h.reshape(b * t // TOKEN_BLOCK, TOKEN_BLOCK, d)

    def block(xb):
        q = (xb @ w_query).reshape(TOKEN_BLOCK, PEER_HEADS, 2, PEER_QDIM // 2)
        s = jnp.einsum("nhpd,hpkd->nhpk", q, sub_keys).astype(jnp.float32)
        sv, si = lax.top_k(s, PEER_TOPK)
        cand = sv[:, :, 0, :, None] + sv[:, :, 1, None, :]
        cidx = si[:, :, 0, :, None] * PEER_NKEYS + si[:, :, 1, None, :]
        cand = cand.reshape(TOKEN_BLOCK, PEER_HEADS, PEER_TOPK * PEER_TOPK)
        cidx = cidx.reshape(TOKEN_BLOCK, PEER_HEADS, PEER_TOPK * PEER_TOPK)
        top_s, top_pos = lax.top_k(cand, PEER_TOPK)
        eidx = jnp.take_along_axis(cidx, top_pos, axis=-1).reshape(TOKEN_BLOCK, PEER_HEADS * PEER_TOPK)
        g = jax.nn.softmax(top_s, axis=-1).reshape(TOKEN_BLOCK, PEER_HEADS * PEER_TOPK)
        u = u_tab[eidx]
        hid = jax.nn.gelu(jnp.einsum("nd,ned->ne", xb, u), approximate=False)
        w = (g * hid.astype(jnp.float32)).astype(xb.dtype)
        return jnp.einsum("ne,ned->nd", w, v_tab[eidx])

    return lax.map(block, xf).reshape(b, t, d)

def _layer(x, c, l, ada_w, ada_b, mix_pre_w, mix_post_w, ffn_pre_w, ffn_post_w,
           w_in, w_out, ret_decay_fwd, ret_decay_bwd, ret_gn_w,
           diff_lambda_q1, diff_lambda_k1, diff_lambda_q2, diff_lambda_k2, diff_subln_w,
           peer_w_query, peer_sub_keys, peer_u, peer_v):
    mod = jax.nn.silu(c) @ ada_w[l] + ada_b[l]
    sh1, sc1, g1, sh2, sc2, g2 = jnp.split(mod, 6, axis=-1)
    h = _modulate(_rmsnorm(x, mix_pre_w[l]), sh1, sc1)
    o = _hybrid_mixer(h, w_in[l], w_out[l], ret_decay_fwd[l], ret_decay_bwd[l], ret_gn_w[l],
                      diff_lambda_q1[l], diff_lambda_k1[l], diff_lambda_q2[l], diff_lambda_k2[l],
                      diff_subln_w[l], l)
    x = x + g1[:, None, :] * _rmsnorm(o, mix_post_w[l])
    h = _modulate(_rmsnorm(x, ffn_pre_w[l]), sh2, sc2)
    o = _peer(h, peer_w_query[l], peer_sub_keys[l], peer_u[l], peer_v[l])
    return x + g2[:, None, :] * _rmsnorm(o, ffn_post_w[l])

def setup_inputs(seed: int = 0) -> dict:
    key = jax.random.key(seed)
    ks = jax.random.split(key, 32)
    f32 = jnp.float32
    nrm = lambda k, shape, s: jax.random.normal(k, shape, f32) * s
    base_logit = jnp.log(2.0 ** (5.0 + jnp.arange(RET_HEADS, dtype=f32)) - 1.0)
    return {
        "x_prompt": nrm(ks[0], (BATCH, SEQ, D_MODEL), 1.0),
        "x_sample": nrm(ks[1], (DEC_BATCH, DEC_SEQ, D_MODEL), 1.0),
        "c_prompt": nrm(ks[2], (BATCH, D_MODEL), 1.0),
        "c_sample": nrm(ks[3], (DEC_BATCH, D_MODEL), 1.0),
        "ada_w": nrm(ks[4], (DEPTH, D_MODEL, 6 * D_MODEL), 0.5 * D_MODEL ** -0.5),
        "ada_b": nrm(ks[5], (DEPTH, 6 * D_MODEL), 0.02),
        "mix_pre_w": 1.0 + nrm(ks[6], (DEPTH, D_MODEL), 0.02),
        "mix_post_w": 1.0 + nrm(ks[7], (DEPTH, D_MODEL), 0.02),
        "ffn_pre_w": 1.0 + nrm(ks[8], (DEPTH, D_MODEL), 0.02),
        "ffn_post_w": 1.0 + nrm(ks[9], (DEPTH, D_MODEL), 0.02),
        "w_in": nrm(ks[10], (DEPTH, D_MODEL, P_IN), D_MODEL ** -0.5),
        "w_out": nrm(ks[11], (DEPTH, MIX_WIDTH, D_MODEL), MIX_WIDTH ** -0.5),
        "ret_decay_fwd": base_logit[None] + nrm(ks[12], (DEPTH, RET_HEADS), 0.1),
        "ret_decay_bwd": base_logit[None] + nrm(ks[13], (DEPTH, RET_HEADS), 0.1),
        "ret_gn_w": 1.0 + nrm(ks[14], (DEPTH, RET_WIDTH), 0.02),
        "diff_lambda_q1": nrm(ks[15], (DEPTH, DIFF_DQK), 0.1),
        "diff_lambda_k1": nrm(ks[16], (DEPTH, DIFF_DQK), 0.1),
        "diff_lambda_q2": nrm(ks[17], (DEPTH, DIFF_DQK), 0.1),
        "diff_lambda_k2": nrm(ks[18], (DEPTH, DIFF_DQK), 0.1),
        "diff_subln_w": 1.0 + nrm(ks[19], (DEPTH, DIFF_DV), 0.02),
        "peer_w_query": nrm(ks[20], (DEPTH, D_MODEL, PEER_HEADS * PEER_QDIM), D_MODEL ** -0.5),
        "peer_sub_keys": nrm(ks[21], (DEPTH, PEER_HEADS, 2, PEER_NKEYS, PEER_QDIM // 2), (PEER_QDIM // 2) ** -0.5),
        "peer_u": nrm(ks[22], (DEPTH, PEER_N, D_MODEL), D_MODEL ** -0.5),
        "peer_v": nrm(ks[23], (DEPTH, PEER_N, D_MODEL), D_MODEL ** -0.5),
    }

def reference(x_prompt, x_sample, c_prompt, c_sample, ada_w, ada_b, mix_pre_w, mix_post_w,
              ffn_pre_w, ffn_post_w, w_in, w_out, ret_decay_fwd, ret_decay_bwd, ret_gn_w,
              diff_lambda_q1, diff_lambda_k1, diff_lambda_q2, diff_lambda_k2, diff_subln_w,
              peer_w_query, peer_sub_keys, peer_u, peer_v):
    def run(x, c):
        for l in range(DEPTH):
            x = _layer(x, c, l, ada_w, ada_b, mix_pre_w, mix_post_w, ffn_pre_w, ffn_post_w,
                       w_in, w_out, ret_decay_fwd, ret_decay_bwd, ret_gn_w,
                       diff_lambda_q1, diff_lambda_k1, diff_lambda_q2, diff_lambda_k2, diff_subln_w,
                       peer_w_query, peer_sub_keys, peer_u, peer_v)
        return x

    y_prompt = run(x_prompt, c_prompt)
    y_sample = run(x_sample, c_sample)
    return (y_prompt, y_sample)


_drawn_inputs = setup_inputs


def setup_inputs(seed=0):
    import zlib

    import numpy as np

    out = dict(_drawn_inputs(seed))
    spreads = {}
    factors = {'ffn_post_w': 8.0, 'ret_gn_w': 2.908}
    for name, (base, spread) in spreads.items():
        noise = np.random.default_rng([zlib.crc32(name.encode()), seed]).standard_normal(out[name].shape)
        drawn = base * np.exp(spread * noise) if base else spread * noise
        out[name] = __import__('jax').numpy.asarray(drawn.astype(out[name].dtype))
    for name, factor in factors.items():
        out[name] = (out[name] * factor).astype(out[name].dtype)
    return out
```

```python
import math
import numpy as np

P = 128
D = 2048
KD = D // P
SEQ = 256
GROUPS = 2
TPG = SEQ // P
NT = GROUPS * TPG
T = NT * P
HEADS = 8
DQK = 64
MODS = 6
NB = 512
ADA_BLOCKS = MODS * D // NB
EPS = 1e-6
LAM_INIT = 0.8 - 0.6 * math.exp(-0.3 * 0)
PEER_HEADS = 8
NKEYS = 128
TOPK = 16
SLOTS = PEER_HEADS * TOPK
BATCH = 4
BATCHES = SLOTS // BATCH
WOC = 256
RSQRT_MAGIC = 0x5F3759DF
LOWEST = -3.0e38


def build_program(nc, x, ct, ada_w, ada_b, rows, w_t, w_v, w_o, w_q, keys_t, decay, lams, post1, pre2, post2,
                  u_tab, v_tab, ident_c, dist_c, alibi_c, iota_c, out, mod_d):
    import concourse.bass as bass
    from concourse import mybir
    from contextlib import ExitStack

    f32, i32, u32 = mybir.dt.float32, mybir.dt.int32, mybir.dt.uint32
    ALU, ACT, AX = mybir.AluOpType, mybir.ActivationFunctionType, mybir.AxisListType.X
    ds = bass.ds

    with ExitStack() as ctx:
        def sbuf(name, shape, dtype=f32):
            return ctx.enter_context(nc.sbuf_tensor("sb_" + name, shape, dtype))

        def semaphore(name):
            return ctx.enter_context(nc.semaphore(name))

        big_x = sbuf("x", [P, NT * D])
        big_h = sbuf("h", [P, NT * D])
        big_m = sbuf("m", [P, NT * D])
        big_w = sbuf("w", [P, 14336])
        small = sbuf("small", [P, 11264])
        ident = sbuf("ident", [P, P])
        cols = sbuf("cols", [P, 96])
        tiny = sbuf("tiny", [P, 512])

        x_sb = big_x[:, :].rearrange("p (t d) -> p t d", t=NT)
        h_t = big_h[:, :].rearrange("p (k t) -> p k t", k=KD)
        o_sb = big_h[:, :].rearrange("p (t d) -> p t d", t=NT)
        mix_t = big_m[:, :].rearrange("p (k t) -> p k t", k=KD)
        slab_t = big_w[:, 0:8192].rearrange("p (k c) -> p k c", k=KD)
        slab_v = big_w[:, 8192:14336].rearrange("p (k c) -> p k c", k=KD)

        def carver(arena):
            at = [0]

            def take(n):
                at[0] += n
                assert at[0] <= arena.shape[1], at[0]
                return arena[:, at[0] - n:at[0]]
            return take

        take = carver(small)
        k_t, q_t, dk_t, dq_t = (take(T) for _ in range(4))
        vd = take(NT * 2 * P).rearrange("p (t m c) -> p t m c", t=NT, m=2)
        e_g = take(NT * P).rearrange("p (t c) -> p t c", t=NT)
        gate = take(NT * P).rearrange("p (t c) -> p t c", t=NT)
        dist = take(2 * 384).rearrange("p (s u) -> p s u", s=2)
        decay_log = take(384)
        decay_tab = take(384)
        ret_p = take(GROUPS * 512).rearrange("p (g s t) -> p g s t", g=GROUPS, s=TPG)
        soft = take(4 * 512).rearrange("p (u m k) -> p u m k", u=4, m=2)
        attn = take(4 * SEQ).rearrange("p (u k) -> p u k", u=4)
        attn_t = take(4 * SEQ).rearrange("p (u s q) -> p u s q", u=4, s=TPG)
        alibi = take(2 * SEQ).rearrange("p (t k) -> p t k", t=TPG)
        take = carver(small)
        eidx = take(NT * SLOTS).bitcast(u32).rearrange("p (t s) -> p t s", t=NT)
        gates = take(NT * SLOTS).rearrange("p (t s) -> p t s", t=NT)
        keys_sb = take(2 * PEER_HEADS * NKEYS)
        qt_sb = take(2 * T).rearrange("p (m t) -> p m t", m=2)
        masked = take(NT * 256).rearrange("p (t j) -> p t j", t=NT)
        cand = take(NT * 256).rearrange("p (t j) -> p t j", t=NT)
        onehot = take(NT * 256)
        mod_rows = small[0:GROUPS, 0:3 * NB].rearrange("g (r n) -> g r n", r=3)
        cols_in = small[:, 6 * NB + 256:6 * NB + 384]
        lam_in = small[:, 6 * NB:6 * NB + 4 * DQK].rearrange("p (v d) -> p v d", v=4)
        bias_rows = small[0:GROUPS, 3 * NB:6 * NB].rearrange("g (r n) -> g r n", r=3)
        ada_ring = [big_w[:, 0:8192], big_m[:, :], big_h[:, :]]
        ada_ring = [a.rearrange("p (k n) -> p k n", k=KD) for a in ada_ring]
        wo_ring = [big_w[:, i * KD * WOC:(i + 1) * KD * WOC].rearrange("p (k n) -> p k n", k=KD) for i in range(2)]
        post1_sb, pre2_sb = (big_w[:, i * D:(i + 1) * D] for i in (0, 1))
        gate1_sb, scale2_sb, shift2_sb = (big_w[:, i * D:(i + 1) * D] for i in (4, 5, 6))
        wq_ring = [big_w[:, 4096:8192], big_w[:, 8192:12288]]
        wq_ring = [w.rearrange("p (k n) -> p k n", k=KD) for w in wq_ring]
        h2_t = mix_t
        u_ring = big_m[:, :].rearrange("p (r d) -> p r d", r=BATCH)
        v_ring = big_w[:, 0:BATCH * D].rearrange("p (r d) -> p r d", r=BATCH)
        gate2_sb, post2_sb, out_sb = (big_w[:, i * D:(i + 1) * D] for i in range(BATCH, BATCH + 3))

        take = carver(tiny)
        ss_x = take(8)
        rstd_x = take(8)
        nt_a, nt_b, nt_y = take(8), take(8), take(8)
        silu_c = take(2 * KD)
        silu_e = take(2 * KD)
        lg_all = take(2 * HEADS)
        lg_t = [take(2 * HEADS) for _ in range(3)]
        lg_h = take(2)
        lam_dot = take(4)
        lam = take(2)
        bn6 = take(NT * 6).rearrange("p (t s) -> p t s", t=NT)
        mv = take(NT * 2).rearrange("p (t s) -> p t s", t=NT)
        nmax = take(4 * 2).rearrange("p (u m) -> p u m", u=4)
        esum = take(4 * 2).rearrange("p (u m) -> p u m", u=4)
        coef = take(4 * 2).rearrange("p (u m) -> p u m", u=4)
        iota16 = take(16)
        stage_u = [take(BATCH).bitcast(u32) for _ in range(2)]
        stage_v = [take(BATCH).bitcast(u32) for _ in range(2)]
        hid = take(BATCH)
        hid_whole = take(BATCH)
        act_h = take(BATCH)
        w_slot = take(BATCH)
        ss_out = take(4)
        dif_ss = take(4)
        sub_w = take(1)
        take = carver(sbuf("ret_out", [P, 8 * P]))
        ret_o = take(NT * P).rearrange("p (t c) -> p t c", t=NT)
        diff_o = take(NT * P).rearrange("p (t c) -> p t c", t=NT)
        take = carver(sbuf("tops", [P, 896]))
        top_v = take(2 * NT * TOPK).rearrange("p (m t k) -> p m t k", m=2, t=NT)
        top_i = take(2 * NT * TOPK).bitcast(u32).rearrange("p (m t k) -> p m t k", m=2, t=NT)
        top_if = take(2 * NT * TOPK).rearrange("p (m t k) -> p m t k", m=2, t=NT)
        best_v = take(NT * TOPK).rearrange("p (t k) -> p t k", t=NT)
        best_p = take(NT * TOPK).bitcast(u32).rearrange("p (t k) -> p t k", t=NT)
        part_u = take(NT * TOPK).bitcast(u32)
        part_f = take(NT * TOPK)
        pick = take(2 * NT * TOPK).rearrange("p (m t k) -> p m t k", m=2, t=NT)
        soft_e = take(NT * TOPK)

        psum = ctx.enter_context(nc.psum_tensor("ps_all", [P, 8 * NB], f32))

        def bank(i):
            return psum[:, i * NB:(i + 1) * NB]

        names = """consts rows_in x_in cols_in sumsq silu_e silu colsT cols_ev a1_cols lg_e lam_e lg_rdy
            ada_in0 ada_in1 ada_in2 ada_mm ada_row mod_out0 mod_out1 mod_out2 xs xtr xtr_act xtr_dve
            w_t_in w_v_in alibi_in proj proj_ev gate
            dlog dtab ret_s ret_pd ret_v ret_n dif_s dif_sd dif_m dif_e dif_c dif_t dif_te dif_v dif_sq dif_n out_t out_te
            wo_in0 wo_in1 wo_mm wo_act wo_dve coef_in o_sq x1 x1_sq h2 grp_done h2tr h2tr_ev
            wq_in0 wq_in1 key_in q_mm q_ev sc_mm sc_dve gl_in gl_exp eidx_rdy
            stage u_in0 u_in1 u_in2 u_in3 v_in0 v_in1 v_in2 v_in3 u_dot hid v_acc gelu w_rdy g2_in h2_ps acc_sq y y_out
            dve act spare""".split()
        S = {n: semaphore("s_" + n) for n in names}

        block = ctx.enter_context(nc.Block())

        def wait(eng, name, value):
            if not isinstance(value, int) or value > 0:
                eng.wait_ge(S[name], value)

        def wait_alone(eng, name, value):
            wait(eng, name, value)
            eng.sem_inc(S["spare"], 1)

        PRE1, GN, SUB = 4 * KD, 5 * KD, 5 * KD + HEADS
        MOD_ROWS = 2 * 2 * KD

        def groups_of(unit):
            return unit // TPG, unit % TPG

        @block.sync
        def _(sp):
            sp.dma_start(silu_c, ct).then_inc(S["consts"], 16)
            sp.dma_start(ident[:, :], ident_c).then_inc(S["consts"], 16)
            sp.dma_start(iota16, iota_c).then_inc(S["consts"], 16)
            sp.dma_start(lg_all, decay.partition_broadcast(P)).then_inc(S["rows_in"], 16)
            sp.dma_start(lam_in, lams.partition_broadcast(P)).then_inc(S["rows_in"], 16)
            sp.dma_start(cols_in[MOD_ROWS:MOD_ROWS + KD + HEADS + 1, :], rows).then_inc(S["cols_in"], 16)

            def ada_load(n, r):
                sp.dma_start(ada_ring[r], ada_w[ds(n, 1)].rearrange("a p k n -> p (a k) n")).then_inc(S[f"ada_in{r}"], 16)
                sp.dma_start(bias_rows[:, r, :], ada_b[:, ds(n * NB, NB)].partition_broadcast(GROUPS)).then_inc(S[f"ada_in{r}"], 16)

            def mod_store(n, r):
                sp.wait_ge(S["ada_row"], n + 1)
                sp.dma_start(mod_d[:, ds(n * NB, NB)], mod_rows[:, r, :]).then_inc(S[f"mod_out{r}"], 16)

            for r in range(3):
                ada_load(r, r)
            for t in range(NT):
                sp.dma_start(x_sb[:, t, :], x[t * P:(t + 1) * P, :]).then_inc(S["x_in"], 16)
            with sp.Fori(0, ADA_BLOCKS // 3 - 1) as i:
                for r in range(3):
                    mod_store(i * 3 + r, r)
                    ada_load(i * 3 + r + 3, r)
            for r in range(3):
                mod_store(ADA_BLOCKS - 3 + r, r)
            for r in range(3):
                sp.wait_ge(S[f"mod_out{r}"], 16 * (ADA_BLOCKS // 3))
            for g in range(GROUPS):
                sp.dma_start(cols_in[g * 2 * KD:(g + 1) * 2 * KD, :],
                             mod_d[g, 0:2 * D].rearrange("(r c) -> r c", c=P)).then_inc(S["cols_in"], 16)

            def slab_loads(h):
                wait(sp, "proj", 8 * (h - 1) + 4)
                sp.dma_start(slab_t, w_t[ds(h, 1)].rearrange("a p k n -> p (a k) n")).then_inc(S["w_t_in"], 16)
                wait(sp, "dif_sd", 4 * (h - 1))
                if isinstance(h, int) and h == 0:
                    return
                sp.dma_start(alibi, alibi_c[ds(h - 1, 1)].rearrange("a p t k -> p (a t) k")).then_inc(S["alibi_in"], 16)
                wait(sp, "proj", 8 * (h - 1) + 8)
                sp.dma_start(slab_v, w_v[ds(h, 1)].rearrange("a p k n -> p (a k) n")).then_inc(S["w_v_in"], 16)

            slab_loads(0)
            sp.dma_start(slab_v, w_v[0]).then_inc(S["w_v_in"], 16)
            sp.wait_ge(S["cols_ev"], 1)
            sp.wait_ge(S["lg_rdy"], 1)
            sp.dma_start(dist, dist_c).then_inc(S["rows_in"], 16)
            slab_loads(1)
            with sp.Fori(2, HEADS) as h:
                slab_loads(h)
            sp.wait_ge(S["dif_sd"], 4 * (HEADS - 1))
            sp.dma_start(alibi, alibi_c[HEADS - 1]).then_inc(S["alibi_in"], 16)

            def wo_load(n, r):
                sp.dma_start(wo_ring[r], w_o[ds(n, 1)].rearrange("a p k n -> p (a k) n")).then_inc(S[f"wo_in{r}"], 16)

            sp.wait_ge(S["proj"], 8 * HEADS)
            for r in range(2):
                wo_load(r, r)

            def coef_load(g):
                for dst, v in ((gate1_sb, 2), (shift2_sb, 3), (scale2_sb, 4)):
                    sp.dma_start(dst, mod_d[g:g + 1, v * D:(v + 1) * D].partition_broadcast(P)).then_inc(S["coef_in"], 16)

            coef_load(0)
            with sp.Fori(1, D // WOC // 2) as i:
                for r in range(2):
                    sp.wait_ge(S["wo_mm"], (i * 2 + r - 1) * NT)
                    wo_load(i * 2 + r, r)
            sp.wait_ge(S["wo_mm"], D // WOC * NT)
            sp.dma_start(post1_sb, post1.partition_broadcast(P)).then_inc(S["coef_in"], 16)
            sp.dma_start(pre2_sb, pre2.partition_broadcast(P)).then_inc(S["coef_in"], 16)
            sp.dma_start(wq_ring[0], w_q[0]).then_inc(S["wq_in0"], 16)
            sp.dma_start(keys_sb, keys_t).then_inc(S["key_in"], 16)
            sp.wait_ge(S["grp_done"], 1)
            coef_load(1)
            sp.wait_ge(S["grp_done"], 2)
            sp.dma_start(wq_ring[1], w_q[1]).then_inc(S["wq_in1"], 16)
            with sp.Fori(1, PEER_HEADS // 2) as i:
                for r in range(2):
                    sp.wait_ge(S["q_mm"], 2 * (i * 2 + r - 1))
                    sp.dma_start(wq_ring[r], w_q[ds(i * 2 + r, 1)].rearrange("a p k n -> p (a k) n")).then_inc(S[f"wq_in{r}"], 16)

            sp.wait_ge(S["q_mm"], 2 * PEER_HEADS)
            sp.dma_start(post2_sb, post2.partition_broadcast(P)).then_inc(S["rows_in"], 16)
            for t in range(NT):
                g = t // TPG
                sp.dma_start(gate2_sb, mod_d[g:g + 1, 5 * D:6 * D].partition_broadcast(P)).then_inc(S["g2_in"], 16)
                sp.wait_ge(S["y"], t + 2)
                sp.dma_start(out[t * P:(t + 1) * P, :], out_sb).then_inc(S["y_out"], 16)
            sp.wait_ge(S["y_out"], 16 * NT + 1)

        @block.tensor
        def _(pe):
            mm = nc.tensor.matmul

            def ada_block(i, r):
                n = i * 3 + r
                wait(pe, f"ada_in{r}", 32 * (i + 1))
                wait(pe, "ada_row", n - 2)
                for k in range(KD):
                    last = mm(bank(r)[0:GROUPS, :], silu_c[:, k * GROUPS:(k + 1) * GROUPS], ada_ring[r][:, k, :],
                              start=k == 0, stop=k == KD - 1)
                last.then_inc(S["ada_mm"], 1)

            pe.wait_ge(S["silu"], 1)
            for r in range(3):
                ada_block(0, r)
            with pe.Fori(1, ADA_BLOCKS // 3) as i:
                for r in range(3):
                    ada_block(i, r)

            pe.wait_ge(S["consts"], 48)
            pe.wait_ge(S["cols_in"], 48)
            n_rows = MOD_ROWS + KD + HEADS + 1
            nc.tensor.transpose(bank(3)[:, 0:n_rows], cols_in[0:n_rows, :], ident[0:n_rows, 0:n_rows]).then_inc(S["colsT"], 1)

            pe.wait_ge(S["xs"], NT)
            for k in range(KD):
                if k >= 4:
                    wait(pe, "xtr_dve" if k % 2 else "xtr_act", (k - 4) // 2 + 1)
                for t in range(NT):
                    last = nc.tensor.transpose(bank(4 + k % 4)[:, t * P:(t + 1) * P],
                                               big_m[:, t * D + k * P:t * D + (k + 1) * P], ident[:, :])
                last.then_inc(S["xtr"], 1)

            def project(h, n):
                if n == 0:
                    wait(pe, "w_t_in", 16 * (h + 1))
                if n == 4:
                    wait(pe, "w_v_in", 16 * (h + 1))
                if n < 4:
                    wait(pe, "gate", 4 * (h - 1) + n + 1)
                else:
                    wait(pe, "proj_ev", 8 * h + n - 3)
                for k in range(KD):
                    if n < 4:
                        last = mm(bank(n), slab_t[:, k, n * P:(n + 1) * P], h_t[:, k, :], start=k == 0, stop=k == KD - 1)
                    else:
                        last = mm(bank(n - 4)[:, 0:3 * P], h_t[:, k, (n - 4) * P:(n - 3) * P], slab_v[:, k, :],
                                  start=k == 0, stop=k == KD - 1)
                last.then_inc(S["proj"], 1)

            def ret_scores(a, g):
                wait(pe, "proj_ev", 8 * a + 2)
                wait(pe, "out_te", 2 * (a - 1) + g + 1)
                for s in range(TPG):
                    last = mm(bank(4 + g)[:, s * SEQ:(s + 1) * SEQ], k_t[:, (g * TPG + s) * P:(g * TPG + s + 1) * P],
                              q_t[:, g * SEQ:(g + 1) * SEQ], start=True, stop=True)
                last.then_inc(S["ret_s"], 1)

            def dif_scores(a, u):
                g, m = groups_of(u)
                wait(pe, "proj_ev", 8 * a + 4)
                if u < 2:
                    wait(pe, "dif_n", 4 * (a - 1) + u + 3)
                else:
                    wait(pe, "ret_pd", 2 * a + u - 1)
                b = bank(6 + u if u < 2 else 2 + u)
                for t in range(g * TPG, (g + 1) * TPG):
                    last = mm(b[:, t % TPG * SEQ:(t % TPG + 1) * SEQ], dq_t[m * DQK:(m + 1) * DQK, t * P:(t + 1) * P],
                              dk_t[m * DQK:(m + 1) * DQK, g * SEQ:(g + 1) * SEQ], start=True, stop=True)
                last.then_inc(S["dif_s"], 1)

            def ret_values(a, g):
                wait(pe, "dif_sd", 4 * a + g + 1)
                wait(pe, "ret_pd", 2 * a + g + 1)
                wait(pe, "proj_ev", 8 * a + 6 + 2 * g)
                for tt in range(TPG):
                    for s in range(TPG):
                        last = mm(bank(6 + g)[:, tt * P:(tt + 1) * P], ret_p[:, g, s, tt * P:(tt + 1) * P],
                                  vd[:, g * TPG + s, 0, :], start=s == 0, stop=s == TPG - 1)
                last.then_inc(S["ret_v"], 1)

            def dif_transposes(a, u):
                wait(pe, "dif_c", 4 * a + u + 1)
                if u < 2:
                    wait(pe, "dif_sd", 4 * a + u + 3)
                else:
                    wait(pe, "dif_te", 4 * a + u - 1)
                for s in range(TPG):
                    last = nc.tensor.transpose(bank(4 + u % 2)[:, s * P:(s + 1) * P], attn[:, u, s * P:(s + 1) * P], ident[:, :])
                last.then_inc(S["dif_t"], 1)

            def dif_values(a, u):
                g, qt = groups_of(u)
                wait(pe, "dif_te", 4 * a + u + 1)
                if u < 2:
                    wait(pe, "ret_n", 2 * a + u + 1)
                else:
                    wait(pe, "dif_n", 4 * a + u - 1)
                for s in range(TPG):
                    last = mm(bank(6 + u % 2)[:, 0:P], attn_t[:, u, s, :], vd[:, g * TPG + s, 1, :],
                              start=s == 0, stop=s == TPG - 1)
                last.then_inc(S["dif_v"], 1)

            def out_transposes(a, w):
                wait(pe, "dif_te", 4 * a + 3 + w)
                if w == 0:
                    wait(pe, "ret_n", 2 * a + 2)
                else:
                    wait(pe, "dif_n", 4 * a + 4)
                src = diff_o if w else ret_o
                for t in range(NT):
                    last = nc.tensor.transpose(bank(4 + w)[:, t * P:(t + 1) * P], src[:, t, :], ident[:, :])
                last.then_inc(S["out_t"], 1)

            def head_step(h, a):
                def p(n):
                    if h is not None:
                        project(h, n)

                def step(f, *units):
                    if a is not None:
                        for u in units:
                            f(a, u)
                p(0)
                step(ret_scores, 0, 1)
                step(dif_scores, 0, 1)
                p(1)
                step(dif_scores, 2, 3)
                p(2)
                step(ret_values, 0, 1)
                p(3)
                step(dif_transposes, 0, 1)
                p(4)
                step(dif_values, 0, 1)
                step(dif_transposes, 2, 3)
                p(5)
                step(dif_values, 2, 3)
                p(6)
                p(7)
                step(out_transposes, 0, 1)

            pe.wait_ge(S["xtr_act"], KD // 2)
            pe.wait_ge(S["xtr_dve"], KD // 2)
            head_step(0, None)
            head_step(1, 0)
            with pe.Fori(2, HEADS) as h:
                head_step(h, h - 1)
            head_step(None, HEADS - 1)

            def wo_block(i, r):
                wait(pe, f"wo_in{r}", 16 * (i + 1))
                wait(pe, "wo_dve" if r else "wo_act", NT * i)
                for t in range(NT):
                    for k in range(KD):
                        last = mm(bank(4 * r + t)[:, 0:WOC], mix_t[:, k, t * P:(t + 1) * P], wo_ring[r][:, k, :],
                                  start=k == 0, stop=k == KD - 1)
                    last.then_inc(S["wo_mm"], 1)

            pe.wait_ge(S["out_te"], 2 * HEADS)
            for r in range(2):
                wo_block(0, r)
            with pe.Fori(1, D // WOC // 2) as i:
                for r in range(2):
                    wo_block(i, r)

            pe.wait_ge(S["wo_act"], NT * D // WOC // 2)
            for t in range(NT):
                pe.wait_ge(S["h2"], t + 1)
                for kk in range(4):
                    wait(pe, "h2tr_ev", 4 * (t - 1) + kk + 1)
                    for j in range(4):
                        k = 4 * kk + j
                        last = nc.tensor.transpose(bank(kk)[:, j * P:(j + 1) * P], o_sb[:, t, k * P:(k + 1) * P], ident[:, :])
                    last.then_inc(S["h2tr"], 1)

            def route_head(i, r):
                hd = i * 2 + r
                wait(pe, f"wq_in{r}", 16 * (i + 1))
                for m in range(2):
                    wait(pe, "q_ev", 2 * (hd - 1) + m + 1)
                    for k in range(KD):
                        last = mm(bank(m), wq_ring[r][:, k, m * P:(m + 1) * P], h2_t[:, k, :], start=k == 0, stop=k == KD - 1)
                    last.then_inc(S["q_mm"], 1)
                for m in range(2):
                    wait(pe, "q_ev", 2 * hd + m + 1)
                    wait(pe, "sc_dve", 2 * (hd - 2) + m + 1)
                    for t in range(NT):
                        last = mm(bank(2 + m + 4 * r)[:, t * P:(t + 1) * P], qt_sb[:, m, t * P:(t + 1) * P],
                                  keys_sb[:, ds((2 * hd + m) * NKEYS, NKEYS)], start=True, stop=True)
                    last.then_inc(S["sc_mm"], 1)

            pe.wait_ge(S["h2tr_ev"], 4 * NT)
            pe.wait_ge(S["key_in"], 16)
            for r in range(2):
                route_head(0, r)
            with pe.Fori(1, PEER_HEADS // 2) as i:
                for r in range(2):
                    route_head(i, r)

        @block.scalar
        def _(act):
            acti = nc.scalar.activation
            act.wait_ge(S["consts"], 16 * 3)
            acti(silu_e, silu_c, ACT.Exp, scale=-1.0).then_inc(S["silu_e"], 1)
            act.wait_ge(S["lg_e"], 1)
            acti(lg_t[0], lg_t[0], ACT.Exp, scale=-1.0).then_inc(S["lg_e"], 1)
            act.wait_ge(S["lam_e"], 1)
            acti(lam_dot[:, 0:2], lam_dot[:, 0:2], ACT.Exp).then_inc(S["lam_e"], 1)
            for t in range(NT):
                act.wait_ge(S["x_in"], 16 * NT)
                wait(act, "sumsq", t)
                acti(psum[:, 4 * NB:8 * NB], x_sb[:, t, :], ACT.Square, accum_out=ss_x[:, t:t + 1]).then_inc(S["sumsq"], 1)
            act.wait_ge(S["colsT"], 1)
            acti(cols[:, 0:SUB + 1], bank(3)[:, 0:SUB + 1], ACT.Copy).then_inc(S["cols_ev"], 1)
            act.wait_ge(S["a1_cols"], 1)
            for k in range(0, KD, 2):
                act.wait_ge(S["xtr"], k + 1)
                for g in range(GROUPS):
                    last = acti(h_t[:, k, g * SEQ:(g + 1) * SEQ], bank(4 + k % 4)[:, g * SEQ:(g + 1) * SEQ], ACT.Identity,
                                scale=cols[:, (2 * g + 1) * KD + k:(2 * g + 1) * KD + k + 1],
                                bias=cols[:, 2 * g * KD + k:2 * g * KD + k + 1])
                last.then_inc(S["xtr_act"], 1)

            def decay_exp(a):
                act.wait_ge(S["dlog"], a + 1)
                wait(act, "ret_pd", 2 * a)
                acti(decay_tab, decay_log, ACT.Exp).then_inc(S["dtab"], 1)

            def evacuate(h, n):
                wait(act, "proj", 8 * h + n + 1)
                if n < 4:
                    wait(act, "ret_s" if n < 2 else "dif_s", 2 * h if n < 2 else 4 * h)
                    dst = (k_t, q_t, dk_t, dq_t)[n]
                    acti(dst, bank(n), ACT.Copy, scale=P ** -0.5 if n == 0 else 1.0).then_inc(S["proj_ev"], 1)
                else:
                    t = n - 4
                    g = t // TPG
                    wait(act, "ret_v", 2 * (h - 1) + g + 1)
                    wait(act, "dif_v", 4 * (h - 1) + 2 * g + 2)
                    wait(act, "gate", 4 * (h - 1) + t + 1)
                    v = bank(t)[:, 0:3 * P].rearrange("p (m c) -> p m c", m=3)
                    acti(vd[:, t, :, :], v[:, 0:3:2, :], ACT.Copy)
                    acti(e_g[:, t, :], v[:, 1, :], ACT.Exp, scale=-1.0).then_inc(S["proj_ev"], 1)

            def soft_exp(a, u):
                wait(act, "dif_m", 4 * a + u // TPG * TPG + 2)
                for m in range(2):
                    last = acti(soft[:, u, m, :], soft[:, u, m, :], ACT.Exp, scale=DQK ** -0.5, bias=nmax[:, u, m:m + 1],
                                accum_out=esum[:, u, m:m + 1])
                last.then_inc(S["dif_e"], 1)

            def attn_evacuate(a, u):
                wait(act, "dif_t", 4 * a + u + 1)
                wait(act, "dif_v", 4 * (a - 1) + u + 1)
                acti(attn_t[:, u, :, :], bank(4 + u % 2)[:, 0:SEQ].rearrange("p (s q) -> p s q", s=TPG), ACT.Copy)\
                    .then_inc(S["dif_te"], 1)

            def dif_square(a, u):
                wait(act, "dif_v", 4 * a + u + 1)
                acti(soft[:, u, 0, 0:P], bank(6 + u % 2)[:, 0:P], ACT.Square, accum_out=dif_ss[:, u:u + 1])\
                    .then_inc(S["dif_sq"], 1)

            def out_evacuate(a, w):
                wait_alone(act, "out_t", 2 * a + w + 1)
                scale = sub_w if w else cols[:, ds(GN + a, 1)]
                acti(mix_t[:, ds(a + w * HEADS, 1), :].rearrange("p a t -> p (a t)"), bank(4 + w), ACT.Copy, scale=scale)\
                    .then_inc(S["out_te"], 1)

            def head_step(h, a):
                def p(*ns):
                    if h is not None:
                        for n in ns:
                            evacuate(h, n)

                def step(f, *units):
                    if a is not None:
                        for u in units:
                            f(a, u)
                if a is not None:
                    decay_exp(a)
                p(0)
                step(soft_exp, 0, 1)
                p(1)
                step(soft_exp, 2, 3)
                p(2, 3)
                step(attn_evacuate, 0, 1)
                p(4)
                step(dif_square, 0, 1)
                step(attn_evacuate, 2, 3)
                p(5)
                step(dif_square, 2, 3)
                p(6, 7)
                step(out_evacuate, 0, 1)

            head_step(0, None)
            head_step(1, 0)
            with act.Fori(2, HEADS) as h:
                head_step(h, h - 1)
            head_step(None, HEADS - 1)

            def wo_evacuate(i):
                for t in range(NT):
                    wait_alone(act, "wo_mm", (2 * i) * NT + t + 1)
                    acti(o_sb[:, t, ds(2 * i * WOC, WOC)], bank(t)[:, 0:WOC], ACT.Copy).then_inc(S["wo_act"], 1)

            with act.Fori(0, D // WOC // 2) as i:
                wo_evacuate(i)
            act.wait_ge(S["wo_dve"], NT * D // WOC // 2)
            act.wait_ge(S["wo_act"], NT * D // WOC // 2)
            junk = psum[:, 4 * NB:8 * NB]
            for t in range(NT):
                wait(act, "o_sq", t)
                acti(junk, o_sb[:, t, :], ACT.Square, accum_out=ss_x[:, t:t + 1]).then_inc(S["o_sq"], 1)

            def h2_evacuate(t):
                for kk in range(4):
                    act.wait_ge(S["h2tr"], 4 * t + kk + 1)
                    acti(h2_t[:, 4 * kk:4 * kk + 4, t * P:(t + 1) * P], bank(kk).rearrange("p (j c) -> p j c", j=4), ACT.Copy)\
                        .then_inc(S["h2tr_ev"], 1)

            act.wait_ge(S["o_sq"], NT)
            for t in range(NT):
                act.wait_ge(S["x1"], t + 1)
                wait(act, "x1_sq", t)
                acti(junk, x_sb[:, t, :], ACT.Square, accum_out=ss_x[:, 4 + t:5 + t]).then_inc(S["x1_sq"], 1)
                if t >= 1:
                    h2_evacuate(t - 1)
            h2_evacuate(NT - 1)

            def query_evacuate(i):
                for r in range(2):
                    for m in range(2):
                        hd = i * 2 + r
                        wait(act, "q_mm", 2 * hd + m + 1)
                        wait(act, "sc_mm", 2 * (hd - 1) + m + 1)
                        acti(qt_sb[:, m, :], bank(m), ACT.Copy).then_inc(S["q_ev"], 1)

            query_evacuate(0)
            with act.Fori(1, PEER_HEADS // 2) as i:
                query_evacuate(i)
            act.wait_ge(S["gl_in"], 1)
            acti(gates, gates, ACT.Exp).then_inc(S["gl_exp"], 1)

            with act.Fori(0, NT) as t:
                wait_alone(act, "u_dot", t * SLOTS + BATCH)
                wait_alone(act, "acc_sq", t + 1)
                acti(psum[:, 0:D], o_sb[:, ds(t, 1), :].rearrange("p a d -> p (a d)"), ACT.Copy).then_inc(S["h2_ps"], 1)
                with act.Fori(0, BATCHES) as b:
                    n = t * BATCHES + b
                    wait_alone(act, "w_rdy", n + 1)
                    wait(act, "hid", n + 2)
                    acti(act_h, hid_whole, ACT.Gelu).then_inc(S["gelu"], 1)
                wait(act, "v_acc", t * SLOTS + SLOTS + BATCH)
                acti(psum[:, 0:D], psum[:, D:2 * D], ACT.Square, accum_out=ss_out[:, 0:1]).then_inc(S["acc_sq"], 1)

        @block.vector
        def _(dve):
            vec = nc.vector
            chain = [0]

            def link(ins):
                chain[0] += 1
                ins.then_inc(S["dve"], 1)
                dve.wait_ge(S["dve"], chain[0])

            class Chain:
                def __init__(self, before, turn, per_turn):
                    self.base, self.n, self.per_turn = turn * per_turn + before, 0, per_turn

                def __call__(self, ins, alone=False):
                    self.n += 1
                    ins.then_inc(S["dve"], 1)
                    (wait_alone if alone else wait)(dve, "dve", self.base + self.n)

                def done(self):
                    assert self.n == self.per_turn, self.n

            def rsqrt(link, out_, v, y, a):
                link(vec.tensor_scalar(a.bitcast(i32), v.bitcast(i32), 1, None, ALU.logical_shift_right))
                link(vec.tensor_scalar(y.bitcast(i32), a.bitcast(i32), -1.0, float(RSQRT_MAGIC), ALU.mult, ALU.add))
                for n in range(4):
                    link(vec.scalar_tensor_tensor(a, y, -0.5, y, ALU.mult, ALU.mult))
                    link(vec.tensor_tensor(a, a, v, ALU.mult))
                    link(vec.scalar_tensor_tensor(out_ if n == 3 else y, a, 1.5, y, ALU.add, ALU.mult))
            RSQRT = 14

            dve.wait_ge(S["silu_e"], 1)
            link(vec.tensor_scalar(silu_e, silu_e, 1.0, None, ALU.add))
            link(vec.reciprocal(silu_e, silu_e))
            vec.tensor_tensor(silu_c, silu_c, silu_e, ALU.mult).then_inc(S["silu"], 1)
            dve.wait_ge(S["rows_in"], 32)
            e, z, q = lg_t
            link(vec.tensor_scalar(e, lg_all, -1.0, None, ALU.mult))
            vec.tensor_tensor(e, e, lg_all, ALU.max).then_inc(S["lg_e"], 1)
            dve.wait_ge(S["lg_e"], 2)
            link(vec.tensor_scalar(z, e, 2.0, None, ALU.add))
            link(vec.reciprocal(z, z))
            link(vec.tensor_tensor(z, z, e, ALU.mult))
            link(vec.tensor_tensor(q, z, z, ALU.mult))
            link(vec.tensor_scalar(e, q, 1.0 / 17, 1.0 / 15, ALU.mult, ALU.add))
            for n in (13, 11, 9, 7, 5, 3, 1):
                link(vec.tensor_tensor(e, e, q, ALU.mult))
                link(vec.tensor_scalar(e, e, 1.0 / n, None, ALU.add))
            link(vec.tensor_tensor(e, e, z, ALU.mult))
            link(vec.tensor_scalar(lg_all, lg_all, 0.0, None, ALU.min))
            link(vec.scalar_tensor_tensor(lg_all, e, -2.0, lg_all, ALU.mult, ALU.add))
            for n in range(2):
                last = vec.tensor_tensor_reduce(out=lam_in[:, 2 * n, :], in0=lam_in[:, 2 * n, :], in1=lam_in[:, 2 * n + 1, :],
                                                scale=1.0, scalar=0.0, op0=ALU.mult, op1=ALU.add, accum_out=lam_dot[:, n:n + 1])
            last.then_inc(S["lam_e"], 1)
            dve.wait_ge(S["lam_e"], 2)
            link(vec.tensor_tensor(lam[:, 0:1], lam_dot[:, 1:2], lam_dot[:, 0:1], ALU.subtract))
            vec.tensor_scalar(lam[:, 0:1], lam[:, 0:1], -LAM_INIT, None, ALU.add).then_inc(S["lg_rdy"], 1)
            dve.wait_ge(S["sumsq"], NT)
            link(vec.tensor_scalar(nt_a[:, 0:NT], ss_x[:, 0:NT], 1.0 / D, EPS, ALU.mult, ALU.add))
            rsqrt(link, rstd_x[:, 0:NT], nt_a[:, 0:NT], nt_y[:, 0:NT], nt_b[:, 0:NT])

            def ada_row(i, r):
                wait(dve, "ada_mm", i * 3 + r + 1)
                wait(dve, f"mod_out{r}", 16 * i)
                vec.tensor_tensor(mod_rows[:, r, :], bank(r)[0:GROUPS, :], bias_rows[:, r, :], ALU.add).then_inc(S["ada_row"], 1)

            for r in range(3):
                ada_row(0, r)
            with dve.Fori(1, ADA_BLOCKS // 3) as i:
                for r in range(3):
                    ada_row(i, r)

            for t in range(NT):
                vec.tensor_scalar(big_m[:, t * D:(t + 1) * D], x_sb[:, t, :], rstd_x[:, t:t + 1], None, ALU.mult).then_inc(S["xs"], 1)
            dve.wait_ge(S["cols_ev"], 1)
            link(vec.tensor_scalar(sub_w, cols[:, SUB:SUB + 1], 1.0 - LAM_INIT, None, ALU.mult))
            for g in range(GROUPS):
                sc = cols[:, (2 * g + 1) * KD:(2 * g + 2) * KD]
                last = vec.scalar_tensor_tensor(sc, sc, 1.0, cols[:, PRE1:PRE1 + KD], ALU.add, ALU.mult)
            last.then_inc(S["a1_cols"], 1)
            dve.wait_ge(S["a1_cols"], 1)
            for k in range(1, KD, 2):
                dve.wait_ge(S["xtr"], k + 1)
                for g in range(GROUPS):
                    last = vec.tensor_scalar(h_t[:, k, g * SEQ:(g + 1) * SEQ], bank(4 + k % 4)[:, g * SEQ:(g + 1) * SEQ],
                                             cols[:, (2 * g + 1) * KD + k:(2 * g + 1) * KD + k + 1],
                                             cols[:, 2 * g * KD + k:2 * g * KD + k + 1], ALU.mult, ALU.add)
                last.then_inc(S["xtr_dve"], 1)

            def decay_logs(a, link):
                wait(dve, "dtab", a)
                dve.sem_inc(S["spare"], 1)
                link(vec.tensor_copy(lg_h, lg_all[:, ds(2 * a, 2)]))
                link(vec.tensor_scalar(decay_log, dist[:, 1, :], lg_h[:, 1:2], None, ALU.mult))
                vec.scalar_tensor_tensor(decay_log, dist[:, 0, :], lg_h[:, 0:1], decay_log, ALU.mult, ALU.add).then_inc(S["dlog"], 1)

            def ret_decay(a, g, link):
                wait(dve, "ret_s", 2 * a + g + 1)
                wait(dve, "dtab", a + 1)
                wait(dve, "ret_v", 2 * (a - 1) + g + 1)
                for s in range(TPG):
                    last = vec.tensor_tensor(ret_p[:, g, s, :], bank(4 + g)[:, s * SEQ:(s + 1) * SEQ],
                                             decay_tab[:, P * (1 - s):P * (1 - s) + SEQ], ALU.mult)
                last.then_inc(S["ret_pd"], 1)

            def dif_soft(a, u, link):
                g, m = groups_of(u)
                units = slice(g * TPG, (g + 1) * TPG)
                wait(dve, "alibi_in", 16 * (a + 1))
                wait(dve, "dif_s", 4 * a + u + 1)
                b = bank(6 + u if u < 2 else 2 + u)
                vec.tensor_tensor(soft[:, units, m, :], b.rearrange("p (t k) -> p t k", t=TPG), alibi, ALU.add)\
                    .then_inc(S["dif_sd"], 1)
                wait(dve, "dif_sd", 4 * a + u + 1)
                link(vec.tensor_reduce(nmax[:, units, m], soft[:, units, m, :], axis=AX, op=ALU.max, negate=True))
                vec.tensor_scalar(nmax[:, units, m], nmax[:, units, m], DQK ** -0.5, None, ALU.mult).then_inc(S["dif_m"], 1)

            def dif_combine(a, u, link):
                wait(dve, "dif_e", 4 * a + u + 1)
                wait(dve, "dif_t", 4 * (a - 1) + u + 1)
                link(vec.reciprocal(coef[:, u, :], esum[:, u, :]))
                vec.tensor_scalar(coef[:, u, 1:2], coef[:, u, 1:2], lam[:, 0:1], None, ALU.mult)
                link(vec.tensor_scalar(attn[:, u, :], soft[:, u, 0, :], coef[:, u, 0:1], None, ALU.mult))
                vec.scalar_tensor_tensor(attn[:, u, :], soft[:, u, 1, :], coef[:, u, 1:2], attn[:, u, :], ALU.mult, ALU.add)\
                    .then_inc(S["dif_c"], 1)

            def ret_norm(a, g, link):
                wait(dve, "ret_v", 2 * a + g + 1)
                wait(dve, "out_t", 2 * a)
                for tt in range(TPG):
                    last = vec.bn_stats(bn6[:, g * TPG + tt, :], bank(6 + g)[:, tt * P:(tt + 1) * P])
                link(last, alone=True)
                for tt in range(TPG):
                    last = vec.bn_aggr(mv[:, g * TPG + tt, :], bn6[:, g * TPG + tt, :])
                link(last)
                link(vec.tensor_scalar(nt_a[:, 0:TPG], mv[:, g * TPG:(g + 1) * TPG, 1], EPS, None, ALU.add))
                rsqrt(link, nt_y[:, 4:4 + TPG], nt_a[:, 0:TPG], nt_y[:, 0:TPG], nt_b[:, 0:TPG])
                for tt in range(TPG):
                    t = g * TPG + tt
                    last = vec.tensor_scalar(ret_o[:, t, :], bank(6 + g)[:, tt * P:(tt + 1) * P], mv[:, t, 0:1],
                                             nt_y[:, 4 + tt:5 + tt], ALU.subtract, ALU.mult)
                link(last)
                vec.tensor_tensor(ret_o[:, g * TPG:(g + 1) * TPG, :], ret_o[:, g * TPG:(g + 1) * TPG, :],
                                  gate[:, g * TPG:(g + 1) * TPG, :], ALU.mult).then_inc(S["ret_n"], 1)

            def dif_norm(a, pair, link):
                wait(dve, "dif_sq", 4 * a + 2 * pair + 2)
                wait(dve, "out_t", 2 * a)
                link(vec.tensor_scalar(nt_a[:, 0:2], dif_ss[:, 2 * pair:2 * pair + 2], 1.0 / P, EPS, ALU.mult, ALU.add))
                rsqrt(link, nt_y[:, 4:6], nt_a[:, 0:2], nt_y[:, 0:2], nt_b[:, 0:2])
                for j in range(2):
                    vec.tensor_scalar(diff_o[:, 2 * pair + j, :], bank(6 + j)[:, 0:P], nt_y[:, 4 + j:5 + j], None, ALU.mult)\
                        .then_inc(S["dif_n"], 1)

            def silu_gate(h, t, link):
                wait(dve, "proj_ev", 8 * h + 5 + t)
                link(vec.tensor_scalar(e_g[:, t, :], e_g[:, t, :], 1.0, None, ALU.add))
                link(vec.reciprocal(e_g[:, t, :], e_g[:, t, :]))
                vec.tensor_tensor(gate[:, t, :], e_g[:, t, :], bank(t)[:, P:2 * P], ALU.mult).then_inc(S["gate"], 1)

            def head_step(h, a, link):
                def step(f, *units):
                    if a is not None:
                        for u in units:
                            f(a, u, link)

                def gates_of(*tiles):
                    if h is not None:
                        for t in tiles:
                            silu_gate(h, t, link)
                step(ret_decay, 0, 1)
                step(dif_soft, 0, 1, 2, 3)
                step(dif_combine, 0, 1)
                step(ret_norm, 0, 1)
                step(dif_combine, 2, 3)
                step(dif_norm, 0)
                gates_of(0, 1)
                step(dif_norm, 1)
                gates_of(2, 3)
                if h is not None:
                    decay_logs(h, link)

            def plain(ins, alone=False):
                link(ins)

            dve.wait_ge(S["rows_in"], 48)
            head_step(0, None, plain)
            head_step(1, 0, plain)
            PER_HEAD = 4 + 8 + 2 * (3 + RSQRT + 1) + 2 * (1 + RSQRT) + 8 + 2
            with dve.Fori(2, HEADS) as h:
                c = Chain(chain[0] - 2 * PER_HEAD, h, PER_HEAD)
                head_step(h, h - 1, c)
                c.done()
            chain[0] += (HEADS - 2) * PER_HEAD
            head_step(None, HEADS - 1, plain)

            with dve.Fori(0, D // WOC // 2) as i:
                for t in range(NT):
                    wait_alone(dve, "wo_mm", (2 * i + 1) * NT + t + 1)
                    vec.tensor_copy(o_sb[:, t, ds((2 * i + 1) * WOC, WOC)], bank(4 + t)[:, 0:WOC]).then_inc(S["wo_dve"], 1)

            dve.wait_ge(S["o_sq"], NT)
            link(vec.tensor_scalar(nt_a[:, 0:NT], ss_x[:, 0:NT], 1.0 / D, EPS, ALU.mult, ALU.add))
            rsqrt(link, rstd_x[:, 0:NT], nt_a[:, 0:NT], nt_y[:, 0:NT], nt_b[:, 0:NT])
            for g in range(GROUPS):
                dve.wait_ge(S["coef_in"], 16 * (5 + 3 * g))
                link(vec.tensor_tensor(gate1_sb, gate1_sb, post1_sb, ALU.mult))
                vec.scalar_tensor_tensor(scale2_sb, scale2_sb, 1.0, pre2_sb, ALU.add, ALU.mult)
                for tt in range(TPG):
                    t = g * TPG + tt
                    link(vec.scalar_tensor_tensor(o_sb[:, t, :], o_sb[:, t, :], rstd_x[:, t:t + 1], gate1_sb, ALU.mult, ALU.mult))
                    vec.tensor_tensor(x_sb[:, t, :], x_sb[:, t, :], o_sb[:, t, :], ALU.add).then_inc(S["x1"], 1)
                for tt in range(TPG):
                    t = g * TPG + tt
                    dve.wait_ge(S["x1_sq"], t + 1)
                    link(vec.tensor_scalar(nt_a[:, 0:1], ss_x[:, 4 + t:5 + t], 1.0 / D, EPS, ALU.mult, ALU.add))
                    rsqrt(link, rstd_x[:, 4 + t:5 + t], nt_a[:, 0:1], nt_y[:, 0:1], nt_b[:, 0:1])
                    link(vec.scalar_tensor_tensor(o_sb[:, t, :], x_sb[:, t, :], rstd_x[:, 4 + t:5 + t], scale2_sb, ALU.mult, ALU.mult))
                    vec.tensor_tensor(o_sb[:, t, :], o_sb[:, t, :], shift2_sb, ALU.add).then_inc(S["h2"], 1)
                dve.wait_ge(S["h2"], TPG * (g + 1))
                dve.sem_inc(S["grp_done"], 1)

            def top16(values, work, best, where, link):
                for t in range(NT):
                    last = vec.max(best[:, t, 0:8], values(t))
                link(last, alone=True)
                for t in range(NT):
                    last = vec.match_replace(work(t), best[:, t, 0:8], values(t), LOWEST)
                link(last, alone=True)
                for t in range(NT):
                    last = vec.max(best[:, t, 8:16], work(t))
                link(last, alone=True)
                for t in range(NT):
                    vec.max_index(where[:, t, 8:16], best[:, t, 8:16], work(t))
                for t in range(NT):
                    last = vec.max_index(where[:, t, 0:8], best[:, t, 0:8], values(t))
                return last

            def route_head(i, r, link):
                hd = i * 2 + r
                for m in range(2):
                    b = bank(2 + m + 4 * r)
                    wait_alone(dve, "sc_mm", 2 * hd + m + 1)
                    top16(lambda t: b[:, t * P:(t + 1) * P], lambda t: masked[:, t, 0:NKEYS], top_v[:, m], top_i[:, m], link)\
                        .then_inc(S["sc_dve"], 1)
                wait(dve, "sc_dve", 2 * hd + 2)
                link(vec.tensor_copy(top_if, top_i))
                pairs = [P, NT, TOPK, TOPK]
                link(vec.tensor_tensor(cand.rearrange("p t (i j) -> p t i j", i=TOPK), top_v[:, 0].unsqueeze(3).to_broadcast(pairs),
                                       top_v[:, 1].unsqueeze(2).to_broadcast(pairs), ALU.add), alone=True)
                link(top16(lambda t: cand[:, t, :], lambda t: masked[:, t, :], best_v, best_p, link))
                hot = onehot.rearrange("p (t k i) -> p t k i", t=NT, k=TOPK)
                for m in range(2):
                    op, by = (ALU.bitwise_and, TOPK - 1) if m else (ALU.logical_shift_right, 4)
                    link(vec.tensor_scalar(part_u, best_p.rearrange("p t k -> p (t k)"), by, None, op))
                    link(vec.tensor_copy(part_f, part_u))
                    link(vec.tensor_tensor(hot, part_f.rearrange("p (t k) -> p t k", t=NT).unsqueeze(3).to_broadcast(pairs),
                                           iota16.unsqueeze(1).unsqueeze(1).to_broadcast(pairs), ALU.is_equal))
                    link(vec.tensor_tensor(hot, hot, top_if[:, m].unsqueeze(2).to_broadcast(pairs), ALU.mult))
                    link(vec.tensor_reduce(pick[:, m], hot, axis=AX, op=ALU.add))
                link(vec.scalar_tensor_tensor(pick[:, 0].rearrange("p t k -> p (t k)"), pick[:, 0].rearrange("p t k -> p (t k)"),
                                              float(NKEYS), pick[:, 1].rearrange("p t k -> p (t k)"), ALU.mult, ALU.add), alone=True)
                vec.tensor_copy(eidx[:, :, ds(hd * TOPK, TOPK)], pick[:, 0])
                link(vec.tensor_tensor(gates[:, :, ds(hd * TOPK, TOPK)], best_v, best_v[:, :, 0:1].to_broadcast([P, NT, TOPK]),
                                       ALU.subtract))
            PER_ROUTE = 3 * 3 + 4 + 10 + 1 + 0

            with dve.Fori(0, PEER_HEADS // 2) as i:
                c = Chain(chain[0], i, 2 * PER_ROUTE)
                for r in range(2):
                    route_head(i, r, c)
                c.done()
            chain[0] += PEER_HEADS * PER_ROUTE
            dve.sem_inc(S["gl_in"], 1)
            dve.sem_inc(S["eidx_rdy"], 1)
            dve.wait_ge(S["gl_exp"], 1)
            by_head = gates.rearrange("p t (h k) -> p (t h) k", k=TOPK)
            sums = soft_e[:, 0:NT * PEER_HEADS]
            link(vec.tensor_reduce(sums, by_head, axis=AX, op=ALU.add))
            link(vec.reciprocal(sums, sums))
            link(vec.tensor_tensor(by_head, by_head, sums.unsqueeze(2).to_broadcast([P, NT * PEER_HEADS, TOPK]), ALU.mult))

            dve.sem_inc(S["u_dot"], BATCH)
            dve.sem_inc(S["v_acc"], BATCH)
            dve.sem_inc(S["hid"], 1)
            dve.sem_inc(S["w_rdy"], 1)
            dve.sem_inc(S["acc_sq"], 1)
            dve.sem_inc(S["y_out"], 1)
            dve.sem_inc(S["y"], 1)
            acc = psum[:, D:2 * D]

            def dot(n, j):
                if j == 0:
                    wait_alone(dve, "hid", n + 1)
                wait(dve, f"u_in{j}", 16 * (n + 1))
                vec.tensor_tensor_reduce(out=u_ring[:, j, :], in0=u_ring[:, j, :], in1=psum[:, 0:D], scale=1.0, scalar=0.0,
                                         op0=ALU.mult, op1=ALU.add, accum_out=hid[:, j:j + 1]).then_inc(S["u_dot"], 1)

            def batch_dots(n):
                wait(dve, "u_dot", (n + 2) * BATCH)
                vec.tensor_copy(hid_whole, hid).then_inc(S["hid"], 1)

            def weights(t, b, n):
                wait(dve, "gelu", n + 1)
                wait_alone(dve, "v_acc", n * BATCH + BATCH)
                vec.tensor_tensor(w_slot, act_h, gates[:, ds(t, 1), ds(b * BATCH, BATCH)].rearrange("p a k -> p (a k)"), ALU.mult)\
                    .then_inc(S["w_rdy"], 1)
                wait(dve, "w_rdy", n + 2)

            def accumulate(n, j):
                wait(dve, f"v_in{j}", 16 * (n + 1))
                wait(dve, "v_acc", n * BATCH + BATCH + j)
                vec.scalar_tensor_tensor(acc, v_ring[:, j, :], w_slot[:, j:j + 1], acc, ALU.mult, ALU.add).then_inc(S["v_acc"], 1)

            dve.wait_ge(S["rows_in"], 64)
            with dve.Fori(0, NT) as t:
                wait_alone(dve, "y", t + 1)
                vec.memset(acc, 0.0)
                wait(dve, "h2_ps", t + 1)
                for j in range(BATCH):
                    dot(t * BATCHES, j)
                batch_dots(t * BATCHES)
                with dve.Fori(1, BATCHES) as b:
                    n = t * BATCHES + b
                    for j in range(BATCH):
                        dot(n, j)
                        if j == 0:
                            weights(t, b - 1, n - 1)
                        if j == BATCH - 1:
                            batch_dots(n)
                        accumulate(n - 1, j)
                n = t * BATCHES + BATCHES - 1
                weights(t, BATCHES - 1, n)
                for j in range(BATCH):
                    accumulate(n, j)
                c = Chain(chain[0], t, 1 + RSQRT + 2)
                wait(dve, "acc_sq", t + 2)
                c(vec.tensor_scalar(nt_a[:, 0:1], ss_out[:, 0:1], 1.0 / D, EPS, ALU.mult, ALU.add))
                rsqrt(c, nt_y[:, 4:5], nt_a[:, 0:1], nt_y[:, 0:1], nt_b[:, 0:1])
                wait_alone(dve, "g2_in", 16 * (t + 1))
                wait_alone(dve, "y_out", 16 * t + 1)
                c(vec.scalar_tensor_tensor(out_sb, acc, nt_y[:, 4:5], gate2_sb, ALU.mult, ALU.mult))
                c(vec.tensor_tensor(out_sb, out_sb, post2_sb, ALU.mult))
                c.done()
                vec.tensor_tensor(out_sb, out_sb, x_sb[:, ds(t, 1), :].rearrange("p a d -> p (a d)"), ALU.add).then_inc(S["y"], 1)

        @block.gpsimd
        def _(pool):
            def stage_index(dst, t, b):
                nc.gpsimd.tensor_copy(dst, eidx[:, ds(t, 1), ds(b * BATCH, BATCH)].rearrange("p a k -> p (a k)")).then_inc(S["stage"], 1)

            def gather(table, ring, stage, sem, j):
                pool.indirect_dma_start(out=ring[:, j, :], out_offset=None, in_=table,
                                        in_offset=bass.IndirectOffsetOnAxis(ap=stage[:, j:j + 1], axis=0)).then_inc(S[f"{sem}{j}"], 16)

            def gathers(t, b, u_parity, v_parity):
                n = t * BATCHES + b
                copies = t * 2 * BATCHES + 2 * b
                if u_parity is not None:
                    stage_index(stage_u[u_parity], t, b)
                if v_parity is not None:
                    stage_index(stage_v[v_parity], t, b - 1)
                wait_alone(pool, "stage", copies + (u_parity is not None))
                for j in range(BATCH):
                    if u_parity is not None:
                        wait_alone(pool, "u_dot", n * BATCH + j + 1)
                        gather(u_tab, u_ring, stage_u[u_parity], "u_in", j)
                    if v_parity is not None:
                        wait_alone(pool, "v_acc", (n - 1) * BATCH + j + 1)
                        gather(v_tab, v_ring, stage_v[v_parity], "v_in", j)

            pool.wait_ge(S["eidx_rdy"], 1)
            pool.wait_ge(S["q_mm"], 2 * PEER_HEADS)
            with pool.Fori(0, NT) as t:
                gathers(t, 0, 0, None)
                with pool.Fori(0, BATCHES // 2 - 1) as i:
                    gathers(t, 2 * i + 1, 1, 0)
                    gathers(t, 2 * i + 2, 0, 1)
                gathers(t, BATCHES - 1, 1, 0)
                gathers(t, BATCHES, None, 1)


_INS = ["x", "ct", "ada_w", "ada_b", "rows", "w_t", "w_v", "w_o", "w_q", "keys_t", "decay", "lams", "post1", "pre2", "post2",
        "u_tab", "v_tab", "ident", "dist", "alibi", "iota"]


def constants():
    s = np.arange(P)[:, None]
    rel = np.arange(384)[None, :] - P - s
    dist = np.stack([np.maximum(rel, 0), np.maximum(-rel, 0)], 1).astype(np.float32)
    slopes = 2.0 ** (-8.0 * np.arange(1, HEADS + 1) / HEADS)
    q = np.arange(SEQ).reshape(TPG, P).T
    away = np.abs(q[:, :, None] - np.arange(SEQ)[None, None, :])
    alibi = (-slopes[:, None, None, None] * DQK ** 0.5 * away[None]).astype(np.float32)
    return {"ident": np.eye(P, dtype=np.float32), "dist": dist, "alibi": alibi,
            "iota": np.tile(np.arange(TOPK, dtype=np.float32), (P, 1))}


def lay_out(i):
    w_in = i["w_in"][0].reshape(KD, P, 7, HEADS, P)
    rq, rk, rv, rg, dq, dk, dv = (w_in[:, :, n] for n in range(7))

    def heads(*mats):
        return np.stack(mats, 3).transpose(2, 1, 0, 3, 4).reshape(HEADS, P, KD, len(mats) * P)

    def blocks(w, n):
        return w.reshape(KD, P, w.shape[1] // n, n).transpose(2, 1, 0, 3)
    a = {
        "x": np.concatenate([i["x_prompt"][0], i["x_sample"][0]], 0),
        "ct": np.concatenate([i["c_prompt"], i["c_sample"]], 0).reshape(GROUPS, KD, P).transpose(2, 1, 0).reshape(P, -1),
        "ada_w": blocks(i["ada_w"][0], NB),
        "ada_b": i["ada_b"],
        "rows": np.concatenate([i["mix_pre_w"][0].reshape(KD, P), i["ret_gn_w"][0].reshape(HEADS, P), i["diff_subln_w"]], 0),
        "w_t": heads(rk, rq, dk, dq),
        "w_v": heads(rv, rg, dv),
        "w_o": blocks(i["w_out"][0], WOC),
        "w_q": blocks(i["peer_w_query"][0], 2 * P),
        "keys_t": i["peer_sub_keys"][0].transpose(3, 0, 1, 2).reshape(P, -1),
        "decay": np.stack([i["ret_decay_fwd"][0], i["ret_decay_bwd"][0]], 1).reshape(1, -1),
        "lams": np.concatenate([i["diff_lambda_q1"], i["diff_lambda_k1"], i["diff_lambda_q2"], i["diff_lambda_k2"]], 1),
        "post1": i["mix_post_w"], "pre2": i["ffn_pre_w"], "post2": i["ffn_post_w"],
        "u_tab": i["peer_u"][0], "v_tab": i["peer_v"][0],
    }
    return {**a, **constants()}


def kernel(**inputs):
    import concourse.bacc as bacc
    from concourse import mybir
    from concourse.bass_utils import run_bass_kernel_spmd

    nc = bacc.Bacc("TRN2", target_bir_lowering=False, num_devices=1)
    laid = lay_out({k: np.asarray(v) for k, v in inputs.items()})
    arrays, args = {}, []
    for name in _INS:
        a = np.ascontiguousarray(laid[name])
        arrays[f"in_{name}"] = a
        args.append(nc.dram_tensor(f"in_{name}", a.shape, mybir.dt.from_np(a.dtype), kind="ExternalInput").ap())
    out = nc.dram_tensor("out_0", (T, D), mybir.dt.float32, kind="ExternalOutput").ap()
    mod_d = nc.dram_tensor("mod_scratch", (GROUPS, MODS * D), mybir.dt.float32).ap()
    build_program(nc, *args, out, mod_d)
    got = run_bass_kernel_spmd(nc, [arrays], core_ids=[0]).results[0]["out_0"]
    return got[0:SEQ][None], got[SEQ:T][None]
```

```python
import math
import numpy as np

P = 128
D = 2048
KD = D // P
SEQ = 256
GROUPS = 2
TPG = SEQ // P
NT = GROUPS * TPG
T = NT * P
HEADS = 8
DQK = 64
MODS = 6
NB = 512
ADA_BLOCKS = 2 * D // NB
LATE = (MODS - 2) * KD
PIECE = D // 2
PIECES = 2 * LATE // 8
EPS = 1e-6
LAM_INIT = 0.8 - 0.6 * math.exp(-0.3 * 0)
PEER_HEADS = 8
NKEYS = 128
TOPK = 16
SLOTS = PEER_HEADS * TOPK
WOC = 256
RSQRT_MAGIC = 0x5F3759DF
LOWEST = -3.0e38
GATHERED = 1
DT = NT - GATHERED
ND = DT * P
RING = 4
HALF = D // 2
PAIRS = NKEYS // 2


def build_program(nc, x, ct, c_rows, ada_w, ada_wt, ada_b, rows, w_t, w_v, w_o, w_q, keys_t, decay, lams, post1, pre2, post2,
                  u_t, u_tab, v_tab, ident_c, dist_c, alibi_c, iota_c, out, mod_d, silu_d, g_d, w_d):
    import concourse.bass as bass
    from concourse import mybir
    from contextlib import ExitStack

    f32, i32, u32, f32r = mybir.dt.float32, mybir.dt.int32, mybir.dt.uint32, mybir.dt.float32r
    ALU, ACT, AX = mybir.AluOpType, mybir.ActivationFunctionType, mybir.AxisListType.X
    ds = bass.ds

    with ExitStack() as ctx:
        def sbuf(name, shape, dtype=f32):
            return ctx.enter_context(nc.sbuf_tensor("sb_" + name, shape, dtype))

        def semaphore(name):
            return ctx.enter_context(nc.semaphore(name))

        base = (nc.sbuf_base + 31) // 32 * 32
        sizes = [NT * D, NT * D, NT * D, 14336]
        arena = sbuf("arena", [P, sum(sizes)])
        X0, H0, M0, W0 = (sum(sizes[:n]) for n in range(4))
        big_x, big_h, big_m, big_w = (arena[:, a:a + n] for a, n in zip((X0, H0, M0, W0), sizes))
        small = sbuf("small", [P, 11264])

        def placed(name, at, shape, dtype=f32):
            return nc.alloc_sbuf_tensor_at("sb_" + name, shape, dtype, offset=base + 4 * at)

        def rounded(name, at, shape):
            return placed(name, at, shape, f32r)
        ident = sbuf("ident", [P, P])
        cols = sbuf("cols", [P, 96])
        tiny = sbuf("tiny", [P, 512])

        x_sb = big_x[:, :].rearrange("p (t d) -> p t d", t=NT)
        h_t = big_h[:, :].rearrange("p (k t) -> p k t", k=KD)
        o_sb = big_h[:, :].rearrange("p (t d) -> p t d", t=NT)
        mix_t = big_m[:, :].rearrange("p (k t) -> p k t", k=KD)
        slab_t = big_w[:, 0:8192].rearrange("p (k c) -> p k c", k=KD)
        slab_v = big_w[:, 8192:14336].rearrange("p (k c) -> p k c", k=KD)

        def carver(arena):
            at = [0]

            def take(n):
                at[0] += n
                assert at[0] <= arena.shape[1], at[0]
                return arena[:, at[0] - n:at[0]]
            return take

        take = carver(small)
        k_t, q_t, dk_t, dq_t = (take(T) for _ in range(4))
        vd = take(NT * 2 * P).rearrange("p (t m c) -> p t m c", t=NT, m=2)
        e_g = take(NT * P).rearrange("p (t c) -> p t c", t=NT)
        gate = take(NT * P).rearrange("p (t c) -> p t c", t=NT)
        dist = take(2 * 384).rearrange("p (s u) -> p s u", s=2)
        decay_log = take(384)
        decay_tab = take(384)
        ret_p = take(GROUPS * 512).rearrange("p (g s t) -> p g s t", g=GROUPS, s=TPG)
        soft = take(4 * 512).rearrange("p (u m k) -> p u m k", u=4, m=2)
        attn = take(4 * SEQ).rearrange("p (u k) -> p u k", u=4)
        attn_t = take(4 * SEQ).rearrange("p (u s q) -> p u s q", u=4, s=TPG)
        alibi = take(2 * SEQ).rearrange("p (t k) -> p t k", t=TPG)
        take = carver(small)
        keys_sb = take(2 * PEER_HEADS * NKEYS)
        qt_sb = take(2 * T).rearrange("p (m t) -> p m t", m=2)
        masked = take(NT * 256).rearrange("p (t j) -> p t j", t=NT)
        cand = take(NT * 256).rearrange("p (t j) -> p t j", t=NT)
        onehot = take(NT * 256)
        slot_keys = take(2 * NT * SLOTS).rearrange("p (m t s) -> p m t s", m=2, t=NT)
        eidx = small[:, 8192:8704].bitcast(u32).rearrange("p (t s) -> p t s", t=NT)
        gates = small[:, 8704:9216].rearrange("p (t s) -> p t s", t=NT)
        mod_rows = small[0:GROUPS, 0:2 * NB].rearrange("g (r n) -> g r n", r=2)
        cols_in = small[:, 6 * NB + 256:6 * NB + 384]
        lam_in = small[:, 6 * NB:6 * NB + 4 * DQK].rearrange("p (v d) -> p v d", v=4)
        bias_rows = small[0:GROUPS, 3 * NB:5 * NB].rearrange("g (r n) -> g r n", r=2)
        ada_ring = [big_w[:, 0:8192], big_h]
        silu_r, silu_re = (small[0:GROUPS * KD, a:a + P] for a in (4096, 4096 + P))
        silu_b = big_x[:, 0:GROUPS * D].rearrange("p (g d) -> p g d", g=GROUPS)
        col_ring = big_x[:, GROUPS * D:GROUPS * D + 4 * PIECE].rearrange("p (r d) -> p r d", r=4)
        ada_ring = [a.rearrange("p (k n) -> p k n", k=KD) for a in ada_ring]
        wo_ring = [big_w[:, i * KD * WOC:(i + 1) * KD * WOC].rearrange("p (k n) -> p k n", k=KD) for i in range(2)]
        post1_sb, pre2_sb = (small[:, i * D:(i + 1) * D] for i in (1, 2))
        coefs = [[big_w[:, i * D:(i + 1) * D] for i in (4, 5, 6)], [small[:, 3 * D:4 * D], small[:, 4 * D:5 * D], big_w[:, 0:D]]]
        wq_ring = [big_w[:, 4096:8192], big_w[:, 8192:12288]]
        wq_ring = [w.rearrange("p (k n) -> p k n", k=KD) for w in wq_ring]
        h2_t = placed("h2_t", M0, [P, KD, T])
        gather_ring = small[:, 0:RING * D].rearrange("p (r d) -> p r d", r=RING)
        by_slot = small[:, 0:3 * ND].rearrange("p (v n) -> p v n", v=3)
        hot = small[:, 2048:6144].rearrange("p (r v x k) -> p r v x k", r=4, v=2, x=4)
        table_sb = arena[:, H0 + D:H0 + D + NKEYS * P].rearrange("p (i n) -> p i n", i=NKEYS)
        at = H0 + D
        raw_ring = placed("raw_ring", at, [P, 2, D])
        at += 2 * D
        g_ring = arena[:, at:at + 2 * ND].rearrange("p (r n) -> p r n", r=2)
        gelu_sb = arena[:, at + 2 * ND:at + 4 * ND].rearrange("p (r n) -> p r n", r=2)
        w_ring = arena[:, at + 4 * ND:at + 6 * ND].rearrange("p (r n) -> p r n", r=2)
        at += 6 * ND
        raw_hi = rounded("raw_hi", at, [P, 2, D])
        raw_lo = rounded("raw_lo", at + 2 * D, [P, 2, D])
        at = W0 + D
        h2_hi = rounded("h2_hi", at, [P, KD, ND])
        h2_lo = rounded("h2_lo", at + KD * ND, [P, KD, ND])
        wraw_ring = placed("wraw_ring", at, [P, 2, 2, ND])
        w_hi = rounded("w_hi", at + 4 * ND, [P, 2, 2, ND])
        w_lo = rounded("w_lo", at + 8 * ND, [P, 2, 2, ND])
        y_dense = arena[:, at + 12 * ND:at + 12 * ND + DT * D].rearrange("p (t d) -> p t d", t=DT)
        acc = big_h[:, 0:D]
        gate2_sb, post2_sb, out_sb, out2_sb = (small[:, i * D:(i + 1) * D] for i in range(4))
        take = carver(tiny)
        ss_x = take(8)
        rstd_x = take(8)
        nt_a, nt_b, nt_y = take(8), take(8), take(8)
        silu_c = take(2 * KD)
        silu_e = take(2 * KD)
        lg_all = take(2 * HEADS)
        lg_t = [take(2 * HEADS) for _ in range(3)]
        lg_h = take(2)
        lam_dot = take(4)
        lam = take(2)
        bn6 = take(NT * 6).rearrange("p (t s) -> p t s", t=NT)
        mv = take(NT * 2).rearrange("p (t s) -> p t s", t=NT)
        nmax = take(4 * 2).rearrange("p (u m) -> p u m", u=4)
        esum = take(4 * 2).rearrange("p (u m) -> p u m", u=4)
        coef = take(4 * 2).rearrange("p (u m) -> p u m", u=4)
        iota = sbuf("iota", [P, NKEYS])
        iota16 = iota[:, 0:TOPK]
        stage = [take(RING).bitcast(u32) for _ in range(2)]
        hid = take(RING)
        ss_out = take(4)
        dif_ss = take(4)
        sub_w = take(1)
        hid_all = take(SLOTS)
        mod_cols = hid_all.rearrange("p (g c) -> p g c", g=GROUPS)
        mod_part = take(4 * 8).rearrange("p (s g c) -> p s g c", s=2, g=GROUPS)
        take = carver(sbuf("ret_out", [P, 8 * P]))
        ret_o = take(NT * P).rearrange("p (t c) -> p t c", t=NT)
        diff_o = take(NT * P).rearrange("p (t c) -> p t c", t=NT)
        tops = sbuf("tops", [P, PIECE])
        products = tops[:, :]
        mod_bias, mod_late = tops[:, 0:P], tops[:, P:2 * P]
        take = carver(tops)
        top_v = take(2 * NT * TOPK).rearrange("p (m t k) -> p m t k", m=2, t=NT)
        top_i = take(2 * NT * TOPK).bitcast(u32).rearrange("p (m t k) -> p m t k", m=2, t=NT)
        top_if = take(2 * NT * TOPK).rearrange("p (m t k) -> p m t k", m=2, t=NT)
        best_v = take(NT * TOPK).rearrange("p (t k) -> p t k", t=NT)
        best_p = take(NT * TOPK).bitcast(u32).rearrange("p (t k) -> p t k", t=NT)
        part_u = take(NT * TOPK).bitcast(u32)
        part_f = take(NT * TOPK)
        pick = take(2 * NT * TOPK).rearrange("p (m t k) -> p m t k", m=2, t=NT)
        soft_e = take(NT * TOPK)
        pair_id = take(NT * TOPK).rearrange("p (t k) -> p t k", t=NT)

        psum = ctx.enter_context(nc.psum_tensor("ps_all", [P, 8 * NB], f32))

        def bank(i):
            return psum[:, i * NB:(i + 1) * NB]

        names = """consts rows_in x_in cols_in sumsq silu_e silu colsT cols_ev a1_cols lg_e lam_e lg_rdy
            silu_rows silu_out silu_in col_in0 col_in1 col_in2 col_in3 col_a col_used late_cols late_t late_row late_out bias_in
            ada_in0 ada_in1 ada_mm ada_row mod_out0 mod_out1 xs xtr xtr_act xtr_dve
            w_t_in w_v_in alibi_in proj proj_ev gate
            dlog dtab ret_s ret_pd ret_v ret_n dif_s dif_sd dif_m dif_e dif_c dif_t dif_te dif_v dif_sq dif_n out_t out_te
            wo_in0 wo_in1 wo_mm wo_act wo_dve coef_in coef o_sq x1 x1_sq h2 grp_done h2tr h2tr_ev
            wq_in0 wq_in1 key_in q_mm q_ev sc_mm sc_dve gl_in gl_exp eidx_rdy
            h2_hi h2_lo g_fin bs_t bs_ev g_ones g_hot g_mm g_ev g_out g_quarter0 g_quarter1 g_quarter2 g_quarter3 ru_in0 ru_in1 rg_in0 rg_in1 raw_hi raw_lo up_mm gelu w_rdy w_out0 w_out1
            h2_ps stage gr_in0 gr_in1 gr_in2 gr_in3 gr_used hid_rdy hid_gelu slot_w
            rv_in0 rv_in1 rw_in0 rw_in1 whi wlo down_mm down_ev acc_sq y y_out fin_in
            dve act spare""".split()
        S = {n: semaphore("s_" + n) for n in names}

        block = ctx.enter_context(nc.Block())

        def wait(eng, name, value):
            if not isinstance(value, int) or value > 0:
                eng.wait_ge(S[name], value)

        def wait_alone(eng, name, value):
            wait(eng, name, value)
            eng.sem_inc(S["spare"], 1)

        PRE1, GN, SUB = 4 * KD, 5 * KD, 5 * KD + HEADS
        MOD_ROWS = 2 * 2 * KD

        def groups_of(unit):
            return unit // TPG, unit % TPG

        @block.sync
        def _(sp):
            sp.dma_start(silu_c, ct).then_inc(S["consts"], 16)
            sp.dma_start(silu_r, c_rows).then_inc(S["consts"], 16)
            sp.dma_start(ident[:, :], ident_c).then_inc(S["consts"], 16)
            sp.dma_start(iota[:, :], iota_c).then_inc(S["consts"], 16)
            sp.dma_start(lg_all, decay.partition_broadcast(P)).then_inc(S["rows_in"], 16)
            sp.dma_start(lam_in, lams.partition_broadcast(P)).then_inc(S["rows_in"], 16)
            sp.dma_start(cols_in[MOD_ROWS:MOD_ROWS + KD + HEADS + 1, :], rows).then_inc(S["cols_in"], 16)

            def ada_load(n, r):
                sp.dma_start(ada_ring[r], ada_w[ds(n, 1)].rearrange("a p k n -> p (a k) n")).then_inc(S[f"ada_in{r}"], 16)
                sp.dma_start(bias_rows[:, r, :], ada_b[:, ds(n * NB, NB)].partition_broadcast(GROUPS)).then_inc(S[f"ada_in{r}"], 16)

            def mod_store(n, r):
                sp.wait_ge(S["ada_row"], n + 1)
                sp.dma_start(mod_d[:, ds(n * NB, NB)], mod_rows[:, r, :]).then_inc(S[f"mod_out{r}"], 16)

            for r in range(2):
                ada_load(r, r)
            for t in range(NT):
                sp.dma_start(x_sb[:, t, :], x[t * P:(t + 1) * P, :]).then_inc(S["x_in"], 16)
            sp.wait_ge(S["silu_rows"], 1)
            sp.dma_start(silu_d.rearrange("g (k p) -> (g k) p", p=P), silu_r).then_inc(S["silu_out"], 16)
            with sp.Fori(0, ADA_BLOCKS // 2 - 1) as i:
                for r in range(2):
                    mod_store(i * 2 + r, r)
                    ada_load(i * 2 + r + 2, r)
            for r in range(2):
                mod_store(ADA_BLOCKS - 2 + r, r)
            for r in range(2):
                sp.wait_ge(S[f"mod_out{r}"], 16 * (ADA_BLOCKS // 2))
            sp.wait_ge(S["silu_out"], 16)
            for g in range(GROUPS):
                sp.dma_start(cols_in[g * 2 * KD:(g + 1) * 2 * KD, :],
                             mod_d[g, 0:2 * D].rearrange("(r c) -> r c", c=P)).then_inc(S["cols_in"], 16)

            def slab_loads(h):
                wait(sp, "proj", 8 * (h - 1) + 4)
                sp.dma_start(slab_t, w_t[ds(h, 1)].rearrange("a p k n -> p (a k) n")).then_inc(S["w_t_in"], 16)
                wait(sp, "dif_sd", 4 * (h - 1))
                if isinstance(h, int) and h == 0:
                    return
                sp.dma_start(alibi, alibi_c[ds(h - 1, 1)].rearrange("a p t k -> p (a t) k")).then_inc(S["alibi_in"], 16)
                wait(sp, "proj", 8 * (h - 1) + 8)
                sp.dma_start(slab_v, w_v[ds(h, 1)].rearrange("a p k n -> p (a k) n")).then_inc(S["w_v_in"], 16)

            slab_loads(0)
            sp.dma_start(slab_v, w_v[0]).then_inc(S["w_v_in"], 16)
            sp.wait_ge(S["cols_ev"], 1)
            sp.wait_ge(S["lg_rdy"], 1)
            sp.dma_start(dist, dist_c).then_inc(S["rows_in"], 16)
            slab_loads(1)
            with sp.Fori(2, HEADS) as h:
                slab_loads(h)
            sp.wait_ge(S["dif_sd"], 4 * (HEADS - 1))
            sp.dma_start(alibi, alibi_c[HEADS - 1]).then_inc(S["alibi_in"], 16)

            def wo_load(n, r):
                sp.dma_start(wo_ring[r], w_o[ds(n, 1)].rearrange("a p k n -> p (a k) n")).then_inc(S[f"wo_in{r}"], 16)

            sp.wait_ge(S["proj"], 8 * HEADS)
            for r in range(2):
                wo_load(r, r)

            def coef_load(g, n):
                v = (2, 4, 3)[n]
                sp.dma_start(coefs[g][n], mod_d[g:g + 1, v * D:(v + 1) * D].partition_broadcast(P)).then_inc(S["coef_in"], 16)

            sp.wait_ge(S["col_used"], HEADS * PIECES)
            for g in range(GROUPS):
                sp.dma_start(mod_bias[g * LATE:(g + 1) * LATE, :], ada_b[0, 2 * D:MODS * D].rearrange("(c p) -> c p", p=P))\
                    .then_inc(S["bias_in"], 16)
            for t in range(NT):
                sp.dma_start(x_sb[:, t, :], x[t * P:(t + 1) * P, :]).then_inc(S["x_in"], 16)
            sp.wait_ge(S["late_row"], 1)
            for g in range(GROUPS):
                sp.dma_start(mod_d[g, 2 * D:MODS * D].rearrange("(c p) -> c p", p=P), mod_late[g * LATE:(g + 1) * LATE, :])\
                    .then_inc(S["late_out"], 16)
            sp.wait_ge(S["late_out"], 32)
            sp.wait_ge(S["out_te"], 2 * HEADS)
            sp.dma_start(post1_sb, post1.partition_broadcast(P)).then_inc(S["coef_in"], 16)
            sp.dma_start(pre2_sb, pre2.partition_broadcast(P)).then_inc(S["coef_in"], 16)
            for g, n in ((0, 0), (0, 1), (1, 0), (1, 1), (0, 2)):
                coef_load(g, n)
            with sp.Fori(1, D // WOC // 2) as i:
                for r in range(2):
                    sp.wait_ge(S["wo_mm"], (i * 2 + r - 1) * NT)
                    wo_load(i * 2 + r, r)
            sp.wait_ge(S["wo_mm"], D // WOC * NT)
            coef_load(1, 2)
            sp.dma_start(wq_ring[0], w_q[0]).then_inc(S["wq_in0"], 16)
            sp.dma_start(keys_sb, keys_t).then_inc(S["key_in"], 16)
            sp.wait_ge(S["grp_done"], 1)
            sp.dma_start(wq_ring[1], w_q[1]).then_inc(S["wq_in1"], 16)
            with sp.Fori(1, PEER_HEADS // 2) as i:
                for r in range(2):
                    sp.wait_ge(S["q_mm"], 2 * (i * 2 + r - 1))
                    sp.dma_start(wq_ring[r], w_q[ds(i * 2 + r, 1)].rearrange("a p k n -> p (a k) n")).then_inc(S[f"wq_in{r}"], 16)

            for t in range(DT):
                sp.wait_ge(S["g_ev"], 32 * (t + 1) + 4)
                stored = g_d[:, :, t * P:(t + 1) * P].rearrange("i j n -> j i n")
                if t < DT - 1:
                    sp.dma_start(stored, table_sb).then_inc(S["g_out"], 16)
                    continue
                for q in range(4):
                    i = slice(q * NKEYS // 4, (q + 1) * NKEYS // 4)
                    sp.dma_start(stored[:, i, :], table_sb[:, i, :]).then_inc(S[f"g_quarter{q}"], 16)
            sp.wait_ge(S["g_out"], 16 * (DT - 1) + 1)

            def u_load(n, r):
                wait(sp, "raw_lo", n - 1)
                sp.dma_start(raw_ring[:, r, :], u_t[ds(n, 1)].rearrange("a p d -> p (a d)")).then_inc(S[f"ru_in{r}"], 16)

            def g_load(n, r):
                wait(sp, "w_rdy", n + 1)
                sp.dma_start(g_ring[:, r, :], g_d[ds(n, 1)].rearrange("a p n -> p (a n)")).then_inc(S[f"rg_in{r}"], 16)

            def up_store(n, r):
                sp.wait_ge(S["w_rdy"], n + 3)
                sp.dma_start(w_d[ds(n, 1)].rearrange("a p n -> p (a n)"), w_ring[:, r, :]).then_inc(S[f"w_out{r}"], 16)

            sp.wait_ge(S["g_quarter0"], 16)
            for r in range(2):
                u_load(r, r)
            for q in range(1, 4):
                sp.wait_ge(S[f"g_quarter{q}"], 16)
            for r in range(2):
                g_load(r, r)
                u_load(r + 2, r)
            with sp.Fori(1, NKEYS // 2 - 1) as i:
                for r in range(2):
                    u_load(2 * i + r + 2, r)
                    g_load(2 * i + r, r)
                    up_store(2 * i + r - 2, r)
            for r in range(2):
                g_load(NKEYS - 2 + r, r)
                up_store(NKEYS - 4 + r, r)
            for r in range(2):
                up_store(NKEYS - 2 + r, r)
            for r in range(2):
                sp.wait_ge(S[f"w_out{r}"], 16 * NKEYS // 2)

            def down_loads(half, m, r, n):
                wait(sp, "raw_lo", NKEYS + n - 1)
                v = v_tab[ds(m * 2 * P, 2 * P), ds(half * HALF, HALF)].rearrange("(e p) d -> p e d", e=2)
                sp.dma_start(raw_ring[:, r, :].rearrange("p (e d) -> p e d", e=2), v).then_inc(S[f"rv_in{r}"], 16)
                wait(sp, "wlo", n - 1)
                sp.dma_start(wraw_ring[:, r, :, :], w_d[ds(2 * m, 2)].rearrange("e p n -> p e n")).then_inc(S[f"rw_in{r}"], 16)

            sp.wait_ge(S["up_mm"], NKEYS)
            for r in range(2):
                down_loads(0, r, r, r)
            with sp.Fori(1, PAIRS // 2) as i:
                for r in range(2):
                    down_loads(0, 2 * i + r, r, 2 * i + r)
            with sp.Fori(0, PAIRS // 2) as i:
                for r in range(2):
                    down_loads(1, 2 * i + r, r, PAIRS + 2 * i + r)

            sp.wait_ge(S["gr_used"], 2 * SLOTS + RING)
            sp.dma_start(post2_sb, post2.partition_broadcast(P)).then_inc(S["fin_in"], 16)
            for t in range(NT):
                g = t // TPG
                if t % TPG == 0:
                    wait(sp, "y", t)
                    sp.dma_start(gate2_sb, mod_d[g:g + 1, 5 * D:6 * D].partition_broadcast(P)).then_inc(S["fin_in"], 16)
                sp.wait_ge(S["y"], t + 1)
                sp.dma_start(out[t * P:(t + 1) * P, :], out2_sb if t % 2 else out_sb).then_inc(S["y_out"], 16)
            sp.wait_ge(S["y_out"], 16 * NT)

        @block.tensor
        def _(pe):
            mm = nc.tensor.matmul

            def ada_block(i, r):
                n = i * 2 + r
                wait(pe, f"ada_in{r}", 32 * (i + 1))
                wait(pe, "ada_row", n - 1)
                for k in range(KD):
                    last = mm(bank(r)[0:GROUPS, :], silu_c[:, k * GROUPS:(k + 1) * GROUPS], ada_ring[r][:, k, :],
                              start=k == 0, stop=k == KD - 1)
                last.then_inc(S["ada_mm"], 1)

            pe.wait_ge(S["silu"], 1)
            for r in range(2):
                ada_block(0, r)
            with pe.Fori(1, ADA_BLOCKS // 2) as i:
                for r in range(2):
                    ada_block(i, r)

            pe.wait_ge(S["consts"], 64)
            pe.wait_ge(S["cols_in"], 48)
            n_rows = MOD_ROWS + KD + HEADS + 1
            nc.tensor.transpose(bank(3)[:, 0:n_rows], cols_in[0:n_rows, :], ident[0:n_rows, 0:n_rows]).then_inc(S["colsT"], 1)

            pe.wait_ge(S["xs"], NT)
            for k in range(KD):
                if k >= 4:
                    wait(pe, "xtr_dve" if k % 2 else "xtr_act", (k - 4) // 2 + 1)
                for t in range(NT):
                    last = nc.tensor.transpose(bank(4 + k % 4)[:, t * P:(t + 1) * P],
                                               big_m[:, t * D + k * P:t * D + (k + 1) * P], ident[:, :])
                last.then_inc(S["xtr"], 1)

            def project(h, n):
                if n == 0:
                    wait(pe, "w_t_in", 16 * (h + 1))
                if n == 4:
                    wait(pe, "w_v_in", 16 * (h + 1))
                if n < 4:
                    wait(pe, "gate", 4 * (h - 1) + n + 1)
                else:
                    wait(pe, "proj_ev", 8 * h + n - 3)
                for k in range(KD):
                    if n < 4:
                        last = mm(bank(n), slab_t[:, k, n * P:(n + 1) * P], h_t[:, k, :], start=k == 0, stop=k == KD - 1)
                    else:
                        last = mm(bank(n - 4)[:, 0:3 * P], h_t[:, k, (n - 4) * P:(n - 3) * P], slab_v[:, k, :],
                                  start=k == 0, stop=k == KD - 1)
                last.then_inc(S["proj"], 1)

            def ret_scores(a, g):
                wait(pe, "proj_ev", 8 * a + 2)
                wait(pe, "out_te", 2 * (a - 1) + g + 1)
                for s in range(TPG):
                    last = mm(bank(4 + g)[:, s * SEQ:(s + 1) * SEQ], k_t[:, (g * TPG + s) * P:(g * TPG + s + 1) * P],
                              q_t[:, g * SEQ:(g + 1) * SEQ], start=True, stop=True)
                last.then_inc(S["ret_s"], 1)

            def dif_scores(a, u):
                g, m = groups_of(u)
                wait(pe, "proj_ev", 8 * a + 4)
                if u < 2:
                    wait(pe, "dif_n", 4 * (a - 1) + u + 3)
                else:
                    wait(pe, "ret_pd", 2 * a + u - 1)
                b = bank(6 + u if u < 2 else 2 + u)
                for t in range(g * TPG, (g + 1) * TPG):
                    last = mm(b[:, t % TPG * SEQ:(t % TPG + 1) * SEQ], dq_t[m * DQK:(m + 1) * DQK, t * P:(t + 1) * P],
                              dk_t[m * DQK:(m + 1) * DQK, g * SEQ:(g + 1) * SEQ], start=True, stop=True)
                last.then_inc(S["dif_s"], 1)

            def ret_values(a, g):
                wait(pe, "dif_sd", 4 * a + g + 1)
                wait(pe, "ret_pd", 2 * a + g + 1)
                wait(pe, "proj_ev", 8 * a + 6 + 2 * g)
                for tt in range(TPG):
                    for s in range(TPG):
                        last = mm(bank(6 + g)[:, tt * P:(tt + 1) * P], ret_p[:, g, s, tt * P:(tt + 1) * P],
                                  vd[:, g * TPG + s, 0, :], start=s == 0, stop=s == TPG - 1)
                last.then_inc(S["ret_v"], 1)

            def dif_transposes(a, u):
                wait(pe, "dif_c", 4 * a + u + 1)
                if u < 2:
                    wait(pe, "dif_sd", 4 * a + u + 3)
                else:
                    wait(pe, "dif_te", 4 * a + u - 1)
                for s in range(TPG):
                    last = nc.tensor.transpose(bank(4 + u % 2)[:, s * P:(s + 1) * P], attn[:, u, s * P:(s + 1) * P], ident[:, :])
                last.then_inc(S["dif_t"], 1)

            def dif_values(a, u):
                g, qt = groups_of(u)
                wait(pe, "dif_te", 4 * a + u + 1)
                if u < 2:
                    wait(pe, "ret_n", 2 * a + u + 1)
                else:
                    wait(pe, "dif_n", 4 * a + u - 1)
                for s in range(TPG):
                    last = mm(bank(6 + u % 2)[:, 0:P], attn_t[:, u, s, :], vd[:, g * TPG + s, 1, :],
                              start=s == 0, stop=s == TPG - 1)
                last.then_inc(S["dif_v"], 1)

            def out_transposes(a, w):
                wait(pe, "dif_te", 4 * a + 3 + w)
                if w == 0:
                    wait(pe, "ret_n", 2 * a + 2)
                else:
                    wait(pe, "dif_n", 4 * a + 4)
                src = diff_o if w else ret_o
                for t in range(NT):
                    last = nc.tensor.transpose(bank(4 + w)[:, t * P:(t + 1) * P], src[:, t, :], ident[:, :])
                last.then_inc(S["out_t"], 1)

            def head_step(h, a):
                def p(n):
                    if h is not None:
                        project(h, n)

                def step(f, *units):
                    if a is not None:
                        for u in units:
                            f(a, u)
                p(0)
                step(ret_scores, 0, 1)
                step(dif_scores, 0, 1)
                p(1)
                step(dif_scores, 2, 3)
                p(2)
                step(ret_values, 0, 1)
                p(3)
                step(dif_transposes, 0, 1)
                p(4)
                step(dif_values, 0, 1)
                step(dif_transposes, 2, 3)
                p(5)
                step(dif_values, 2, 3)
                p(6)
                p(7)
                step(out_transposes, 0, 1)

            pe.wait_ge(S["xtr_act"], KD // 2)
            pe.wait_ge(S["xtr_dve"], KD // 2)
            head_step(0, None)
            head_step(1, 0)
            with pe.Fori(2, HEADS) as h:
                head_step(h, h - 1)
            head_step(None, HEADS - 1)

            def wo_block(i, r):
                wait(pe, f"wo_in{r}", 16 * (i + 1))
                wait(pe, "wo_dve" if r else "wo_act", NT * i)
                for t in range(NT):
                    for k in range(KD):
                        last = mm(bank(4 * r + t)[:, 0:WOC], mix_t[:, k, t * P:(t + 1) * P], wo_ring[r][:, k, :],
                                  start=k == 0, stop=k == KD - 1)
                    last.then_inc(S["wo_mm"], 1)

            pe.wait_ge(S["out_te"], 2 * HEADS)
            pe.wait_ge(S["late_cols"], 1)
            nc.tensor.transpose(bank(7)[:, 0:P], hid_all, ident[:, :]).then_inc(S["late_t"], 1)
            wo_block(0, 0)
            pe.wait_ge(S["late_row"], 1)
            wo_block(0, 1)
            with pe.Fori(1, D // WOC // 2) as i:
                for r in range(2):
                    wo_block(i, r)

            pe.wait_ge(S["wo_act"], NT * D // WOC // 2)
            for t in range(NT):
                pe.wait_ge(S["h2"], t + 1)
                for kk in range(4):
                    wait(pe, "h2tr_ev", 4 * (t - 1) + kk + 1)
                    for j in range(4):
                        k = 4 * kk + j
                        last = nc.tensor.transpose(bank(kk)[:, j * P:(j + 1) * P], o_sb[:, t, k * P:(k + 1) * P], ident[:, :])
                    last.then_inc(S["h2tr"], 1)

            def route_head(i, r):
                hd = i * 2 + r
                wait(pe, f"wq_in{r}", 16 * (i + 1))
                for m in range(2):
                    wait(pe, "q_ev", 2 * (hd - 1) + m + 1)
                    for k in range(KD):
                        last = mm(bank(m), wq_ring[r][:, k, m * P:(m + 1) * P], h2_t[:, k, :], start=k == 0, stop=k == KD - 1)
                    last.then_inc(S["q_mm"], 1)
                for m in range(2):
                    wait(pe, "q_ev", 2 * hd + m + 1)
                    wait(pe, "sc_dve", 2 * (hd - 2) + m + 1)
                    for t in range(NT):
                        last = mm(bank(2 + m + 4 * r)[:, t * P:(t + 1) * P], qt_sb[:, m, t * P:(t + 1) * P],
                                  keys_sb[:, ds((2 * hd + m) * NKEYS, NKEYS)], start=True, stop=True)
                    last.then_inc(S["sc_mm"], 1)

            pe.wait_ge(S["h2tr_ev"], 4 * NT)
            pe.wait_ge(S["key_in"], 16)
            for r in range(2):
                route_head(0, r)
            with pe.Fori(1, PEER_HEADS // 2) as i:
                for r in range(2):
                    route_head(i, r)

            pe.wait_ge(S["g_fin"], 1)
            for v, src in enumerate((slot_keys[:, 0], slot_keys[:, 1], gates)):
                for t in range(DT):
                    last = nc.tensor.transpose(bank(4 + v)[:, t * P:(t + 1) * P], src[:, GATHERED + t, :], ident[:, :])
            last.then_inc(S["bs_t"], 1)
            pe.wait_ge(S["bs_ev"], 1)
            with pe.Fori(0, DT * P // 16) as i:
                for s in range(4):
                    n = i * 4 + s
                    wait(pe, "g_hot", n + 1)
                    wait(pe, "g_ev", n + 1)
                    for x in range(4):
                        last = mm(bank(4 + s)[:, x * P:(x + 1) * P], hot[:, s, 1, x, :], hot[:, s, 0, x, :],
                                  start=True, stop=True)
                    last.then_inc(S["g_mm"], 1)

            def split_products(b, parts, start, stop):
                (a_hi, a_lo), (b_hi, b_lo) = parts
                mm(b, a_hi, b_hi, start=start, stop=False)
                mm(b, a_hi, b_lo, start=False, stop=False)
                return mm(b, a_lo, b_hi, start=False, stop=stop)

            pe.wait_ge(S["h2_lo"], 1)
            with pe.Fori(0, NKEYS // 2) as i:
                for r in range(2):
                    n = 2 * i + r
                    wait(pe, "raw_lo", n + 1)
                    wait(pe, "gelu", n + 1)
                    for k in range(KD):
                        e = slice(k * P, (k + 1) * P)
                        last = split_products(bank(4 + r)[:, 0:ND], ((raw_hi[:, r, e], raw_lo[:, r, e]), (h2_hi[:, k, :], h2_lo[:, k, :])),
                                              k == 0, k == KD - 1)
                    last.then_inc(S["up_mm"], 1)

            def down_pair(n, r, first, final):
                wait(pe, "raw_lo", NKEYS + n + 1)
                wait(pe, "wlo", n + 1)
                for e in range(2):
                    start, stop = first and e == 0, final and e == 1
                    for t in range(DT):
                        toks = slice(t * P, (t + 1) * P)
                        hi, lo = w_hi[:, r, e, toks], w_lo[:, r, e, toks]
                        for w, vs in ((hi, raw_hi), (hi, raw_lo), (lo, raw_hi)):
                            for b in range(2):
                                cols_ = slice(e * HALF + b * NB, e * HALF + (b + 1) * NB)
                                last = mm(bank(2 * t + b), w, vs[:, r, cols_], start=start and w is hi and vs is raw_hi,
                                          stop=stop and w is lo)
                last.then_inc(S["down_mm"], 1)

            for half in range(2):
                if half:
                    pe.wait_ge(S["down_ev"], 2 * DT)
                for r in range(2):
                    down_pair(half * PAIRS + r, r, r == 0, False)
                with pe.Fori(1, PAIRS // 2 - 1) as i:
                    for r in range(2):
                        down_pair(half * PAIRS + 2 * i + r, r, False, False)
                for r in range(2):
                    down_pair((half + 1) * PAIRS - 2 + r, r, False, r == 1)

        @block.scalar
        def _(act):
            acti = nc.scalar.activation
            act.wait_ge(S["consts"], 16 * 4)
            acti(silu_e, silu_c, ACT.Exp, scale=-1.0).then_inc(S["silu_e"], 1)
            acti(silu_re, silu_r, ACT.Exp, scale=-1.0).then_inc(S["silu_e"], 1)
            act.wait_ge(S["lg_e"], 1)
            acti(lg_t[0], lg_t[0], ACT.Exp, scale=-1.0).then_inc(S["lg_e"], 1)
            act.wait_ge(S["lam_e"], 1)
            acti(lam_dot[:, 0:2], lam_dot[:, 0:2], ACT.Exp).then_inc(S["lam_e"], 1)
            for t in range(NT):
                act.wait_ge(S["x_in"], 16 * NT)
                wait(act, "sumsq", t)
                acti(psum[:, 4 * NB:8 * NB], x_sb[:, t, :], ACT.Square, accum_out=ss_x[:, t:t + 1]).then_inc(S["sumsq"], 1)
            act.wait_ge(S["colsT"], 1)
            acti(cols[:, 0:SUB + 1], bank(3)[:, 0:SUB + 1], ACT.Copy).then_inc(S["cols_ev"], 1)
            act.wait_ge(S["a1_cols"], 1)
            for k in range(0, KD, 2):
                act.wait_ge(S["xtr"], k + 1)
                for g in range(GROUPS):
                    last = acti(h_t[:, k, g * SEQ:(g + 1) * SEQ], bank(4 + k % 4)[:, g * SEQ:(g + 1) * SEQ], ACT.Identity,
                                scale=cols[:, (2 * g + 1) * KD + k:(2 * g + 1) * KD + k + 1],
                                bias=cols[:, 2 * g * KD + k:2 * g * KD + k + 1])
                last.then_inc(S["xtr_act"], 1)

            def decay_exp(a):
                act.wait_ge(S["dlog"], a + 1)
                wait(act, "ret_pd", 2 * a)
                acti(decay_tab, decay_log, ACT.Exp).then_inc(S["dtab"], 1)

            def evacuate(h, n):
                wait(act, "proj", 8 * h + n + 1)
                if n < 4:
                    wait(act, "ret_s" if n < 2 else "dif_s", 2 * h if n < 2 else 4 * h)
                    dst = (k_t, q_t, dk_t, dq_t)[n]
                    acti(dst, bank(n), ACT.Copy, scale=P ** -0.5 if n == 0 else 1.0).then_inc(S["proj_ev"], 1)
                else:
                    t = n - 4
                    g = t // TPG
                    wait(act, "ret_v", 2 * (h - 1) + g + 1)
                    wait(act, "dif_v", 4 * (h - 1) + 2 * g + 2)
                    wait(act, "gate", 4 * (h - 1) + t + 1)
                    v = bank(t)[:, 0:3 * P].rearrange("p (m c) -> p m c", m=3)
                    acti(vd[:, t, :, :], v[:, 0:3:2, :], ACT.Copy)
                    acti(e_g[:, t, :], v[:, 1, :], ACT.Exp, scale=-1.0).then_inc(S["proj_ev"], 1)

            def soft_exp(a, u):
                wait(act, "dif_m", 4 * a + u // TPG * TPG + 2)
                for m in range(2):
                    last = acti(soft[:, u, m, :], soft[:, u, m, :], ACT.Exp, scale=DQK ** -0.5, bias=nmax[:, u, m:m + 1],
                                accum_out=esum[:, u, m:m + 1])
                last.then_inc(S["dif_e"], 1)

            def attn_evacuate(a, u):
                wait(act, "dif_t", 4 * a + u + 1)
                wait(act, "dif_v", 4 * (a - 1) + u + 1)
                acti(attn_t[:, u, :, :], bank(4 + u % 2)[:, 0:SEQ].rearrange("p (s q) -> p s q", s=TPG), ACT.Copy)\
                    .then_inc(S["dif_te"], 1)

            def dif_square(a, u):
                wait(act, "dif_v", 4 * a + u + 1)
                acti(soft[:, u, 0, 0:P], bank(6 + u % 2)[:, 0:P], ACT.Square, accum_out=dif_ss[:, u:u + 1])\
                    .then_inc(S["dif_sq"], 1)

            def out_evacuate(a, w):
                wait_alone(act, "out_t", 2 * a + w + 1)
                scale = sub_w if w else cols[:, ds(GN + a, 1)]
                acti(mix_t[:, ds(a + w * HEADS, 1), :].rearrange("p a t -> p (a t)"), bank(4 + w), ACT.Copy, scale=scale)\
                    .then_inc(S["out_te"], 1)

            def head_step(h, a):
                def p(*ns):
                    if h is not None:
                        for n in ns:
                            evacuate(h, n)

                def step(f, *units):
                    if a is not None:
                        for u in units:
                            f(a, u)
                if a is not None:
                    decay_exp(a)
                p(0)
                step(soft_exp, 0, 1)
                p(1)
                step(soft_exp, 2, 3)
                p(2, 3)
                step(attn_evacuate, 0, 1)
                p(4)
                step(dif_square, 0, 1)
                step(attn_evacuate, 2, 3)
                p(5)
                step(dif_square, 2, 3)
                p(6, 7)
                step(out_evacuate, 0, 1)

            head_step(0, None)
            head_step(1, 0)
            with act.Fori(2, HEADS) as h:
                head_step(h, h - 1)
            head_step(None, HEADS - 1)

            def wo_evacuate(i):
                for t in range(NT):
                    wait_alone(act, "wo_mm", (2 * i) * NT + t + 1)
                    acti(o_sb[:, t, ds(2 * i * WOC, WOC)], bank(t)[:, 0:WOC], ACT.Copy).then_inc(S["wo_act"], 1)

            with act.Fori(0, D // WOC // 2) as i:
                wo_evacuate(i)
            act.wait_ge(S["wo_dve"], NT * D // WOC // 2)
            act.wait_ge(S["wo_act"], NT * D // WOC // 2)
            junk = psum[:, 4 * NB:8 * NB]
            for t in range(NT):
                wait(act, "o_sq", t)
                acti(junk, o_sb[:, t, :], ACT.Square, accum_out=ss_x[:, t:t + 1]).then_inc(S["o_sq"], 1)

            def h2_evacuate(t):
                for kk in range(4):
                    act.wait_ge(S["h2tr"], 4 * t + kk + 1)
                    acti(h2_t[:, 4 * kk:4 * kk + 4, t * P:(t + 1) * P], bank(kk).rearrange("p (j c) -> p j c", j=4), ACT.Copy)\
                        .then_inc(S["h2tr_ev"], 1)

            act.wait_ge(S["o_sq"], NT)
            for t in range(NT):
                act.wait_ge(S["x1"], t + 1)
                wait(act, "x1_sq", t)
                acti(junk, x_sb[:, t, :], ACT.Square, accum_out=ss_x[:, 4 + t:5 + t]).then_inc(S["x1_sq"], 1)
                if t >= 1:
                    h2_evacuate(t - 1)
            h2_evacuate(NT - 1)

            def query_evacuate(i):
                for r in range(2):
                    for m in range(2):
                        hd = i * 2 + r
                        wait(act, "q_mm", 2 * hd + m + 1)
                        wait(act, "sc_mm", 2 * (hd - 1) + m + 1)
                        acti(qt_sb[:, m, :], bank(m), ACT.Copy).then_inc(S["q_ev"], 1)

            query_evacuate(0)
            with act.Fori(1, PEER_HEADS // 2) as i:
                query_evacuate(i)
            act.wait_ge(S["gl_in"], 1)
            acti(gates, gates, ACT.Exp).then_inc(S["gl_exp"], 1)

            act.wait_ge(S["q_mm"], 2 * PEER_HEADS)
            acti(h2_hi[:, :, :], h2_t[:, :, GATHERED * P:T], ACT.Copy).then_inc(S["h2_hi"], 1)
            act.wait_ge(S["sc_dve"], 2 * PEER_HEADS)
            acti(psum[:, 0:D], o_sb[:, 0, :], ACT.Copy).then_inc(S["h2_ps"], 1)
            act.wait_ge(S["bs_t"], 1)
            acti(by_slot, psum[:, 4 * NB:7 * NB].rearrange("p (v n) -> p v n", v=3)[:, :, 0:ND], ACT.Copy).then_inc(S["bs_ev"], 1)
            act.wait_ge(S["h2_lo"], 1)
            with act.Fori(0, DT) as t:
                with act.Fori(0, P // 16) as q:
                    for s in range(4):
                        n = t * 32 + q * 4 + s
                        if s == 0:
                            wait_alone(act, "g_out", 16 * t + 1)
                        wait_alone(act, "g_mm", n + 5)
                        acti(table_sb[:, :, ds(q * 16 + s * 4, 4)], bank(4 + s).rearrange("p (x i) -> p i x", x=4), ACT.Copy)\
                            .then_inc(S["g_ev"], 1)

            def high_part(n, r, sem, count):
                wait(act, f"{sem}_in{r}", count)
                return acti(raw_hi[:, r, :], raw_ring[:, r, :], ACT.Copy)

            def up_gelu(n, r):
                wait(act, "up_mm", n + 1)
                wait(act, "w_rdy", n + 1)
                acti(gelu_sb[:, r, :], bank(4 + r)[:, 0:ND], ACT.Gelu).then_inc(S["gelu"], 1)

            act.wait_ge(S["g_quarter1"], 16)
            for r in range(2):
                high_part(r, r, "ru", 16).then_inc(S["raw_hi"], 1)
            act.wait_ge(S["g_quarter3"], 16)
            with act.Fori(1, NKEYS // 2) as i:
                for r in range(2):
                    n = 2 * i + r
                    wait(act, "up_mm", n - 1)
                    high_part(n, r, "ru", 16 * (i + 1)).then_inc(S["raw_hi"], 1)
                    up_gelu(n - 2, r)
            for r in range(2):
                up_gelu(NKEYS - 2 + r, r)
            act.wait_ge(S["hid_rdy"], SLOTS // RING + 1)
            acti(hid_all, hid_all, ACT.Gelu).then_inc(S["hid_gelu"], 1)

            def down_parts(n, r, uses):
                wait(act, "down_mm", n - 1)
                high_part(n, r, "rv", 16 * (uses + 1)).then_inc(S["raw_hi"], 1)
                wait(act, f"rw_in{r}", 16 * (uses + 1))
                acti(w_hi[:, r, :, :], wraw_ring[:, r, :, :], ACT.Copy).then_inc(S["whi"], 1)

            def down_evacuate(half):
                act.wait_ge(S["down_mm"], (half + 1) * PAIRS)
                for t in range(DT):
                    last = acti(y_dense[:, t, half * HALF:(half + 1) * HALF], psum[:, 2 * t * NB:2 * (t + 1) * NB], ACT.Copy)
                    last.then_inc(S["down_ev"], 2)

            for r in range(2):
                down_parts(r, r, 0)
            with act.Fori(1, PAIRS // 2) as i:
                for r in range(2):
                    down_parts(2 * i + r, r, i)
            for r in range(2):
                down_parts(PAIRS + r, r, PAIRS // 2)
            down_evacuate(0)
            with act.Fori(1, PAIRS // 2) as i:
                for r in range(2):
                    down_parts(PAIRS + 2 * i + r, r, PAIRS // 2 + i)
            down_evacuate(1)
            act.wait_ge(S["down_ev"], 4 * DT)
            act.wait_ge(S["gr_used"], 2 * SLOTS + RING)
            for t in range(NT):
                wait(act, "acc_sq", t)
                acti(junk, acc if t == 0 else y_dense[:, t - 1, :], ACT.Square, accum_out=ss_out[:, t:t + 1]).then_inc(S["acc_sq"], 1)

        @block.vector
        def _(dve):
            vec = nc.vector
            chain = [0]

            def link(ins):
                chain[0] += 1
                ins.then_inc(S["dve"], 1)
                dve.wait_ge(S["dve"], chain[0])

            class Chain:
                def __init__(self, before, turn, per_turn):
                    self.base, self.n, self.per_turn = turn * per_turn + before, 0, per_turn

                def __call__(self, ins, alone=False):
                    self.n += 1
                    ins.then_inc(S["dve"], 1)
                    (wait_alone if alone else wait)(dve, "dve", self.base + self.n)

                def done(self):
                    assert self.n == self.per_turn, self.n

            def rsqrt(link, out_, v, y, a):
                link(vec.tensor_scalar(a.bitcast(i32), v.bitcast(i32), 1, None, ALU.logical_shift_right))
                link(vec.tensor_scalar(y.bitcast(i32), a.bitcast(i32), -1.0, float(RSQRT_MAGIC), ALU.mult, ALU.add))
                for n in range(4):
                    link(vec.scalar_tensor_tensor(a, y, -0.5, y, ALU.mult, ALU.mult))
                    link(vec.tensor_tensor(a, a, v, ALU.mult))
                    link(vec.scalar_tensor_tensor(out_ if n == 3 else y, a, 1.5, y, ALU.add, ALU.mult))
            RSQRT = 14

            dve.wait_ge(S["silu_e"], 1)
            link(vec.tensor_scalar(silu_e, silu_e, 1.0, None, ALU.add))
            link(vec.reciprocal(silu_e, silu_e))
            vec.tensor_tensor(silu_c, silu_c, silu_e, ALU.mult).then_inc(S["silu"], 1)
            dve.wait_ge(S["silu_e"], 2)
            link(vec.tensor_scalar(silu_re, silu_re, 1.0, None, ALU.add))
            link(vec.reciprocal(silu_re, silu_re))
            vec.tensor_tensor(silu_r, silu_r, silu_re, ALU.mult).then_inc(S["silu_rows"], 1)
            dve.wait_ge(S["rows_in"], 32)
            e, z, q = lg_t
            link(vec.tensor_scalar(e, lg_all, -1.0, None, ALU.mult))
            vec.tensor_tensor(e, e, lg_all, ALU.max).then_inc(S["lg_e"], 1)
            dve.wait_ge(S["lg_e"], 2)
            link(vec.tensor_scalar(z, e, 2.0, None, ALU.add))
            link(vec.reciprocal(z, z))
            link(vec.tensor_tensor(z, z, e, ALU.mult))
            link(vec.tensor_tensor(q, z, z, ALU.mult))
            link(vec.tensor_scalar(e, q, 1.0 / 17, 1.0 / 15, ALU.mult, ALU.add))
            for n in (13, 11, 9, 7, 5, 3, 1):
                link(vec.tensor_tensor(e, e, q, ALU.mult))
                link(vec.tensor_scalar(e, e, 1.0 / n, None, ALU.add))
            link(vec.tensor_tensor(e, e, z, ALU.mult))
            link(vec.tensor_scalar(lg_all, lg_all, 0.0, None, ALU.min))
            link(vec.scalar_tensor_tensor(lg_all, e, -2.0, lg_all, ALU.mult, ALU.add))
            for n in range(2):
                last = vec.tensor_tensor_reduce(out=lam_in[:, 2 * n, :], in0=lam_in[:, 2 * n, :], in1=lam_in[:, 2 * n + 1, :],
                                                scale=1.0, scalar=0.0, op0=ALU.mult, op1=ALU.add, accum_out=lam_dot[:, n:n + 1])
            last.then_inc(S["lam_e"], 1)
            dve.wait_ge(S["lam_e"], 2)
            link(vec.tensor_tensor(lam[:, 0:1], lam_dot[:, 1:2], lam_dot[:, 0:1], ALU.subtract))
            vec.tensor_scalar(lam[:, 0:1], lam[:, 0:1], -LAM_INIT, None, ALU.add).then_inc(S["lg_rdy"], 1)
            def ada_row(i, r):
                wait(dve, "ada_mm", i * 2 + r + 1)
                wait(dve, f"mod_out{r}", 16 * i)
                vec.tensor_tensor(mod_rows[:, r, :], bank(r)[0:GROUPS, :], bias_rows[:, r, :], ALU.add).then_inc(S["ada_row"], 1)

            for r in range(2):
                ada_row(0, r)
            dve.wait_ge(S["sumsq"], NT)
            link(vec.tensor_scalar(nt_a[:, 0:NT], ss_x[:, 0:NT], 1.0 / D, EPS, ALU.mult, ALU.add))
            rsqrt(link, rstd_x[:, 0:NT], nt_a[:, 0:NT], nt_y[:, 0:NT], nt_b[:, 0:NT])

            for t in range(NT):
                vec.tensor_scalar(big_m[:, t * D:(t + 1) * D], x_sb[:, t, :], rstd_x[:, t:t + 1], None, ALU.mult).then_inc(S["xs"], 1)

            with dve.Fori(1, ADA_BLOCKS // 2) as i:
                for r in range(2):
                    ada_row(i, r)

            dve.wait_ge(S["cols_ev"], 1)
            link(vec.tensor_scalar(sub_w, cols[:, SUB:SUB + 1], 1.0 - LAM_INIT, None, ALU.mult))
            for g in range(GROUPS):
                sc = cols[:, (2 * g + 1) * KD:(2 * g + 2) * KD]
                last = vec.scalar_tensor_tensor(sc, sc, 1.0, cols[:, PRE1:PRE1 + KD], ALU.add, ALU.mult)
            last.then_inc(S["a1_cols"], 1)
            dve.wait_ge(S["a1_cols"], 1)
            for k in range(1, KD, 2):
                dve.wait_ge(S["xtr"], k + 1)
                for g in range(GROUPS):
                    last = vec.tensor_scalar(h_t[:, k, g * SEQ:(g + 1) * SEQ], bank(4 + k % 4)[:, g * SEQ:(g + 1) * SEQ],
                                             cols[:, (2 * g + 1) * KD + k:(2 * g + 1) * KD + k + 1],
                                             cols[:, 2 * g * KD + k:2 * g * KD + k + 1], ALU.mult, ALU.add)
                last.then_inc(S["xtr_dve"], 1)

            def decay_logs(a, link):
                wait(dve, "dtab", a)
                dve.sem_inc(S["spare"], 1)
                link(vec.tensor_copy(lg_h, lg_all[:, ds(2 * a, 2)]))
                link(vec.tensor_scalar(decay_log, dist[:, 1, :], lg_h[:, 1:2], None, ALU.mult))
                vec.scalar_tensor_tensor(decay_log, dist[:, 0, :], lg_h[:, 0:1], decay_log, ALU.mult, ALU.add).then_inc(S["dlog"], 1)

            def ret_decay(a, g, link):
                wait(dve, "ret_s", 2 * a + g + 1)
                wait(dve, "dtab", a + 1)
                wait(dve, "ret_v", 2 * (a - 1) + g + 1)
                for s in range(TPG):
                    last = vec.tensor_tensor(ret_p[:, g, s, :], bank(4 + g)[:, s * SEQ:(s + 1) * SEQ],
                                             decay_tab[:, P * (1 - s):P * (1 - s) + SEQ], ALU.mult)
                last.then_inc(S["ret_pd"], 1)

            def dif_soft(a, u, link):
                g, m = groups_of(u)
                units = slice(g * TPG, (g + 1) * TPG)
                wait(dve, "alibi_in", 16 * (a + 1))
                wait(dve, "dif_s", 4 * a + u + 1)
                b = bank(6 + u if u < 2 else 2 + u)
                vec.tensor_tensor(soft[:, units, m, :], b.rearrange("p (t k) -> p t k", t=TPG), alibi, ALU.add)\
                    .then_inc(S["dif_sd"], 1)
                wait(dve, "dif_sd", 4 * a + u + 1)
                link(vec.tensor_reduce(nmax[:, units, m], soft[:, units, m, :], axis=AX, op=ALU.max, negate=True))
                vec.tensor_scalar(nmax[:, units, m], nmax[:, units, m], DQK ** -0.5, None, ALU.mult).then_inc(S["dif_m"], 1)

            def dif_combine(a, u, link):
                wait(dve, "dif_e", 4 * a + u + 1)
                wait(dve, "dif_t", 4 * (a - 1) + u + 1)
                link(vec.reciprocal(coef[:, u, :], esum[:, u, :]))
                vec.tensor_scalar(coef[:, u, 1:2], coef[:, u, 1:2], lam[:, 0:1], None, ALU.mult)
                link(vec.tensor_scalar(attn[:, u, :], soft[:, u, 0, :], coef[:, u, 0:1], None, ALU.mult))
                vec.scalar_tensor_tensor(attn[:, u, :], soft[:, u, 1, :], coef[:, u, 1:2], attn[:, u, :], ALU.mult, ALU.add)\
                    .then_inc(S["dif_c"], 1)

            def ret_norm(a, g, link):
                wait(dve, "ret_v", 2 * a + g + 1)
                wait(dve, "out_t", 2 * a)
                for tt in range(TPG):
                    last = vec.bn_stats(bn6[:, g * TPG + tt, :], bank(6 + g)[:, tt * P:(tt + 1) * P])
                link(last, alone=True)
                for tt in range(TPG):
                    last = vec.bn_aggr(mv[:, g * TPG + tt, :], bn6[:, g * TPG + tt, :])
                link(last)
                link(vec.tensor_scalar(nt_a[:, 0:TPG], mv[:, g * TPG:(g + 1) * TPG, 1], EPS, None, ALU.add))
                rsqrt(link, nt_y[:, 4:4 + TPG], nt_a[:, 0:TPG], nt_y[:, 0:TPG], nt_b[:, 0:TPG])
                for tt in range(TPG):
                    t = g * TPG + tt
                    last = vec.tensor_scalar(ret_o[:, t, :], bank(6 + g)[:, tt * P:(tt + 1) * P], mv[:, t, 0:1],
                                             nt_y[:, 4 + tt:5 + tt], ALU.subtract, ALU.mult)
                link(last)
                vec.tensor_tensor(ret_o[:, g * TPG:(g + 1) * TPG, :], ret_o[:, g * TPG:(g + 1) * TPG, :],
                                  gate[:, g * TPG:(g + 1) * TPG, :], ALU.mult).then_inc(S["ret_n"], 1)

            def dif_norm(a, pair, link):
                wait(dve, "dif_sq", 4 * a + 2 * pair + 2)
                wait(dve, "out_t", 2 * a)
                link(vec.tensor_scalar(nt_a[:, 0:2], dif_ss[:, 2 * pair:2 * pair + 2], 1.0 / P, EPS, ALU.mult, ALU.add))
                rsqrt(link, nt_y[:, 4:6], nt_a[:, 0:2], nt_y[:, 0:2], nt_b[:, 0:2])
                for j in range(2):
                    vec.tensor_scalar(diff_o[:, 2 * pair + j, :], bank(6 + j)[:, 0:P], nt_y[:, 4 + j:5 + j], None, ALU.mult)\
                        .then_inc(S["dif_n"], 1)

            def silu_gate(h, t, link):
                wait(dve, "proj_ev", 8 * h + 5 + t)
                link(vec.tensor_scalar(e_g[:, t, :], e_g[:, t, :], 1.0, None, ALU.add))
                link(vec.reciprocal(e_g[:, t, :], e_g[:, t, :]))
                vec.tensor_tensor(gate[:, t, :], e_g[:, t, :], bank(t)[:, P:2 * P], ALU.mult).then_inc(S["gate"], 1)

            def late_pieces(h, pieces):
                for n in pieces:
                    c, half, place = n // 2, n % 2, n % 4
                    w = col_ring[:, place, :]
                    silu = [silu_b[:, g, half * PIECE:(half + 1) * PIECE] for g in range(GROUPS)]
                    wait(dve, f"col_in{place}", 16 * (h * (PIECES // 4) + n // 4 + 1))
                    wait(dve, "col_used", h * PIECES + n)
                    vec.tensor_tensor_reduce(out=products, in0=w, in1=silu[0], scale=1.0, scalar=0.0, op0=ALU.mult, op1=ALU.add,
                                             accum_out=mod_part[:, half, 0, c:c + 1]).then_inc(S["col_a"], 1)
                    wait(dve, "col_a", h * PIECES + n + 1)
                    vec.tensor_tensor_reduce(out=w, in0=w, in1=silu[1], scale=1.0, scalar=0.0, op0=ALU.mult, op1=ALU.add,
                                             accum_out=mod_part[:, half, 1, c:c + 1]).then_inc(S["col_used"], 1)

            def late_sums(h, link):
                wait(dve, "col_used", (h + 1) * PIECES)
                dve.sem_inc(S["spare"], 1)
                link(vec.tensor_tensor(mod_cols[:, :, ds(h * 8, 8)], mod_part[:, 0, :, :], mod_part[:, 1, :, :], ALU.add))

            def head_step(h, a, link):
                def step(f, *units):
                    if a is not None:
                        for u in units:
                            f(a, u, link)

                def late(*pieces):
                    if h is not None:
                        late_pieces(h, pieces)

                def gates_of(*tiles):
                    if h is not None:
                        for t in tiles:
                            silu_gate(h, t, link)
                step(ret_decay, 0, 1)
                step(dif_soft, 0, 1)
                late(0, 1, 2)
                step(dif_soft, 2, 3)
                late(3, 4, 5)
                step(dif_combine, 0, 1)
                late(6)
                step(ret_norm, 0, 1)
                late(7, 8, 9)
                step(dif_combine, 2, 3)
                late(10, 11)
                step(dif_norm, 0)
                gates_of(0, 1)
                late(12, 13)
                step(dif_norm, 1)
                gates_of(2)
                late(14, 15)
                gates_of(3)
                if h is not None:
                    late_sums(h, link)
                    decay_logs(h, link)

            def plain(ins, alone=False):
                link(ins)

            dve.wait_ge(S["rows_in"], 48)
            head_step(0, None, plain)
            head_step(1, 0, plain)
            PER_HEAD = 1 + 4 + 8 + 2 * (3 + RSQRT + 1) + 2 * (1 + RSQRT) + 8 + 2
            with dve.Fori(2, HEADS) as h:
                c = Chain(chain[0] - 2 * PER_HEAD, h, PER_HEAD)
                head_step(h, h - 1, c)
                c.done()
            chain[0] += (HEADS - 2) * PER_HEAD
            dve.sem_inc(S["late_cols"], 1)
            head_step(None, HEADS - 1, plain)
            dve.wait_ge(S["late_t"], 1)
            dve.wait_ge(S["bias_in"], 32)
            vec.tensor_tensor(mod_late, bank(7)[:, 0:P], mod_bias, ALU.add).then_inc(S["late_row"], 1)

            dve.wait_ge(S["coef_in"], 16 * 7)
            for g in range(GROUPS):
                vec.tensor_tensor(coefs[g][0], coefs[g][0], post1_sb, ALU.mult).then_inc(S["coef"], 1)
                vec.scalar_tensor_tensor(coefs[g][1], coefs[g][1], 1.0, pre2_sb, ALU.add, ALU.mult).then_inc(S["coef"], 1)

            with dve.Fori(0, D // WOC // 2) as i:
                for t in range(NT):
                    wait_alone(dve, "wo_mm", (2 * i + 1) * NT + t + 1)
                    vec.tensor_copy(o_sb[:, t, ds((2 * i + 1) * WOC, WOC)], bank(4 + t)[:, 0:WOC]).then_inc(S["wo_dve"], 1)

            dve.wait_ge(S["o_sq"], NT)
            link(vec.tensor_scalar(nt_a[:, 0:NT], ss_x[:, 0:NT], 1.0 / D, EPS, ALU.mult, ALU.add))
            rsqrt(link, rstd_x[:, 0:NT], nt_a[:, 0:NT], nt_y[:, 0:NT], nt_b[:, 0:NT])
            for g in range(GROUPS):
                gate1_sb, scale2_sb, shift2_sb = coefs[g]
                dve.wait_ge(S["coef"], 2 * GROUPS)
                if g:
                    dve.wait_ge(S["coef_in"], 16 * 8)
                for tt in range(TPG):
                    t = g * TPG + tt
                    link(vec.scalar_tensor_tensor(o_sb[:, t, :], o_sb[:, t, :], rstd_x[:, t:t + 1], gate1_sb, ALU.mult, ALU.mult))
                    dve.wait_ge(S["x_in"], 16 * 2 * NT)
                    vec.tensor_tensor(x_sb[:, t, :], x_sb[:, t, :], o_sb[:, t, :], ALU.add).then_inc(S["x1"], 1)
                tiles = slice(4 + g * TPG, 4 + (g + 1) * TPG)
                dve.wait_ge(S["x1_sq"], (g + 1) * TPG)
                link(vec.tensor_scalar(nt_a[:, 0:TPG], ss_x[:, tiles], 1.0 / D, EPS, ALU.mult, ALU.add))
                rsqrt(link, rstd_x[:, tiles], nt_a[:, 0:TPG], nt_y[:, 0:TPG], nt_b[:, 0:TPG])
                for tt in range(TPG):
                    t = g * TPG + tt
                    link(vec.scalar_tensor_tensor(o_sb[:, t, :], x_sb[:, t, :], rstd_x[:, 4 + t:5 + t], scale2_sb, ALU.mult, ALU.mult))
                    vec.tensor_tensor(o_sb[:, t, :], o_sb[:, t, :], shift2_sb, ALU.add).then_inc(S["h2"], 1)
                dve.wait_ge(S["h2"], TPG * (g + 1))
                dve.sem_inc(S["grp_done"], 1)

            def top16(values, work, best, where, link):
                for t in range(NT):
                    last = vec.max(best[:, t, 0:8], values(t))
                link(last, alone=True)
                for t in range(NT):
                    last = vec.match_replace(work(t), best[:, t, 0:8], values(t), LOWEST)
                link(last, alone=True)
                for t in range(NT):
                    last = vec.max(best[:, t, 8:16], work(t))
                link(last, alone=True)
                for t in range(NT):
                    vec.max_index(where[:, t, 8:16], best[:, t, 8:16], work(t))
                for t in range(NT):
                    last = vec.max_index(where[:, t, 0:8], best[:, t, 0:8], values(t))
                return last

            def route_head(i, r, link):
                hd = i * 2 + r
                for m in range(2):
                    b = bank(2 + m + 4 * r)
                    wait_alone(dve, "sc_mm", 2 * hd + m + 1)
                    top16(lambda t: b[:, t * P:(t + 1) * P], lambda t: masked[:, t, 0:NKEYS], top_v[:, m], top_i[:, m], link)\
                        .then_inc(S["sc_dve"], 1)
                wait(dve, "sc_dve", 2 * hd + 2)
                link(vec.tensor_copy(top_if, top_i))
                pairs = [P, NT, TOPK, TOPK]
                link(vec.tensor_tensor(cand.rearrange("p t (i j) -> p t i j", i=TOPK), top_v[:, 0].unsqueeze(3).to_broadcast(pairs),
                                       top_v[:, 1].unsqueeze(2).to_broadcast(pairs), ALU.add), alone=True)
                link(top16(lambda t: cand[:, t, :], lambda t: masked[:, t, :], best_v, best_p, link))
                hot = onehot.rearrange("p (t k i) -> p t k i", t=NT, k=TOPK)
                for m in range(2):
                    op, by = (ALU.bitwise_and, TOPK - 1) if m else (ALU.logical_shift_right, 4)
                    link(vec.tensor_scalar(part_u, best_p.rearrange("p t k -> p (t k)"), by, None, op))
                    link(vec.tensor_copy(part_f, part_u))
                    link(vec.tensor_tensor(hot, part_f.rearrange("p (t k) -> p t k", t=NT).unsqueeze(3).to_broadcast(pairs),
                                           iota16.unsqueeze(1).unsqueeze(1).to_broadcast(pairs), ALU.is_equal))
                    link(vec.tensor_tensor(hot, hot, top_if[:, m].unsqueeze(2).to_broadcast(pairs), ALU.mult))
                    link(vec.tensor_reduce(pick[:, m], hot, axis=AX, op=ALU.add))
                link(vec.scalar_tensor_tensor(pair_id.rearrange("p t k -> p (t k)"), pick[:, 0].rearrange("p t k -> p (t k)"),
                                              float(NKEYS), pick[:, 1].rearrange("p t k -> p (t k)"), ALU.mult, ALU.add), alone=True)
                for m in range(2):
                    vec.tensor_copy(slot_keys[:, m, :, ds(hd * TOPK, TOPK)], pick[:, m])
                vec.tensor_copy(eidx[:, :, ds(hd * TOPK, TOPK)], pair_id)
                link(vec.tensor_tensor(gates[:, :, ds(hd * TOPK, TOPK)], best_v, best_v[:, :, 0:1].to_broadcast([P, NT, TOPK]),
                                       ALU.subtract))
            PER_ROUTE = 3 * 3 + 4 + 10 + 1 + 0

            with dve.Fori(0, PEER_HEADS // 2) as i:
                c = Chain(chain[0], i, 2 * PER_ROUTE)
                for r in range(2):
                    route_head(i, r, c)
                c.done()
            chain[0] += PEER_HEADS * PER_ROUTE
            dve.sem_inc(S["gl_in"], 1)
            dve.wait_ge(S["gl_exp"], 1)
            by_head = gates.rearrange("p t (h k) -> p (t h) k", k=TOPK)
            sums = soft_e[:, 0:NT * PEER_HEADS]
            link(vec.tensor_reduce(sums, by_head, axis=AX, op=ALU.add))
            link(vec.reciprocal(sums, sums))
            link(vec.tensor_tensor(by_head, by_head, sums.unsqueeze(2).to_broadcast([P, NT * PEER_HEADS, TOPK]), ALU.mult))
            dve.sem_inc(S["g_fin"], 1)
            dve.wait_ge(S["h2_hi"], 1)
            vec.tensor_tensor(h2_lo[:, :, :], h2_t[:, :, GATHERED * P:T], h2_hi[:, :, :].bitcast(f32), ALU.subtract).then_inc(S["h2_lo"], 1)

            for name, n in (("g_ev", 4), ("g_mm", 4), ("g_out", 1), ("gelu", 2), ("gr_used", RING), ("hid_rdy", 1), ("w_rdy", 2)):
                dve.sem_inc(S[name], n)

            dve.wait_ge(S["bs_ev"], 1)
            with dve.Fori(0, DT * P // 16) as i:
                for s in range(4):
                    wait_alone(dve, "g_mm", i * 4 + s + 1)
                    shape = [P, 2, 4, NKEYS]
                    vec.tensor_tensor(hot[:, s, :, :, :], iota[:, :].unsqueeze(1).unsqueeze(1).to_broadcast(shape),
                                      by_slot[:, 0:2, ds(i * 16 + s * 4, 4)].unsqueeze(3).to_broadcast(shape), ALU.is_equal)\
                        .then_inc(S["g_ones"], 1)

            def low_part(n, r):
                wait(dve, "raw_hi", n + 1)
                vec.tensor_tensor(raw_lo[:, r, :], raw_ring[:, r, :], raw_hi[:, r, :].bitcast(f32), ALU.subtract).then_inc(S["raw_lo"], 1)

            def up_weights(n, r, uses):
                wait(dve, "gelu", n + 3)
                wait(dve, f"rg_in{r}", 16 * (uses + 1))
                wait(dve, f"w_out{r}", 16 * uses)
                vec.tensor_tensor(w_ring[:, r, :], gelu_sb[:, r, :], g_ring[:, r, :], ALU.mult).then_inc(S["w_rdy"], 1)

            def dot(i, j):
                if j == 0:
                    wait_alone(dve, "hid_rdy", i + 1)
                wait(dve, f"gr_in{j}", 16 * (i + 1))
                vec.tensor_tensor_reduce(out=gather_ring[:, j, :], in0=gather_ring[:, j, :], in1=psum[:, 0:D], scale=1.0, scalar=0.0,
                                         op0=ALU.mult, op1=ALU.add, accum_out=hid[:, j:j + 1]).then_inc(S["gr_used"], 1)

            def dots_done(i):
                wait_alone(dve, "gr_used", (i + 2) * RING)
                vec.tensor_copy(hid_all[:, ds(i * RING, RING)], hid).then_inc(S["hid_rdy"], 1)

            dve.wait_ge(S["h2_ps"], 1)
            dve.wait_ge(S["g_quarter2"], 16)
            for r in range(2):
                low_part(r, r)
            for j in range(2):
                dot(0, j)
            for j in range(2, RING):
                low_part(j, j % 2)
                dot(0, j)
                up_weights(j - 2, j % 2, 0)
            dots_done(0)
            with dve.Fori(1, SLOTS // RING) as i:
                for j in range(RING):
                    n = i * RING + j
                    wait(dve, "up_mm", n - 1)
                    low_part(n, j % 2)
                    dot(i, j)
                    up_weights(n - 2, j % 2, i * 2 + j // 2 - 1)
                dots_done(i)
            for r in range(2):
                up_weights(NKEYS - 2 + r, r, NKEYS // 2 - 1)
            vec.memset(acc, 0.0)
            dve.wait_ge(S["hid_gelu"], 1)
            link(vec.tensor_tensor(hid_all, hid_all, gates[:, 0, :], ALU.mult))

            def down_low(n, r):
                wait(dve, "down_mm", n - 1)
                low_part(NKEYS + n, r)
                wait(dve, "whi", n + 1)
                vec.tensor_tensor(w_lo[:, r, :, :], wraw_ring[:, r, :, :], w_hi[:, r, :, :].bitcast(f32), ALU.subtract).then_inc(S["wlo"], 1)

            def accumulate(i, j):
                wait(dve, f"gr_in{j}", 16 * (SLOTS // RING + i + 1))
                wait_alone(dve, "gr_used", SLOTS + RING + i * RING + j)
                vec.scalar_tensor_tensor(acc, gather_ring[:, j, :], hid_all[:, ds(i * RING + j, 1)], acc, ALU.mult, ALU.add)\
                    .then_inc(S["gr_used"], 1)

            for j in range(RING):
                down_low(j, j % 2)
                accumulate(0, j)
            with dve.Fori(1, SLOTS // RING) as i:
                for j in range(RING):
                    down_low(i * RING + j, j % 2)
                    accumulate(i, j)

            dve.wait_ge(S["acc_sq"], NT)
            link(vec.tensor_scalar(nt_a[:, 0:NT], ss_out[:, 0:NT], 1.0 / D, EPS, ALU.mult, ALU.add))
            rsqrt(link, nt_y[:, 4:4 + NT], nt_a[:, 0:NT], nt_y[:, 0:NT], nt_b[:, 0:NT])
            for t in range(NT):
                y = acc if t == 0 else y_dense[:, t - 1, :]
                o = out2_sb if t % 2 else out_sb
                if t % TPG == 0:
                    dve.wait_ge(S["fin_in"], 16 * (2 + t // TPG))
                    link(vec.tensor_tensor(gate2_sb, gate2_sb, post2_sb, ALU.mult))
                wait(dve, "y_out", 16 * (t - 1))
                link(vec.scalar_tensor_tensor(o, y, nt_y[:, 4 + t:5 + t], gate2_sb, ALU.mult, ALU.mult))
                vec.tensor_tensor(o, o, x_sb[:, t, :], ALU.add).then_inc(S["y"], 1)

        @block.gpsimd
        def _(pool):
            def gathers(table, before, i, parity):
                nc.gpsimd.tensor_copy(stage[parity], eidx[:, 0, ds(i * RING, RING)]).then_inc(S["stage"], 1)
                wait_alone(pool, "stage", before + i + 1)
                for j in range(RING):
                    wait_alone(pool, "gr_used", (before + i) * RING + j + 1)
                    pool.indirect_dma_start(out=gather_ring[:, j, :], out_offset=None, in_=table,
                                            in_offset=bass.IndirectOffsetOnAxis(ap=stage[parity][:, j:j + 1], axis=0))\
                        .then_inc(S[f"gr_in{j}"], 16)

            pool.wait_ge(S["xs"], NT)
            pool.wait_ge(S["silu_out"], 16)
            for g in range(GROUPS):
                pool.dma_start(silu_b[:, g, :], silu_d[g:g + 1, :].partition_broadcast(P)).then_inc(S["silu_in"], 16)
            pool.wait_ge(S["silu_in"], 32)

            def piece_loads(h, first):
                for n in range(PIECES):
                    if first and n < 4:
                        pass
                    else:
                        wait(pool, "col_used", h * PIECES + n - 3)
                    pool.dma_start(col_ring[:, n % 4, :], ada_wt[ds(h, 1), n // 2, :, n % 2, :].rearrange("a p k -> p (a k)"))\
                        .then_inc(S[f"col_in{n % 4}"], 16)

            piece_loads(0, True)
            with pool.Fori(1, HEADS) as h:
                piece_loads(h, False)

            with pool.Fori(0, DT * P // 16) as i:
                for s in range(4):
                    wait_alone(pool, "g_ones", i * 4 + s + 1)
                    gate_of = by_slot[:, 2, ds(i * 16 + s * 4, 4)].unsqueeze(2).to_broadcast([P, 4, NKEYS])
                    nc.gpsimd.tensor_tensor(hot[:, s, 1, :, :], hot[:, s, 1, :, :], gate_of, ALU.mult).then_inc(S["g_hot"], 1)

            pool.wait_ge(S["g_mm"], DT * P // 4 + 4)
            pool.wait_ge(S["g_hot"], DT * P // 4)
            for before, table in ((0, u_tab), (SLOTS // RING, v_tab)):
                with pool.Fori(0, SLOTS // RING // 2) as i:
                    for parity in range(2):
                        gathers(table, before, 2 * i + parity, parity)


_INS = ["x", "ct", "c_rows", "ada_w", "ada_wt", "ada_b", "rows", "w_t", "w_v", "w_o", "w_q", "keys_t", "decay", "lams", "post1", "pre2", "post2",
        "u_t", "u_tab", "v_tab", "ident", "dist", "alibi", "iota"]


def constants():
    s = np.arange(P)[:, None]
    rel = np.arange(384)[None, :] - P - s
    dist = np.stack([np.maximum(rel, 0), np.maximum(-rel, 0)], 1).astype(np.float32)
    slopes = 2.0 ** (-8.0 * np.arange(1, HEADS + 1) / HEADS)
    q = np.arange(SEQ).reshape(TPG, P).T
    away = np.abs(q[:, :, None] - np.arange(SEQ)[None, None, :])
    alibi = (-slopes[:, None, None, None] * DQK ** 0.5 * away[None]).astype(np.float32)
    return {"ident": np.eye(P, dtype=np.float32), "dist": dist, "alibi": alibi,
            "iota": np.tile(np.arange(NKEYS, dtype=np.float32), (P, 1))}


def lay_out(i):
    w_in = i["w_in"][0].reshape(KD, P, 7, HEADS, P)
    rq, rk, rv, rg, dq, dk, dv = (w_in[:, :, n] for n in range(7))

    def heads(*mats):
        return np.stack(mats, 3).transpose(2, 1, 0, 3, 4).reshape(HEADS, P, KD, len(mats) * P)

    def blocks(w, n):
        return w.reshape(KD, P, w.shape[1] // n, n).transpose(2, 1, 0, 3)
    a = {
        "x": np.concatenate([i["x_prompt"][0], i["x_sample"][0]], 0),
        "ct": np.concatenate([i["c_prompt"], i["c_sample"]], 0).reshape(GROUPS, KD, P).transpose(2, 1, 0).reshape(P, -1),
        "c_rows": np.concatenate([i["c_prompt"], i["c_sample"]], 0).reshape(GROUPS * KD, P),
        "ada_w": blocks(i["ada_w"][0][:, 0:2 * D], NB),
        "ada_wt": i["ada_w"][0][:, 2 * D:].T.reshape(HEADS, 8, P, 2, PIECE),
        "ada_b": i["ada_b"],
        "rows": np.concatenate([i["mix_pre_w"][0].reshape(KD, P), i["ret_gn_w"][0].reshape(HEADS, P), i["diff_subln_w"]], 0),
        "w_t": heads(rk, rq, dk, dq),
        "w_v": heads(rv, rg, dv),
        "w_o": blocks(i["w_out"][0], WOC),
        "w_q": blocks(i["peer_w_query"][0], 2 * P),
        "keys_t": i["peer_sub_keys"][0].transpose(3, 0, 1, 2).reshape(P, -1),
        "decay": np.stack([i["ret_decay_fwd"][0], i["ret_decay_bwd"][0]], 1).reshape(1, -1),
        "lams": np.concatenate([i["diff_lambda_q1"], i["diff_lambda_k1"], i["diff_lambda_q2"], i["diff_lambda_k2"]], 1),
        "post1": i["mix_post_w"], "pre2": i["ffn_pre_w"], "post2": i["ffn_post_w"],
        "u_t": i["peer_u"][0].reshape(NKEYS, NKEYS, KD, P).transpose(0, 3, 2, 1).reshape(NKEYS, P, -1),
        "u_tab": i["peer_u"][0], "v_tab": i["peer_v"][0],
    }
    return {**a, **constants()}


def kernel(**inputs):
    import concourse.bacc as bacc
    from concourse import mybir
    from concourse.bass_utils import run_bass_kernel_spmd

    nc = bacc.Bacc("TRN2", target_bir_lowering=False, num_devices=1)
    laid = lay_out({k: np.asarray(v) for k, v in inputs.items()})
    arrays, args = {}, []
    for name in _INS:
        a = np.ascontiguousarray(laid[name])
        arrays[f"in_{name}"] = a
        args.append(nc.dram_tensor(f"in_{name}", a.shape, mybir.dt.from_np(a.dtype), kind="ExternalInput").ap())
    out = nc.dram_tensor("out_0", (T, D), mybir.dt.float32, kind="ExternalOutput").ap()
    mod_d = nc.dram_tensor("mod_scratch", (GROUPS, MODS * D), mybir.dt.float32).ap()
    silu_d = nc.dram_tensor("silu_scratch", (GROUPS, D), mybir.dt.float32).ap()
    g_d = nc.dram_tensor("table_scratch", (NKEYS, P, ND), mybir.dt.float32).ap()
    w_d = nc.dram_tensor("weights_scratch", (NKEYS, P, ND), mybir.dt.float32).ap()
    build_program(nc, *args, out, mod_d, silu_d, g_d, w_d)
    got = run_bass_kernel_spmd(nc, [arrays], core_ids=[0]).results[0]["out_0"]
    return got[0:SEQ][None], got[SEQ:T][None]
```

```python
import math
import numpy as np

P = 128
D = 2048
KD = D // P
SEQ = 256
GROUPS = 2
TPG = SEQ // P
NT = GROUPS * TPG
T = NT * P
HEADS = 8
DQK = 64
MODS = 6
NB = 512
ADA_BLOCKS = 2 * D // NB
LATE = (MODS - 2) * KD
PIECE = D // 2
PIECES = 2 * LATE // 8
WT = KD * P
WV = KD // 4 * 3 * P
EPS = 1e-6
LAM_INIT = 0.8 - 0.6 * math.exp(-0.3 * 0)
PEER_HEADS = 8
NKEYS = 128
TOPK = 16
SLOTS = PEER_HEADS * TOPK
WOC = 256
RSQRT_MAGIC = 0x5F3759DF
LOWEST = -3.0e38
GATHERED = 1
DT = NT - GATHERED
ND = DT * P
RING = 4
HALF = D // 2
PAIRS = NKEYS // 2


def build_program(nc, x, ct, c_rows, ada_w, ada_wt, ada_b, rows, w_t, w_v, w_o, w_q, keys_t, decay, lams, post1, pre2, post2,
                  u_t, u_tab, v_tab, ident_c, dist_c, alibi_c, iota_c, out, mod_d, silu_d, mix_d, g_d, w_d):
    import concourse.bass as bass
    from concourse import mybir
    from contextlib import ExitStack

    f32, i32, u32, f32r = mybir.dt.float32, mybir.dt.int32, mybir.dt.uint32, mybir.dt.float32r
    ALU, ACT, AX = mybir.AluOpType, mybir.ActivationFunctionType, mybir.AxisListType.X
    ds = bass.ds

    with ExitStack() as ctx:
        def sbuf(name, shape, dtype=f32):
            return ctx.enter_context(nc.sbuf_tensor("sb_" + name, shape, dtype))

        def semaphore(name):
            return ctx.enter_context(nc.semaphore(name))

        base = (nc.sbuf_base + 31) // 32 * 32
        sizes = [NT * D, NT * D, NT * D, 14336]
        arena = sbuf("arena", [P, sum(sizes)])
        X0, H0, M0, W0 = (sum(sizes[:n]) for n in range(4))
        big_x, big_h, big_m, big_w = (arena[:, a:a + n] for a, n in zip((X0, H0, M0, W0), sizes))
        small = sbuf("small", [P, 11264])

        def placed(name, at, shape, dtype=f32):
            return nc.alloc_sbuf_tensor_at("sb_" + name, shape, dtype, offset=base + 4 * at)

        def rounded(name, at, shape):
            return placed(name, at, shape, f32r)
        ident = sbuf("ident", [P, P])
        cols = sbuf("cols", [P, 96])
        tiny = sbuf("tiny", [P, 512])

        x_sb = big_x[:, :].rearrange("p (t d) -> p t d", t=NT)
        h_hi = rounded("h_hi", H0, [P, KD, T])
        h_lo = rounded("h_lo", M0, [P, KD, T])
        w_raw = placed("w_raw", W0, [P, 2, WT])
        w_high = rounded("w_high", W0 + 2 * WT, [P, 2, WT])
        w_low = rounded("w_low", W0 + 4 * WT, [P, 2, WT])
        mix_out_sb = big_w[:, 6 * WT:6 * WT + 2 * T].rearrange("p (w t) -> p w t", w=2)
        o_sb = big_h[:, :].rearrange("p (t d) -> p t d", t=NT)
        mix_t = big_m[:, :].rearrange("p (k t) -> p k t", k=KD)

        def carver(arena):
            at = [0]

            def take(n):
                at[0] += n
                assert at[0] <= arena.shape[1], at[0]
                return arena[:, at[0] - n:at[0]]
            return take

        take = carver(small)
        k_t, q_t, dk_t, dq_t = (take(T) for _ in range(4))
        vd = take(NT * 2 * P).rearrange("p (t m c) -> p t m c", t=NT, m=2)
        e_g = take(NT * P).rearrange("p (t c) -> p t c", t=NT)
        gate = take(NT * P).rearrange("p (t c) -> p t c", t=NT)
        dist = take(2 * 384).rearrange("p (s u) -> p s u", s=2)
        decay_log = take(384)
        decay_tab = take(384)
        ret_p = take(GROUPS * 512).rearrange("p (g s t) -> p g s t", g=GROUPS, s=TPG)
        soft = take(4 * 512).rearrange("p (u m k) -> p u m k", u=4, m=2)
        attn = take(4 * SEQ).rearrange("p (u k) -> p u k", u=4)
        attn_t = take(4 * SEQ).rearrange("p (u s q) -> p u s q", u=4, s=TPG)
        alibi = take(2 * SEQ).rearrange("p (t k) -> p t k", t=TPG)
        take = carver(small)
        keys_sb = take(2 * PEER_HEADS * NKEYS)
        qt_sb = take(2 * T).rearrange("p (m t) -> p m t", m=2)
        masked = take(NT * 256).rearrange("p (t j) -> p t j", t=NT)
        cand = take(NT * 256).rearrange("p (t j) -> p t j", t=NT)
        onehot = take(NT * 256)
        slot_keys = take(2 * NT * SLOTS).rearrange("p (m t s) -> p m t s", m=2, t=NT)
        eidx = small[:, 8192:8704].bitcast(u32).rearrange("p (t s) -> p t s", t=NT)
        gates = small[:, 8704:9216].rearrange("p (t s) -> p t s", t=NT)
        mod_rows = small[0:GROUPS, 0:2 * NB].rearrange("g (r n) -> g r n", r=2)
        cols_in = small[:, 6 * NB + 256:6 * NB + 384]
        lam_in = small[:, 6 * NB:6 * NB + 4 * DQK].rearrange("p (v d) -> p v d", v=4)
        bias_rows = small[0:GROUPS, 3 * NB:5 * NB].rearrange("g (r n) -> g r n", r=2)
        ada_ring = [big_w[:, 0:8192], big_h]
        silu_r, silu_re = (small[0:GROUPS * KD, a:a + P] for a in (4096, 4096 + P))
        silu_b = big_x[:, 0:GROUPS * D].rearrange("p (g d) -> p g d", g=GROUPS)
        col_ring = big_x[:, GROUPS * D:GROUPS * D + 4 * PIECE].rearrange("p (r d) -> p r d", r=4)
        ada_ring = [a.rearrange("p (k n) -> p k n", k=KD) for a in ada_ring]
        mix_hi = rounded("mix_hi", X0, [P, KD, T])
        mix_lo = rounded("mix_lo", M0, [P, KD, T])
        post1_sb, pre2_sb = (small[:, i * D:(i + 1) * D] for i in (1, 2))
        coefs = [[big_w[:, i * D:(i + 1) * D] for i in (4, 5, 6)], [small[:, 3 * D:4 * D], small[:, 4 * D:5 * D], big_w[:, 0:D]]]
        wq_ring = [big_w[:, 4096:8192], big_w[:, 8192:12288]]
        wq_ring = [w.rearrange("p (k n) -> p k n", k=KD) for w in wq_ring]
        h2_t = placed("h2_t", M0, [P, KD, T])
        gather_ring = small[:, 0:RING * D].rearrange("p (r d) -> p r d", r=RING)
        by_slot = small[:, 0:3 * ND].rearrange("p (v n) -> p v n", v=3)
        hot = small[:, 2048:6144].rearrange("p (r v x k) -> p r v x k", r=4, v=2, x=4)
        table_sb = arena[:, H0 + D:H0 + D + NKEYS * P].rearrange("p (i n) -> p i n", i=NKEYS)
        at = H0 + D
        raw_ring = placed("raw_ring", at, [P, 2, D])
        at += 2 * D
        g_ring = arena[:, at:at + 2 * ND].rearrange("p (r n) -> p r n", r=2)
        gelu_sb = arena[:, at + 2 * ND:at + 4 * ND].rearrange("p (r n) -> p r n", r=2)
        w_ring = arena[:, at + 4 * ND:at + 6 * ND].rearrange("p (r n) -> p r n", r=2)
        at += 6 * ND
        raw_hi = rounded("raw_hi", at, [P, 2, D])
        raw_lo = rounded("raw_lo", at + 2 * D, [P, 2, D])
        at = W0 + D
        h2_hi = rounded("h2_hi", at, [P, KD, ND])
        h2_lo = rounded("h2_lo", at + KD * ND, [P, KD, ND])
        wraw_ring = placed("wraw_ring", at, [P, 2, 2, ND])
        w_hi = rounded("w_hi", at + 4 * ND, [P, 2, 2, ND])
        w_lo = rounded("w_lo", at + 8 * ND, [P, 2, 2, ND])
        y_dense = arena[:, at + 12 * ND:at + 12 * ND + DT * D].rearrange("p (t d) -> p t d", t=DT)
        acc = big_h[:, 0:D]
        post2_sb, out_sb, out2_sb = (small[:, i * D:(i + 1) * D] for i in range(3))
        gate2_sb = [small[:, i * D:(i + 1) * D] for i in (3, 4)]
        take = carver(tiny)
        ss_x = take(8)
        rstd_x = take(8)
        nt_a, nt_b, nt_y = take(8), take(8), take(8)
        silu_c = take(2 * KD)
        silu_e = take(2 * KD)
        lg_all = take(2 * HEADS)
        lg_t = [take(2 * HEADS) for _ in range(3)]
        lg_h = take(2)
        lam_dot = take(4)
        lam = take(2)
        bn6 = take(NT * 6).rearrange("p (t s) -> p t s", t=NT)
        mv = take(NT * 2).rearrange("p (t s) -> p t s", t=NT)
        nmax = take(4 * 2).rearrange("p (u m) -> p u m", u=4)
        esum = take(4 * 2).rearrange("p (u m) -> p u m", u=4)
        coef = take(4 * 2).rearrange("p (u m) -> p u m", u=4)
        iota = sbuf("iota", [P, NKEYS])
        iota16 = iota[:, 0:TOPK]
        stage = [take(RING).bitcast(u32) for _ in range(2)]
        hid = take(RING)
        ss_out = take(4)
        dif_ss = take(4)
        sub_w = take(1)
        hid_all = take(SLOTS)
        mod_cols = hid_all.rearrange("p (g c) -> p g c", g=GROUPS)
        mod_part = take(4 * 8).rearrange("p (s g c) -> p s g c", s=2, g=GROUPS)
        ret_out = sbuf("ret_out", [P, 8 * P])
        h_tmp = ret_out[:, :].rearrange("p (r t) -> p r t", r=2)
        take = carver(ret_out)
        ret_o = take(NT * P).rearrange("p (t c) -> p t c", t=NT)
        diff_o = take(NT * P).rearrange("p (t c) -> p t c", t=NT)
        tops = sbuf("tops", [P, PIECE])
        products = tops[:, :]
        mod_bias, mod_late = tops[:, 0:P], tops[:, P:2 * P]
        take = carver(tops)
        top_v = take(2 * NT * TOPK).rearrange("p (m t k) -> p m t k", m=2, t=NT)
        top_i = take(2 * NT * TOPK).bitcast(u32).rearrange("p (m t k) -> p m t k", m=2, t=NT)
        top_if = take(2 * NT * TOPK).rearrange("p (m t k) -> p m t k", m=2, t=NT)
        best_v = take(NT * TOPK).rearrange("p (t k) -> p t k", t=NT)
        best_p = take(NT * TOPK).bitcast(u32).rearrange("p (t k) -> p t k", t=NT)
        part_u = take(NT * TOPK).bitcast(u32)
        part_f = take(NT * TOPK)
        pick = take(2 * NT * TOPK).rearrange("p (m t k) -> p m t k", m=2, t=NT)
        soft_e = take(NT * TOPK)
        pair_id = take(NT * TOPK).rearrange("p (t k) -> p t k", t=NT)

        psum = ctx.enter_context(nc.psum_tensor("ps_all", [P, 8 * NB], f32))

        def bank(i):
            return psum[:, i * NB:(i + 1) * NB]

        names = """consts rows_in x_in cols_in sumsq silu_e silu colsT cols_ev a1_cols lg_e lam_e lg_rdy
            silu_rows silu_out silu_in col_in0 col_in1 col_in2 col_in3 col_a col_used late_cols late_t late_row late_out bias_in
            ada_in0 ada_in1 ada_mm ada_row mod_out0 mod_out1 xs xtr h_tmp h_high h_low
            w_in0 w_in1 w_high w_low mix_out mix_in alibi_in proj proj_ev gate
            dlog dtab ret_s ret_pd ret_v ret_n dif_s dif_sd dif_m dif_e dif_c dif_t dif_te dif_v dif_sq dif_n out_t out_te
            mix_hi mix_lo wo_half wo_mm wo_act wo_dve coef_in gate1_in shift2_in coef o_sq x1 x1_sq h2 grp_done h2tr h2tr_ev
            wq_in0 wq_in1 key_in q_mm q_ev sc_mm sc_dve gl_in gl_exp eidx_rdy
            h2_hi h2_lo g_fin bs_t bs_ev g_ones g_hot g_mm g_ev g_out g_quarter0 g_quarter1 g_quarter2 g_quarter3 ru_in0 ru_in1 rg_in0 rg_in1 raw_hi raw_lo up_mm gelu w_rdy w_out0 w_out1
            h2_ps stage gr_in0 gr_in1 gr_in2 gr_in3 gr_used hid_rdy hid_gelu slot_w
            rv_in0 rv_in1 rw_in0 rw_in1 whi wlo down_mm down_ev acc_sq y y_out0 y_out1 fin_in
            dve act spare""".split()
        S = {n: semaphore("s_" + n) for n in names}

        block = ctx.enter_context(nc.Block())

        def wait(eng, name, value):
            if not isinstance(value, int) or value > 0:
                eng.wait_ge(S[name], value)

        def wait_alone(eng, name, value):
            wait(eng, name, value)
            eng.sem_inc(S["spare"], 1)

        PRE1, GN, SUB = 4 * KD, 5 * KD, 5 * KD + HEADS
        MOD_ROWS = 2 * 2 * KD

        def groups_of(unit):
            return unit // TPG, unit % TPG

        @block.sync
        def _(sp):
            sp.dma_start(silu_c, ct).then_inc(S["consts"], 16)
            sp.dma_start(silu_r, c_rows).then_inc(S["consts"], 16)
            sp.dma_start(ident[:, :], ident_c).then_inc(S["consts"], 16)
            sp.dma_start(iota[:, :], iota_c).then_inc(S["consts"], 16)
            sp.dma_start(lg_all, decay.partition_broadcast(P)).then_inc(S["rows_in"], 16)
            sp.dma_start(lam_in, lams.partition_broadcast(P)).then_inc(S["rows_in"], 16)
            sp.dma_start(cols_in[MOD_ROWS:MOD_ROWS + KD + HEADS + 1, :], rows).then_inc(S["cols_in"], 16)

            def ada_load(n, r):
                sp.dma_start(ada_ring[r], ada_w[ds(n, 1)].rearrange("a p k n -> p (a k) n")).then_inc(S[f"ada_in{r}"], 16)
                sp.dma_start(bias_rows[:, r, :], ada_b[:, ds(n * NB, NB)].partition_broadcast(GROUPS)).then_inc(S[f"ada_in{r}"], 16)

            def mod_store(n, r):
                sp.wait_ge(S["ada_row"], n + 1)
                sp.dma_start(mod_d[:, ds(n * NB, NB)], mod_rows[:, r, :]).then_inc(S[f"mod_out{r}"], 16)

            for r in range(2):
                ada_load(r, r)
            for t in range(NT):
                sp.dma_start(x_sb[:, t, :], x[t * P:(t + 1) * P, :]).then_inc(S["x_in"], 16)
            sp.wait_ge(S["silu_rows"], 1)
            sp.dma_start(silu_d.rearrange("g (k p) -> (g k) p", p=P), silu_r).then_inc(S["silu_out"], 16)
            with sp.Fori(0, ADA_BLOCKS // 2 - 1) as i:
                for r in range(2):
                    mod_store(i * 2 + r, r)
                    ada_load(i * 2 + r + 2, r)
            for r in range(2):
                mod_store(ADA_BLOCKS - 2 + r, r)
            for r in range(2):
                sp.wait_ge(S[f"mod_out{r}"], 16 * (ADA_BLOCKS // 2))
            sp.wait_ge(S["silu_out"], 16)
            for g in range(GROUPS):
                sp.dma_start(cols_in[g * 2 * KD:(g + 1) * 2 * KD, :],
                             mod_d[g, 0:2 * D].rearrange("(r c) -> r c", c=P)).then_inc(S["cols_in"], 16)

            def piece_load(h, n):
                wait(sp, "w_low", 8 * h + n - 1)
                if n < 4:
                    sp.dma_start(w_raw[:, n % 2, :], w_t[ds(h, 1), n].rearrange("a p k c -> p (a k c)")).then_inc(S[f"w_in{n % 2}"], 16)
                else:
                    sp.dma_start(w_raw[:, n % 2, 0:WV], w_v[ds(h, 1), n - 4].rearrange("a p k c -> p (a k c)"))\
                        .then_inc(S[f"w_in{n % 2}"], 16)

            def col_load(h, n):
                if not (isinstance(h, int) and h == 0 and n < 4):
                    wait(sp, "col_used", h * PIECES + n - 3)
                sp.dma_start(col_ring[:, n % 4, :], ada_wt[ds(h, 1), n // 2, :, n % 2, :].rearrange("a p k -> p (a k)"))\
                    .then_inc(S[f"col_in{n % 4}"], 16)

            def mix_store(a):
                sp.wait_ge(S["out_te"], 2 * a + 2)
                for w in range(2):
                    sp.dma_start(mix_d[w, ds(a, 1)].rearrange("a p t -> p (a t)"), mix_out_sb[:, w, :]).then_inc(S["mix_out"], 16)

            def head_loads(h, first=False, second=False, last=False):
                for n in range(8):
                    if n == 0 and not first:
                        wait(sp, "dif_sd", 4 * (h - 1))
                        sp.dma_start(alibi, alibi_c[ds(h - 1, 1)].rearrange("a p t k -> p (a t) k")).then_inc(S["alibi_in"], 16)
                    if n < 6:
                        piece_load(h, n + 2)
                    elif not last:
                        piece_load(h + 1, n - 6)
                    if n == 1 and not first and not second:
                        mix_store(h - 2)
                    for c in range(2):
                        col_load(h, 2 * n + c)

            for n in range(2):
                piece_load(0, n)
            sp.wait_ge(S["cols_ev"], 1)
            sp.wait_ge(S["lg_rdy"], 1)
            sp.dma_start(dist, dist_c).then_inc(S["rows_in"], 16)
            sp.wait_ge(S["xtr"], KD)
            for g in range(GROUPS):
                sp.dma_start(silu_b[:, g, :], silu_d[g:g + 1, :].partition_broadcast(P)).then_inc(S["silu_in"], 16)
            sp.wait_ge(S["silu_in"], 32)
            head_loads(0, first=True)
            head_loads(1, second=True)
            with sp.Fori(2, HEADS - 1) as h:
                head_loads(h)
            head_loads(HEADS - 1, last=True)
            sp.wait_ge(S["dif_sd"], 4 * (HEADS - 1))
            sp.dma_start(alibi, alibi_c[HEADS - 1]).then_inc(S["alibi_in"], 16)
            mix_store(HEADS - 2)

            def wo_load(b, half):
                wait(sp, "w_low", 8 * HEADS + 2 * b + half - 1)
                sp.dma_start(w_raw[:, half, :], w_o[ds(b, 1), half].rearrange("a p k n -> p (a k n)")).then_inc(S[f"w_in{half}"], 16)

            for half in range(2):
                wo_load(0, half)
            sp.wait_ge(S["proj"], 8 * HEADS)

            def coef_load(g, n):
                v = (2, 4, 3)[n]
                return sp.dma_start(coefs[g][n], mod_d[g:g + 1, v * D:(v + 1) * D].partition_broadcast(P))

            def mix_load(heads):
                sp.wait_ge(S["mix_out"], 32 * heads.stop)
                for w in range(2):
                    sp.dma_start(mix_t[:, w * HEADS + heads.start:w * HEADS + heads.stop, :], mix_d[w, heads].rearrange("a p t -> p a t"))\
                        .then_inc(S["mix_in"], 16)

            mix_load(slice(0, HEADS - 1))

            sp.wait_ge(S["col_used"], HEADS * PIECES)
            for g in range(GROUPS):
                sp.dma_start(mod_bias[g * LATE:(g + 1) * LATE, :], ada_b[0, 2 * D:MODS * D].rearrange("(c p) -> c p", p=P))\
                    .then_inc(S["bias_in"], 16)
            mix_store(HEADS - 1)
            mix_load(slice(HEADS - 1, HEADS))
            sp.wait_ge(S["late_row"], 1)
            for g in range(GROUPS):
                sp.dma_start(mod_d[g, 2 * D:MODS * D].rearrange("(c p) -> c p", p=P), mod_late[g * LATE:(g + 1) * LATE, :])\
                    .then_inc(S["late_out"], 16)
            sp.wait_ge(S["late_out"], 32)
            sp.wait_ge(S["out_te"], 2 * HEADS)
            sp.dma_start(post1_sb, post1.partition_broadcast(P)).then_inc(S["coef_in"], 16)
            sp.dma_start(pre2_sb, pre2.partition_broadcast(P)).then_inc(S["coef_in"], 16)
            for g, n in ((1, 0), (1, 1), (0, 2)):
                coef_load(g, n).then_inc(S["coef_in"], 16)
            with sp.Fori(1, D // WOC) as b:
                for half in range(2):
                    wo_load(b, half)
            sp.wait_ge(S["wo_mm"], D // WOC * NT)
            for n in range(2):
                coef_load(0, n).then_inc(S["gate1_in"], 16)
            for t in range(NT):
                sp.dma_start(x_sb[:, t, :], x[t * P:(t + 1) * P, :]).then_inc(S["x_in"], 16)
            coef_load(1, 2).then_inc(S["shift2_in"], 16)
            sp.dma_start(wq_ring[0], w_q[0]).then_inc(S["wq_in0"], 16)
            sp.dma_start(keys_sb, keys_t).then_inc(S["key_in"], 16)
            sp.wait_ge(S["grp_done"], 1)
            sp.dma_start(wq_ring[1], w_q[1]).then_inc(S["wq_in1"], 16)
            with sp.Fori(1, PEER_HEADS // 2) as i:
                for r in range(2):
                    sp.wait_ge(S["q_mm"], 2 * (i * 2 + r - 1))
                    sp.dma_start(wq_ring[r], w_q[ds(i * 2 + r, 1)].rearrange("a p k n -> p (a k) n")).then_inc(S[f"wq_in{r}"], 16)

            for t in range(DT):
                sp.wait_ge(S["g_ev"], 32 * (t + 1) + 4)
                stored = g_d[:, :, t * P:(t + 1) * P].rearrange("i j n -> j i n")
                if t < DT - 1:
                    sp.dma_start(stored, table_sb).then_inc(S["g_out"], 16)
                    continue
                for q in range(4):
                    i = slice(q * NKEYS // 4, (q + 1) * NKEYS // 4)
                    sp.dma_start(stored[:, i, :], table_sb[:, i, :]).then_inc(S[f"g_quarter{q}"], 16)
            sp.wait_ge(S["g_out"], 16 * (DT - 1) + 1)

            def u_load(n, r):
                wait(sp, "raw_lo", n - 1)
                sp.dma_start(raw_ring[:, r, :], u_t[ds(n, 1)].rearrange("a p d -> p (a d)")).then_inc(S[f"ru_in{r}"], 16)

            def g_load(n, r):
                wait(sp, "w_rdy", n + 1)
                sp.dma_start(g_ring[:, r, :], g_d[ds(n, 1)].rearrange("a p n -> p (a n)")).then_inc(S[f"rg_in{r}"], 16)

            def up_store(n, r):
                sp.wait_ge(S["w_rdy"], n + 3)
                sp.dma_start(w_d[ds(n, 1)].rearrange("a p n -> p (a n)"), w_ring[:, r, :]).then_inc(S[f"w_out{r}"], 16)

            sp.wait_ge(S["g_quarter0"], 16)
            for r in range(2):
                u_load(r, r)
            for q in range(1, 4):
                sp.wait_ge(S[f"g_quarter{q}"], 16)
            for r in range(2):
                g_load(r, r)
                u_load(r + 2, r)
            with sp.Fori(1, NKEYS // 2 - 1) as i:
                for r in range(2):
                    u_load(2 * i + r + 2, r)
                    g_load(2 * i + r, r)
                    up_store(2 * i + r - 2, r)
            for r in range(2):
                g_load(NKEYS - 2 + r, r)
                up_store(NKEYS - 4 + r, r)
            for r in range(2):
                up_store(NKEYS - 2 + r, r)
            for r in range(2):
                sp.wait_ge(S[f"w_out{r}"], 16 * NKEYS // 2)

            def down_loads(half, m, r, n):
                wait(sp, "raw_lo", NKEYS + n - 1)
                v = v_tab[ds(m * 2 * P, 2 * P), ds(half * HALF, HALF)].rearrange("(e p) d -> p e d", e=2)
                sp.dma_start(raw_ring[:, r, :].rearrange("p (e d) -> p e d", e=2), v).then_inc(S[f"rv_in{r}"], 16)
                wait(sp, "wlo", n - 1)
                sp.dma_start(wraw_ring[:, r, :, :], w_d[ds(2 * m, 2)].rearrange("e p n -> p e n")).then_inc(S[f"rw_in{r}"], 16)

            sp.wait_ge(S["up_mm"], NKEYS)
            for r in range(2):
                down_loads(0, r, r, r)
            with sp.Fori(1, PAIRS // 2) as i:
                for r in range(2):
                    down_loads(0, 2 * i + r, r, 2 * i + r)
            with sp.Fori(0, PAIRS // 2) as i:
                for r in range(2):
                    down_loads(1, 2 * i + r, r, PAIRS + 2 * i + r)

            sp.wait_ge(S["gr_used"], 2 * SLOTS + RING)
            sp.dma_start(post2_sb, post2.partition_broadcast(P)).then_inc(S["fin_in"], 16)
            for g in range(GROUPS):
                sp.dma_start(gate2_sb[g], mod_d[g:g + 1, 5 * D:6 * D].partition_broadcast(P)).then_inc(S["fin_in"], 16)
            for t in range(NT):
                sp.wait_ge(S["y"], t + 1)
                sp.dma_start(out[t * P:(t + 1) * P, :], out2_sb if t % 2 else out_sb).then_inc(S[f"y_out{t % 2}"], 16)
            for r in range(2):
                sp.wait_ge(S[f"y_out{r}"], 16 * NT // 2)

        @block.tensor
        def _(pe):
            mm = nc.tensor.matmul

            def ada_block(i, r):
                n = i * 2 + r
                wait(pe, f"ada_in{r}", 32 * (i + 1))
                wait(pe, "ada_row", n - 1)
                for k in range(KD):
                    last = mm(bank(r)[0:GROUPS, :], silu_c[:, k * GROUPS:(k + 1) * GROUPS], ada_ring[r][:, k, :],
                              start=k == 0, stop=k == KD - 1)
                last.then_inc(S["ada_mm"], 1)

            pe.wait_ge(S["silu"], 1)
            for r in range(2):
                ada_block(0, r)
            with pe.Fori(1, ADA_BLOCKS // 2) as i:
                for r in range(2):
                    ada_block(i, r)

            pe.wait_ge(S["consts"], 64)
            pe.wait_ge(S["cols_in"], 48)
            n_rows = MOD_ROWS + KD + HEADS + 1
            nc.tensor.transpose(bank(3)[:, 0:n_rows], cols_in[0:n_rows, :], ident[0:n_rows, 0:n_rows]).then_inc(S["colsT"], 1)

            pe.wait_ge(S["xs"], NT)
            for k in range(KD):
                wait(pe, "h_tmp", k - 3)
                for t in range(NT):
                    last = nc.tensor.transpose(bank(4 + k % 4)[:, t * P:(t + 1) * P],
                                               x_sb[:, t, k * P:(k + 1) * P], ident[:, :])
                last.then_inc(S["xtr"], 1)

            def split_products(b, parts, start, stop):
                (a_hi, a_lo), (b_hi, b_lo) = parts
                mm(b, a_hi, b_hi, start=start, stop=False)
                mm(b, a_hi, b_lo, start=False, stop=False)
                return mm(b, a_lo, b_hi, start=False, stop=stop)

            def project(h, n):
                wait(pe, "w_low", 8 * h + n + 1)
                r = n % 2
                if n < 4:
                    wait(pe, "gate", 4 * (h - 1) + n + 1)
                    for k in range(KD):
                        c = slice(k * P, (k + 1) * P)
                        last = split_products(bank(n), ((w_high[:, r, c], w_low[:, r, c]), (h_hi[:, k, :], h_lo[:, k, :])),
                                              k == 0, k == KD - 1)
                else:
                    for t in range(NT):
                        if n == 4:
                            wait(pe, "proj_ev", 8 * h + t + 1)
                        for kk in range(KD // 4):
                            k = (n - 4) * KD // 4 + kk
                            c, toks = slice(kk * 3 * P, (kk + 1) * 3 * P), slice(t * P, (t + 1) * P)
                            last = split_products(bank(t)[:, 0:3 * P], ((h_hi[:, k, toks], h_lo[:, k, toks]),
                                                                        (w_high[:, r, c], w_low[:, r, c])), k == 0, k == KD - 1)
                last.then_inc(S["proj"], 1)

            def ret_scores(a, g):
                wait(pe, "proj_ev", 8 * a + 2)
                wait(pe, "out_te", 2 * (a - 1) + g + 1)
                for s in range(TPG):
                    last = mm(bank(4 + g)[:, s * SEQ:(s + 1) * SEQ], k_t[:, (g * TPG + s) * P:(g * TPG + s + 1) * P],
                              q_t[:, g * SEQ:(g + 1) * SEQ], start=True, stop=True)
                last.then_inc(S["ret_s"], 1)

            def dif_scores(a, u):
                g, m = groups_of(u)
                wait(pe, "proj_ev", 8 * a + 4)
                if u < 2:
                    wait(pe, "dif_n", 4 * (a - 1) + u + 3)
                else:
                    wait(pe, "ret_pd", 2 * a + u - 1)
                b = bank(6 + u if u < 2 else 2 + u)
                for t in range(g * TPG, (g + 1) * TPG):
                    last = mm(b[:, t % TPG * SEQ:(t % TPG + 1) * SEQ], dq_t[m * DQK:(m + 1) * DQK, t * P:(t + 1) * P],
                              dk_t[m * DQK:(m + 1) * DQK, g * SEQ:(g + 1) * SEQ], start=True, stop=True)
                last.then_inc(S["dif_s"], 1)

            def ret_values(a, g):
                wait(pe, "dif_sd", 4 * a + g + 1)
                wait(pe, "ret_pd", 2 * a + g + 1)
                wait(pe, "proj_ev", 8 * a + 6 + 2 * g)
                for tt in range(TPG):
                    for s in range(TPG):
                        last = mm(bank(6 + g)[:, tt * P:(tt + 1) * P], ret_p[:, g, s, tt * P:(tt + 1) * P],
                                  vd[:, g * TPG + s, 0, :], start=s == 0, stop=s == TPG - 1)
                last.then_inc(S["ret_v"], 1)

            def dif_transposes(a, u):
                wait(pe, "dif_c", 4 * a + u + 1)
                if u < 2:
                    wait(pe, "dif_sd", 4 * a + u + 3)
                else:
                    wait(pe, "dif_te", 4 * a + u - 1)
                for s in range(TPG):
                    last = nc.tensor.transpose(bank(4 + u % 2)[:, s * P:(s + 1) * P], attn[:, u, s * P:(s + 1) * P], ident[:, :])
                last.then_inc(S["dif_t"], 1)

            def dif_values(a, u):
                g, qt = groups_of(u)
                wait(pe, "dif_te", 4 * a + u + 1)
                if u < 2:
                    wait(pe, "ret_n", 2 * a + u + 1)
                else:
                    wait(pe, "dif_n", 4 * a + u - 1)
                for s in range(TPG):
                    last = mm(bank(6 + u % 2)[:, 0:P], attn_t[:, u, s, :], vd[:, g * TPG + s, 1, :],
                              start=s == 0, stop=s == TPG - 1)
                last.then_inc(S["dif_v"], 1)

            def out_transposes(a, w):
                wait(pe, "dif_te", 4 * a + 3 + w)
                if w == 0:
                    wait(pe, "ret_n", 2 * a + 2)
                else:
                    wait(pe, "dif_n", 4 * a + 4)
                src = diff_o if w else ret_o
                for t in range(NT):
                    last = nc.tensor.transpose(bank(4 + w)[:, t * P:(t + 1) * P], src[:, t, :], ident[:, :])
                last.then_inc(S["out_t"], 1)

            def head_step(h, a):
                def p(n):
                    if h is not None:
                        project(h, n)

                def step(f, *units):
                    if a is not None:
                        for u in units:
                            f(a, u)
                p(0)
                step(ret_scores, 0, 1)
                step(dif_scores, 0, 1)
                p(1)
                step(dif_scores, 2, 3)
                p(2)
                step(ret_values, 0, 1)
                p(3)
                step(dif_transposes, 0, 1)
                p(4)
                step(dif_values, 0, 1)
                step(dif_transposes, 2, 3)
                p(5)
                step(dif_values, 2, 3)
                p(6)
                p(7)
                step(out_transposes, 0, 1)

            pe.wait_ge(S["h_low"], KD)
            head_step(0, None)
            head_step(1, 0)
            with pe.Fori(2, HEADS) as h:
                head_step(h, h - 1)
            head_step(None, HEADS - 1)

            def wo_block(b, r):
                for half in range(2):
                    wait(pe, "w_low", 8 * HEADS + 2 * b + half + 1)
                    for t in range(NT):
                        for kk in range(KD // 2):
                            k, c, toks = half * KD // 2 + kk, slice(kk * WOC, (kk + 1) * WOC), slice(t * P, (t + 1) * P)
                            last = split_products(bank(4 * r + t)[:, 0:WOC], ((mix_hi[:, k, toks], mix_lo[:, k, toks]),
                                                                              (w_high[:, half, c], w_low[:, half, c])),
                                                  k == 0, k == KD - 1)
                        if half:
                            last.then_inc(S["wo_mm"], 1)
                    if not half:
                        last.then_inc(S["wo_half"], 1)

            pe.wait_ge(S["out_te"], 2 * HEADS)
            pe.wait_ge(S["late_cols"], 1)
            nc.tensor.transpose(bank(7)[:, 0:P], hid_all, ident[:, :]).then_inc(S["late_t"], 1)
            pe.wait_ge(S["mix_lo"], 4)
            wo_block(0, 0)
            pe.wait_ge(S["late_row"], 1)
            wo_block(1, 1)
            with pe.Fori(1, D // WOC // 2) as i:
                for r in range(2):
                    wait(pe, "wo_dve" if r else "wo_act", NT * i)
                    wo_block(2 * i + r, r)

            pe.wait_ge(S["wo_act"], NT * D // WOC // 2)
            for t in range(NT):
                pe.wait_ge(S["h2"], t + 1)
                for kk in range(4):
                    wait(pe, "h2tr_ev", 4 * (t - 1) + kk + 1)
                    for j in range(4):
                        k = 4 * kk + j
                        last = nc.tensor.transpose(bank(kk)[:, j * P:(j + 1) * P], o_sb[:, t, k * P:(k + 1) * P], ident[:, :])
                    last.then_inc(S["h2tr"], 1)

            def route_head(i, r):
                hd = i * 2 + r
                wait(pe, f"wq_in{r}", 16 * (i + 1))
                for m in range(2):
                    wait(pe, "q_ev", 2 * (hd - 1) + m + 1)
                    for k in range(KD):
                        last = mm(bank(m), wq_ring[r][:, k, m * P:(m + 1) * P], h2_t[:, k, :], start=k == 0, stop=k == KD - 1)
                    last.then_inc(S["q_mm"], 1)
                for m in range(2):
                    wait(pe, "q_ev", 2 * hd + m + 1)
                    wait(pe, "sc_dve", 2 * (hd - 2) + m + 1)
                    for t in range(NT):
                        last = mm(bank(2 + m + 4 * r)[:, t * P:(t + 1) * P], qt_sb[:, m, t * P:(t + 1) * P],
                                  keys_sb[:, ds((2 * hd + m) * NKEYS, NKEYS)], start=True, stop=True)
                    last.then_inc(S["sc_mm"], 1)

            pe.wait_ge(S["h2tr_ev"], 4 * NT)
            pe.wait_ge(S["key_in"], 16)
            for r in range(2):
                route_head(0, r)
            with pe.Fori(1, PEER_HEADS // 2) as i:
                for r in range(2):
                    route_head(i, r)

            pe.wait_ge(S["g_fin"], 1)
            for v, src in enumerate((slot_keys[:, 0], slot_keys[:, 1], gates)):
                for t in range(DT):
                    last = nc.tensor.transpose(bank(4 + v)[:, t * P:(t + 1) * P], src[:, GATHERED + t, :], ident[:, :])
            last.then_inc(S["bs_t"], 1)
            pe.wait_ge(S["bs_ev"], 1)
            with pe.Fori(0, DT * P // 16) as i:
                for s in range(4):
                    n = i * 4 + s
                    wait(pe, "g_hot", n + 1)
                    wait(pe, "g_ev", n + 1)
                    for x in range(4):
                        last = mm(bank(4 + s)[:, x * P:(x + 1) * P], hot[:, s, 1, x, :], hot[:, s, 0, x, :],
                                  start=True, stop=True)
                    last.then_inc(S["g_mm"], 1)

            pe.wait_ge(S["h2_lo"], 1)
            with pe.Fori(0, NKEYS // 2) as i:
                for r in range(2):
                    n = 2 * i + r
                    wait(pe, "raw_lo", n + 1)
                    wait(pe, "gelu", n + 1)
                    for k in range(KD):
                        e = slice(k * P, (k + 1) * P)
                        last = split_products(bank(4 + r)[:, 0:ND], ((raw_hi[:, r, e], raw_lo[:, r, e]), (h2_hi[:, k, :], h2_lo[:, k, :])),
                                              k == 0, k == KD - 1)
                    last.then_inc(S["up_mm"], 1)

            def down_pair(n, r, first, final):
                wait(pe, "raw_lo", NKEYS + n + 1)
                wait(pe, "wlo", n + 1)
                for e in range(2):
                    start, stop = first and e == 0, final and e == 1
                    for t in range(DT):
                        toks = slice(t * P, (t + 1) * P)
                        hi, lo = w_hi[:, r, e, toks], w_lo[:, r, e, toks]
                        for w, vs in ((hi, raw_hi), (hi, raw_lo), (lo, raw_hi)):
                            for b in range(2):
                                cols_ = slice(e * HALF + b * NB, e * HALF + (b + 1) * NB)
                                last = mm(bank(2 * t + b), w, vs[:, r, cols_], start=start and w is hi and vs is raw_hi,
                                          stop=stop and w is lo)
                last.then_inc(S["down_mm"], 1)

            for half in range(2):
                if half:
                    pe.wait_ge(S["down_ev"], 2 * DT)
                for r in range(2):
                    down_pair(half * PAIRS + r, r, r == 0, False)
                with pe.Fori(1, PAIRS // 2 - 1) as i:
                    for r in range(2):
                        down_pair(half * PAIRS + 2 * i + r, r, False, False)
                for r in range(2):
                    down_pair((half + 1) * PAIRS - 2 + r, r, False, r == 1)

        @block.scalar
        def _(act):
            acti = nc.scalar.activation
            act.wait_ge(S["consts"], 16 * 4)
            acti(silu_e, silu_c, ACT.Exp, scale=-1.0).then_inc(S["silu_e"], 1)
            acti(silu_re, silu_r, ACT.Exp, scale=-1.0).then_inc(S["silu_e"], 1)
            act.wait_ge(S["lg_e"], 1)
            acti(lg_t[0], lg_t[0], ACT.Exp, scale=-1.0).then_inc(S["lg_e"], 1)
            act.wait_ge(S["lam_e"], 1)
            acti(lam_dot[:, 0:2], lam_dot[:, 0:2], ACT.Exp).then_inc(S["lam_e"], 1)
            for t in range(NT):
                act.wait_ge(S["x_in"], 16 * NT)
                wait(act, "sumsq", t)
                acti(psum[:, 4 * NB:8 * NB], x_sb[:, t, :], ACT.Square, accum_out=ss_x[:, t:t + 1]).then_inc(S["sumsq"], 1)
            act.wait_ge(S["colsT"], 1)
            acti(cols[:, 0:SUB + 1], bank(3)[:, 0:SUB + 1], ACT.Copy).then_inc(S["cols_ev"], 1)
            act.wait_ge(S["a1_cols"], 1)
            for k in range(KD):
                act.wait_ge(S["h_tmp"], k + 1)
                acti(h_hi[:, k, :], h_tmp[:, k % 2, :], ACT.Copy).then_inc(S["h_high"], 1)

            def split_high(h, n):
                wait(act, f"w_in{n % 2}", 16 * (4 * h + n // 2 + 1))
                wait(act, "proj", 8 * h + n - 1)
                w = WT if n < 4 else WV
                acti(w_high[:, n % 2, 0:w], w_raw[:, n % 2, 0:w], ACT.Copy).then_inc(S["w_high"], 1)

            def decay_exp(a):
                act.wait_ge(S["dlog"], a + 1)
                wait(act, "ret_pd", 2 * a)
                acti(decay_tab, decay_log, ACT.Exp).then_inc(S["dtab"], 1)

            def evacuate(h, n):
                wait(act, "proj", 8 * h + min(n + 1, 4) if n < 4 else 8 * h + 8)
                if n < 4:
                    wait(act, "ret_s" if n < 2 else "dif_s", 2 * h if n < 2 else 4 * h)
                    dst = (k_t, q_t, dk_t, dq_t)[n]
                    acti(dst, bank(n), ACT.Copy, scale=P ** -0.5 if n == 0 else 1.0).then_inc(S["proj_ev"], 1)
                else:
                    t = n - 4
                    g = t // TPG
                    wait(act, "ret_v", 2 * (h - 1) + g + 1)
                    wait(act, "dif_v", 4 * (h - 1) + 2 * g + 2)
                    wait(act, "gate", 4 * (h - 1) + t + 1)
                    v = bank(t)[:, 0:3 * P].rearrange("p (m c) -> p m c", m=3)
                    acti(vd[:, t, :, :], v[:, 0:3:2, :], ACT.Copy)
                    acti(e_g[:, t, :], v[:, 1, :], ACT.Exp, scale=-1.0).then_inc(S["proj_ev"], 1)

            def soft_exp(a, u):
                wait(act, "dif_m", 4 * a + u // TPG * TPG + 2)
                for m in range(2):
                    last = acti(soft[:, u, m, :], soft[:, u, m, :], ACT.Exp, scale=DQK ** -0.5, bias=nmax[:, u, m:m + 1],
                                accum_out=esum[:, u, m:m + 1])
                last.then_inc(S["dif_e"], 1)

            def attn_evacuate(a, u):
                wait(act, "dif_t", 4 * a + u + 1)
                wait(act, "dif_v", 4 * (a - 1) + u + 1)
                acti(attn_t[:, u, :, :], bank(4 + u % 2)[:, 0:SEQ].rearrange("p (s q) -> p s q", s=TPG), ACT.Copy)\
                    .then_inc(S["dif_te"], 1)

            def dif_square(a, u):
                wait(act, "dif_v", 4 * a + u + 1)
                acti(soft[:, u, 0, 0:P], bank(6 + u % 2)[:, 0:P], ACT.Square, accum_out=dif_ss[:, u:u + 1])\
                    .then_inc(S["dif_sq"], 1)

            def out_evacuate(a, w):
                if not (isinstance(a, int) and a == 0):
                    wait_alone(act, "mix_out", 32 * a)
                wait_alone(act, "out_t", 2 * a + w + 1)
                scale = sub_w if w else cols[:, ds(GN + a, 1)]
                acti(mix_out_sb[:, w, :], bank(4 + w), ACT.Copy, scale=scale).then_inc(S["out_te"], 1)

            def head_step(h, a, last=False):
                def split(*ns):
                    if h is not None:
                        for n in ns:
                            if n < 8:
                                split_high(h, n)
                            elif not last:
                                split_high(h + 1, n - 8)

                def p(*ns):
                    if h is not None:
                        for n in ns:
                            evacuate(h, n)

                def step(f, *units):
                    if a is not None:
                        for u in units:
                            f(a, u)
                if a is not None:
                    decay_exp(a)
                split(2)
                p(0)
                step(soft_exp, 0, 1)
                split(3)
                p(1)
                step(soft_exp, 2, 3)
                split(4)
                p(2)
                split(5)
                p(3)
                step(attn_evacuate, 0, 1)
                split(6)
                step(dif_square, 0, 1)
                step(attn_evacuate, 2, 3)
                split(7)
                step(dif_square, 2, 3)
                split(8)
                p(4, 5, 6, 7)
                step(out_evacuate, 0, 1)
                split(9)

            for n in range(2):
                split_high(0, n)
            head_step(0, None)
            head_step(1, 0)
            with act.Fori(2, HEADS - 1) as h:
                head_step(h, h - 1)
            head_step(HEADS - 1, HEADS - 2, last=True)
            head_step(None, HEADS - 1)

            for n, heads in enumerate((slice(0, HEADS - 1), slice(HEADS - 1, HEADS))):
                act.wait_ge(S["mix_in"], 32 * (n + 1))
                act.wait_ge(S["late_t"], 1)
                for w in range(2):
                    ks = slice(w * HEADS + heads.start, w * HEADS + heads.stop)
                    acti(mix_hi[:, ks, :], mix_t[:, ks, :], ACT.Copy).then_inc(S["mix_hi"], 1)

            def wo_high(b, half):
                wait(act, f"w_in{half}", 16 * (4 * HEADS + b + 1))
                if not (isinstance(b, int) and b == 0):
                    wait(act, "wo_mm" if half else "wo_half", NT * b if half else b)
                acti(w_high[:, half, :], w_raw[:, half, :], ACT.Copy).then_inc(S["w_high"], 1)

            def wo_turn(i, last=False):
                wo_high(2 * i + 1, 0)
                for t in range(NT):
                    wait_alone(act, "wo_mm", (2 * i) * NT + t + 1)
                    acti(o_sb[:, t, ds(2 * i * WOC, WOC)], bank(t)[:, 0:WOC], ACT.Copy).then_inc(S["wo_act"], 1)
                wo_high(2 * i + 1, 1)
                if not last:
                    for half in range(2):
                        wo_high(2 * i + 2, half)

            act.wait_ge(S["proj"], 8 * HEADS)
            for half in range(2):
                wo_high(0, half)
            with act.Fori(0, D // WOC // 2 - 1) as i:
                wo_turn(i)
            wo_turn(D // WOC // 2 - 1, last=True)
            act.wait_ge(S["wo_dve"], NT * D // WOC // 2)
            act.wait_ge(S["wo_act"], NT * D // WOC // 2)
            junk = psum[:, 4 * NB:8 * NB]
            for t in range(NT):
                wait(act, "o_sq", t)
                acti(junk, o_sb[:, t, :], ACT.Square, accum_out=ss_x[:, t:t + 1]).then_inc(S["o_sq"], 1)

            def h2_evacuate(t):
                for kk in range(4):
                    act.wait_ge(S["h2tr"], 4 * t + kk + 1)
                    acti(h2_t[:, 4 * kk:4 * kk + 4, t * P:(t + 1) * P], bank(kk).rearrange("p (j c) -> p j c", j=4), ACT.Copy)\
                        .then_inc(S["h2tr_ev"], 1)

            act.wait_ge(S["o_sq"], NT)
            for t in range(NT):
                act.wait_ge(S["x1"], t + 1)
                wait(act, "x1_sq", t)
                acti(junk, x_sb[:, t, :], ACT.Square, accum_out=ss_x[:, 4 + t:5 + t]).then_inc(S["x1_sq"], 1)
                if t >= 1:
                    h2_evacuate(t - 1)
            h2_evacuate(NT - 1)

            def query_evacuate(i):
                for r in range(2):
                    for m in range(2):
                        hd = i * 2 + r
                        wait(act, "q_mm", 2 * hd + m + 1)
                        wait(act, "sc_mm", 2 * (hd - 1) + m + 1)
                        acti(qt_sb[:, m, :], bank(m), ACT.Copy).then_inc(S["q_ev"], 1)

            query_evacuate(0)
            with act.Fori(1, PEER_HEADS // 2) as i:
                query_evacuate(i)
            act.wait_ge(S["q_mm"], 2 * PEER_HEADS)
            acti(h2_hi[:, :, :], h2_t[:, :, GATHERED * P:T], ACT.Copy).then_inc(S["h2_hi"], 1)
            act.wait_ge(S["sc_dve"], 2 * PEER_HEADS)
            acti(psum[:, 0:D], o_sb[:, 0, :], ACT.Copy).then_inc(S["h2_ps"], 1)
            act.wait_ge(S["gl_in"], 1)
            acti(gates, gates, ACT.Exp).then_inc(S["gl_exp"], 1)

            act.wait_ge(S["bs_t"], 1)
            acti(by_slot, psum[:, 4 * NB:7 * NB].rearrange("p (v n) -> p v n", v=3)[:, :, 0:ND], ACT.Copy).then_inc(S["bs_ev"], 1)
            act.wait_ge(S["h2_lo"], 1)
            with act.Fori(0, DT) as t:
                with act.Fori(0, P // 16) as q:
                    for s in range(4):
                        n = t * 32 + q * 4 + s
                        if s == 0:
                            wait_alone(act, "g_out", 16 * t + 1)
                        wait_alone(act, "g_mm", n + 5)
                        acti(table_sb[:, :, ds(q * 16 + s * 4, 4)], bank(4 + s).rearrange("p (x i) -> p i x", x=4), ACT.Copy)\
                            .then_inc(S["g_ev"], 1)

            def high_part(n, r, sem, count):
                wait(act, f"{sem}_in{r}", count)
                return acti(raw_hi[:, r, :], raw_ring[:, r, :], ACT.Copy)

            def up_gelu(n, r):
                wait(act, "up_mm", n + 1)
                wait(act, "w_rdy", n + 1)
                acti(gelu_sb[:, r, :], bank(4 + r)[:, 0:ND], ACT.Gelu).then_inc(S["gelu"], 1)

            act.wait_ge(S["g_quarter1"], 16)
            for r in range(2):
                high_part(r, r, "ru", 16).then_inc(S["raw_hi"], 1)
            act.wait_ge(S["g_quarter3"], 16)
            with act.Fori(1, NKEYS // 2) as i:
                for r in range(2):
                    n = 2 * i + r
                    wait(act, "up_mm", n - 1)
                    high_part(n, r, "ru", 16 * (i + 1)).then_inc(S["raw_hi"], 1)
                    up_gelu(n - 2, r)
            for r in range(2):
                up_gelu(NKEYS - 2 + r, r)
            act.wait_ge(S["hid_rdy"], SLOTS // RING + 1)
            acti(hid_all, hid_all, ACT.Gelu).then_inc(S["hid_gelu"], 1)

            def down_parts(n, r, uses):
                wait(act, "down_mm", n - 1)
                high_part(n, r, "rv", 16 * (uses + 1)).then_inc(S["raw_hi"], 1)
                wait(act, f"rw_in{r}", 16 * (uses + 1))
                acti(w_hi[:, r, :, :], wraw_ring[:, r, :, :], ACT.Copy).then_inc(S["whi"], 1)

            def down_evacuate(half):
                act.wait_ge(S["down_mm"], (half + 1) * PAIRS)
                for t in range(DT):
                    last = acti(y_dense[:, t, half * HALF:(half + 1) * HALF], psum[:, 2 * t * NB:2 * (t + 1) * NB], ACT.Copy)
                    last.then_inc(S["down_ev"], 2)

            for r in range(2):
                down_parts(r, r, 0)
            with act.Fori(1, PAIRS // 2) as i:
                for r in range(2):
                    down_parts(2 * i + r, r, i)
            for r in range(2):
                down_parts(PAIRS + r, r, PAIRS // 2)
            down_evacuate(0)
            with act.Fori(1, PAIRS // 2) as i:
                for r in range(2):
                    down_parts(PAIRS + 2 * i + r, r, PAIRS // 2 + i)
            down_evacuate(1)
            act.wait_ge(S["down_ev"], 4 * DT)
            act.wait_ge(S["gr_used"], 2 * SLOTS + RING)
            for t in range(NT):
                wait(act, "acc_sq", t)
                acti(junk, acc if t == 0 else y_dense[:, t - 1, :], ACT.Square, accum_out=ss_out[:, t:t + 1]).then_inc(S["acc_sq"], 1)

        @block.vector
        def _(dve):
            vec = nc.vector
            chain = [0]

            def link(ins):
                chain[0] += 1
                ins.then_inc(S["dve"], 1)
                dve.wait_ge(S["dve"], chain[0])

            class Chain:
                def __init__(self, before, turn, per_turn):
                    self.base, self.n, self.per_turn = turn * per_turn + before, 0, per_turn

                def __call__(self, ins, alone=False):
                    self.n += 1
                    ins.then_inc(S["dve"], 1)
                    (wait_alone if alone else wait)(dve, "dve", self.base + self.n)

                def done(self):
                    assert self.n == self.per_turn, self.n

            def rsqrt(link, out_, v, y, a):
                link(vec.tensor_scalar(a.bitcast(i32), v.bitcast(i32), 1, None, ALU.logical_shift_right))
                link(vec.tensor_scalar(y.bitcast(i32), a.bitcast(i32), -1.0, float(RSQRT_MAGIC), ALU.mult, ALU.add))
                for n in range(4):
                    link(vec.scalar_tensor_tensor(a, y, -0.5, y, ALU.mult, ALU.mult))
                    link(vec.tensor_tensor(a, a, v, ALU.mult))
                    link(vec.scalar_tensor_tensor(out_ if n == 3 else y, a, 1.5, y, ALU.add, ALU.mult))
            RSQRT = 14

            dve.wait_ge(S["silu_e"], 1)
            link(vec.tensor_scalar(silu_e, silu_e, 1.0, None, ALU.add))
            link(vec.reciprocal(silu_e, silu_e))
            vec.tensor_tensor(silu_c, silu_c, silu_e, ALU.mult).then_inc(S["silu"], 1)
            dve.wait_ge(S["silu_e"], 2)
            link(vec.tensor_scalar(silu_re, silu_re, 1.0, None, ALU.add))
            link(vec.reciprocal(silu_re, silu_re))
            vec.tensor_tensor(silu_r, silu_r, silu_re, ALU.mult).then_inc(S["silu_rows"], 1)
            dve.wait_ge(S["rows_in"], 32)
            e, z, q = lg_t
            link(vec.tensor_scalar(e, lg_all, -1.0, None, ALU.mult))
            vec.tensor_tensor(e, e, lg_all, ALU.max).then_inc(S["lg_e"], 1)
            dve.wait_ge(S["lg_e"], 2)
            link(vec.tensor_scalar(z, e, 2.0, None, ALU.add))
            link(vec.reciprocal(z, z))
            link(vec.tensor_tensor(z, z, e, ALU.mult))
            link(vec.tensor_tensor(q, z, z, ALU.mult))
            link(vec.tensor_scalar(e, q, 1.0 / 17, 1.0 / 15, ALU.mult, ALU.add))
            for n in (13, 11, 9, 7, 5, 3, 1):
                link(vec.tensor_tensor(e, e, q, ALU.mult))
                link(vec.tensor_scalar(e, e, 1.0 / n, None, ALU.add))
            link(vec.tensor_tensor(e, e, z, ALU.mult))
            link(vec.tensor_scalar(lg_all, lg_all, 0.0, None, ALU.min))
            link(vec.scalar_tensor_tensor(lg_all, e, -2.0, lg_all, ALU.mult, ALU.add))
            for n in range(2):
                last = vec.tensor_tensor_reduce(out=lam_in[:, 2 * n, :], in0=lam_in[:, 2 * n, :], in1=lam_in[:, 2 * n + 1, :],
                                                scale=1.0, scalar=0.0, op0=ALU.mult, op1=ALU.add, accum_out=lam_dot[:, n:n + 1])
            last.then_inc(S["lam_e"], 1)
            dve.wait_ge(S["lam_e"], 2)
            link(vec.tensor_tensor(lam[:, 0:1], lam_dot[:, 1:2], lam_dot[:, 0:1], ALU.subtract))
            vec.tensor_scalar(lam[:, 0:1], lam[:, 0:1], -LAM_INIT, None, ALU.add).then_inc(S["lg_rdy"], 1)
            def ada_row(i, r):
                wait(dve, "ada_mm", i * 2 + r + 1)
                wait(dve, f"mod_out{r}", 16 * i)
                vec.tensor_tensor(mod_rows[:, r, :], bank(r)[0:GROUPS, :], bias_rows[:, r, :], ALU.add).then_inc(S["ada_row"], 1)

            for r in range(2):
                ada_row(0, r)
            dve.wait_ge(S["sumsq"], NT)
            link(vec.tensor_scalar(nt_a[:, 0:NT], ss_x[:, 0:NT], 1.0 / D, EPS, ALU.mult, ALU.add))
            rsqrt(link, rstd_x[:, 0:NT], nt_a[:, 0:NT], nt_y[:, 0:NT], nt_b[:, 0:NT])

            for t in range(NT):
                vec.tensor_scalar(x_sb[:, t, :], x_sb[:, t, :], rstd_x[:, t:t + 1], None, ALU.mult).then_inc(S["xs"], 1)

            with dve.Fori(1, ADA_BLOCKS // 2) as i:
                for r in range(2):
                    ada_row(i, r)

            dve.wait_ge(S["cols_ev"], 1)
            link(vec.tensor_scalar(sub_w, cols[:, SUB:SUB + 1], 1.0 - LAM_INIT, None, ALU.mult))
            for g in range(GROUPS):
                sc = cols[:, (2 * g + 1) * KD:(2 * g + 2) * KD]
                last = vec.scalar_tensor_tensor(sc, sc, 1.0, cols[:, PRE1:PRE1 + KD], ALU.add, ALU.mult)
            last.then_inc(S["a1_cols"], 1)
            dve.wait_ge(S["a1_cols"], 1)
            def h_low_part(k):
                dve.wait_ge(S["h_high"], k + 1)
                vec.tensor_tensor(h_lo[:, k, :], h_tmp[:, k % 2, :], h_hi[:, k, :].bitcast(f32), ALU.subtract).then_inc(S["h_low"], 1)

            for k in range(KD):
                dve.wait_ge(S["xtr"], k + 1)
                wait(dve, "h_low", k - 1)
                for g in range(GROUPS):
                    last = vec.tensor_scalar(h_tmp[:, k % 2, g * SEQ:(g + 1) * SEQ], bank(4 + k % 4)[:, g * SEQ:(g + 1) * SEQ],
                                             cols[:, (2 * g + 1) * KD + k:(2 * g + 1) * KD + k + 1],
                                             cols[:, 2 * g * KD + k:2 * g * KD + k + 1], ALU.mult, ALU.add)
                last.then_inc(S["h_tmp"], 1)
                if k:
                    h_low_part(k - 1)
            h_low_part(KD - 1)
            dve.wait_ge(S["h_low"], KD)

            def decay_logs(a, link):
                wait(dve, "dtab", a)
                dve.sem_inc(S["spare"], 1)
                link(vec.tensor_copy(lg_h, lg_all[:, ds(2 * a, 2)]))
                link(vec.tensor_scalar(decay_log, dist[:, 1, :], lg_h[:, 1:2], None, ALU.mult))
                vec.scalar_tensor_tensor(decay_log, dist[:, 0, :], lg_h[:, 0:1], decay_log, ALU.mult, ALU.add).then_inc(S["dlog"], 1)

            def ret_decay(a, g, link):
                wait(dve, "ret_s", 2 * a + g + 1)
                wait(dve, "dtab", a + 1)
                wait(dve, "ret_v", 2 * (a - 1) + g + 1)
                for s in range(TPG):
                    last = vec.tensor_tensor(ret_p[:, g, s, :], bank(4 + g)[:, s * SEQ:(s + 1) * SEQ],
                                             decay_tab[:, P * (1 - s):P * (1 - s) + SEQ], ALU.mult)
                last.then_inc(S["ret_pd"], 1)

            def dif_soft(a, u, link):
                g, m = groups_of(u)
                units = slice(g * TPG, (g + 1) * TPG)
                wait(dve, "alibi_in", 16 * (a + 1))
                wait(dve, "dif_s", 4 * a + u + 1)
                b = bank(6 + u if u < 2 else 2 + u)
                vec.tensor_tensor(soft[:, units, m, :], b.rearrange("p (t k) -> p t k", t=TPG), alibi, ALU.add)\
                    .then_inc(S["dif_sd"], 1)
                wait(dve, "dif_sd", 4 * a + u + 1)
                link(vec.tensor_reduce(nmax[:, units, m], soft[:, units, m, :], axis=AX, op=ALU.max, negate=True))
                vec.tensor_scalar(nmax[:, units, m], nmax[:, units, m], DQK ** -0.5, None, ALU.mult).then_inc(S["dif_m"], 1)

            def dif_combine(a, u, link):
                wait(dve, "dif_e", 4 * a + u + 1)
                wait(dve, "dif_t", 4 * (a - 1) + u + 1)
                link(vec.reciprocal(coef[:, u, :], esum[:, u, :]))
                vec.tensor_scalar(coef[:, u, 1:2], coef[:, u, 1:2], lam[:, 0:1], None, ALU.mult)
                link(vec.tensor_scalar(attn[:, u, :], soft[:, u, 0, :], coef[:, u, 0:1], None, ALU.mult))
                vec.scalar_tensor_tensor(attn[:, u, :], soft[:, u, 1, :], coef[:, u, 1:2], attn[:, u, :], ALU.mult, ALU.add)\
                    .then_inc(S["dif_c"], 1)

            def ret_norm(a, g, link):
                wait(dve, "ret_v", 2 * a + g + 1)
                wait(dve, "out_t", 2 * a)
                for tt in range(TPG):
                    last = vec.bn_stats(bn6[:, g * TPG + tt, :], bank(6 + g)[:, tt * P:(tt + 1) * P])
                link(last, alone=True)
                for tt in range(TPG):
                    last = vec.bn_aggr(mv[:, g * TPG + tt, :], bn6[:, g * TPG + tt, :])
                link(last)
                link(vec.tensor_scalar(nt_a[:, 0:TPG], mv[:, g * TPG:(g + 1) * TPG, 1], EPS, None, ALU.add))
                rsqrt(link, nt_y[:, 4:4 + TPG], nt_a[:, 0:TPG], nt_y[:, 0:TPG], nt_b[:, 0:TPG])
                for tt in range(TPG):
                    t = g * TPG + tt
                    last = vec.tensor_scalar(ret_o[:, t, :], bank(6 + g)[:, tt * P:(tt + 1) * P], mv[:, t, 0:1],
                                             nt_y[:, 4 + tt:5 + tt], ALU.subtract, ALU.mult)
                link(last)
                vec.tensor_tensor(ret_o[:, g * TPG:(g + 1) * TPG, :], ret_o[:, g * TPG:(g + 1) * TPG, :],
                                  gate[:, g * TPG:(g + 1) * TPG, :], ALU.mult).then_inc(S["ret_n"], 1)

            def dif_norm(a, pair, link):
                wait(dve, "dif_sq", 4 * a + 2 * pair + 2)
                wait(dve, "out_t", 2 * a)
                link(vec.tensor_scalar(nt_a[:, 0:2], dif_ss[:, 2 * pair:2 * pair + 2], 1.0 / P, EPS, ALU.mult, ALU.add))
                rsqrt(link, nt_y[:, 4:6], nt_a[:, 0:2], nt_y[:, 0:2], nt_b[:, 0:2])
                for j in range(2):
                    vec.tensor_scalar(diff_o[:, 2 * pair + j, :], bank(6 + j)[:, 0:P], nt_y[:, 4 + j:5 + j], None, ALU.mult)\
                        .then_inc(S["dif_n"], 1)

            def silu_gate(h, t, link):
                wait(dve, "proj_ev", 8 * h + 5 + t)
                link(vec.tensor_scalar(e_g[:, t, :], e_g[:, t, :], 1.0, None, ALU.add))
                link(vec.reciprocal(e_g[:, t, :], e_g[:, t, :]))
                vec.tensor_tensor(gate[:, t, :], e_g[:, t, :], bank(t)[:, P:2 * P], ALU.mult).then_inc(S["gate"], 1)

            def late_pieces(h, pieces):
                for n in pieces:
                    c, half, place = n // 2, n % 2, n % 4
                    w = col_ring[:, place, :]
                    silu = [silu_b[:, g, half * PIECE:(half + 1) * PIECE] for g in range(GROUPS)]
                    wait(dve, f"col_in{place}", 16 * (h * (PIECES // 4) + n // 4 + 1))
                    wait(dve, "col_used", h * PIECES + n)
                    vec.tensor_tensor_reduce(out=products, in0=w, in1=silu[0], scale=1.0, scalar=0.0, op0=ALU.mult, op1=ALU.add,
                                             accum_out=mod_part[:, half, 0, c:c + 1]).then_inc(S["col_a"], 1)
                    wait(dve, "col_a", h * PIECES + n + 1)
                    vec.tensor_tensor_reduce(out=w, in0=w, in1=silu[1], scale=1.0, scalar=0.0, op0=ALU.mult, op1=ALU.add,
                                             accum_out=mod_part[:, half, 1, c:c + 1]).then_inc(S["col_used"], 1)

            def late_sums(h, link):
                wait(dve, "col_used", (h + 1) * PIECES)
                dve.sem_inc(S["spare"], 1)
                link(vec.tensor_tensor(mod_cols[:, :, ds(h * 8, 8)], mod_part[:, 0, :, :], mod_part[:, 1, :, :], ALU.add))

            def head_step(h, a, link):
                def step(f, *units):
                    if a is not None:
                        for u in units:
                            f(a, u, link)

                def late(*pieces):
                    if h is not None:
                        late_pieces(h, pieces)

                def gates_of(*tiles):
                    if h is not None:
                        for t in tiles:
                            silu_gate(h, t, link)
                step(ret_decay, 0, 1)
                step(dif_soft, 0, 1)
                late(0, 1, 2)
                step(dif_soft, 2, 3)
                late(3, 4, 5)
                step(dif_combine, 0, 1)
                late(6)
                step(ret_norm, 0, 1)
                late(7, 8, 9)
                step(dif_combine, 2, 3)
                late(10, 11)
                step(dif_norm, 0)
                late(12, 13)
                step(dif_norm, 1)
                late(14, 15)
                gates_of(0, 1, 2, 3)
                if h is not None:
                    late_sums(h, link)
                    decay_logs(h, link)

            def plain(ins, alone=False):
                link(ins)

            dve.wait_ge(S["rows_in"], 48)
            head_step(0, None, plain)
            head_step(1, 0, plain)
            PER_HEAD = 1 + 4 + 8 + 2 * (3 + RSQRT + 1) + 2 * (1 + RSQRT) + 8 + 2
            with dve.Fori(2, HEADS) as h:
                c = Chain(chain[0] - 2 * PER_HEAD, h, PER_HEAD)
                head_step(h, h - 1, c)
                c.done()
            chain[0] += (HEADS - 2) * PER_HEAD
            dve.sem_inc(S["late_cols"], 1)
            head_step(None, HEADS - 1, plain)
            dve.wait_ge(S["late_t"], 1)
            dve.wait_ge(S["bias_in"], 32)
            vec.tensor_tensor(mod_late, bank(7)[:, 0:P], mod_bias, ALU.add).then_inc(S["late_row"], 1)
            for n, heads in enumerate((slice(0, HEADS - 1), slice(HEADS - 1, HEADS))):
                for w in range(2):
                    ks = slice(w * HEADS + heads.start, w * HEADS + heads.stop)
                    dve.wait_ge(S["mix_hi"], 2 * n + w + 1)
                    vec.tensor_tensor(mix_lo[:, ks, :], mix_t[:, ks, :], mix_hi[:, ks, :].bitcast(f32), ALU.subtract)\
                        .then_inc(S["mix_lo"], 1)

            def coef_products(g):
                vec.tensor_tensor(coefs[g][0], coefs[g][0], post1_sb, ALU.mult).then_inc(S["coef"], 1)
                vec.scalar_tensor_tensor(coefs[g][1], coefs[g][1], 1.0, pre2_sb, ALU.add, ALU.mult).then_inc(S["coef"], 1)

            dve.wait_ge(S["coef_in"], 16 * 5)
            coef_products(1)

            with dve.Fori(0, D // WOC // 2) as i:
                for t in range(NT):
                    wait_alone(dve, "wo_mm", (2 * i + 1) * NT + t + 1)
                    vec.tensor_copy(o_sb[:, t, ds((2 * i + 1) * WOC, WOC)], bank(4 + t)[:, 0:WOC]).then_inc(S["wo_dve"], 1)

            dve.wait_ge(S["gate1_in"], 32)
            coef_products(0)
            dve.wait_ge(S["o_sq"], NT)
            link(vec.tensor_scalar(nt_a[:, 0:NT], ss_x[:, 0:NT], 1.0 / D, EPS, ALU.mult, ALU.add))
            rsqrt(link, rstd_x[:, 0:NT], nt_a[:, 0:NT], nt_y[:, 0:NT], nt_b[:, 0:NT])
            for g in range(GROUPS):
                gate1_sb, scale2_sb, shift2_sb = coefs[g]
                dve.wait_ge(S["coef"], 2 * GROUPS)
                if g:
                    dve.wait_ge(S["shift2_in"], 16)
                for tt in range(TPG):
                    t = g * TPG + tt
                    link(vec.scalar_tensor_tensor(o_sb[:, t, :], o_sb[:, t, :], rstd_x[:, t:t + 1], gate1_sb, ALU.mult, ALU.mult))
                    dve.wait_ge(S["x_in"], 16 * 2 * NT)
                    vec.tensor_tensor(x_sb[:, t, :], x_sb[:, t, :], o_sb[:, t, :], ALU.add).then_inc(S["x1"], 1)
                tiles = slice(4 + g * TPG, 4 + (g + 1) * TPG)
                dve.wait_ge(S["x1_sq"], (g + 1) * TPG)
                link(vec.tensor_scalar(nt_a[:, 0:TPG], ss_x[:, tiles], 1.0 / D, EPS, ALU.mult, ALU.add))
                rsqrt(link, rstd_x[:, tiles], nt_a[:, 0:TPG], nt_y[:, 0:TPG], nt_b[:, 0:TPG])
                for tt in range(TPG):
                    t = g * TPG + tt
                    link(vec.scalar_tensor_tensor(o_sb[:, t, :], x_sb[:, t, :], rstd_x[:, 4 + t:5 + t], scale2_sb, ALU.mult, ALU.mult))
                    vec.tensor_tensor(o_sb[:, t, :], o_sb[:, t, :], shift2_sb, ALU.add).then_inc(S["h2"], 1)
                dve.wait_ge(S["h2"], TPG * (g + 1))
                dve.sem_inc(S["grp_done"], 1)

            def top16(values, work, best, where, link):
                for t in range(NT):
                    last = vec.max(best[:, t, 0:8], values(t))
                link(last, alone=True)
                for t in range(NT):
                    last = vec.match_replace(work(t), best[:, t, 0:8], values(t), LOWEST)
                link(last, alone=True)
                for t in range(NT):
                    last = vec.max(best[:, t, 8:16], work(t))
                link(last, alone=True)
                for t in range(NT):
                    vec.max_index(where[:, t, 8:16], best[:, t, 8:16], work(t))
                for t in range(NT):
                    last = vec.max_index(where[:, t, 0:8], best[:, t, 0:8], values(t))
                return last

            def route_head(i, r, link):
                hd = i * 2 + r
                for m in range(2):
                    b = bank(2 + m + 4 * r)
                    wait_alone(dve, "sc_mm", 2 * hd + m + 1)
                    top16(lambda t: b[:, t * P:(t + 1) * P], lambda t: masked[:, t, 0:NKEYS], top_v[:, m], top_i[:, m], link)\
                        .then_inc(S["sc_dve"], 1)
                wait(dve, "sc_dve", 2 * hd + 2)
                link(vec.tensor_copy(top_if, top_i))
                pairs = [P, NT, TOPK, TOPK]
                link(vec.tensor_tensor(cand.rearrange("p t (i j) -> p t i j", i=TOPK), top_v[:, 0].unsqueeze(3).to_broadcast(pairs),
                                       top_v[:, 1].unsqueeze(2).to_broadcast(pairs), ALU.add), alone=True)
                link(top16(lambda t: cand[:, t, :], lambda t: masked[:, t, :], best_v, best_p, link))
                hot = onehot.rearrange("p (t k i) -> p t k i", t=NT, k=TOPK)
                for m in range(2):
                    op, by = (ALU.bitwise_and, TOPK - 1) if m else (ALU.logical_shift_right, 4)
                    link(vec.tensor_scalar(part_u, best_p.rearrange("p t k -> p (t k)"), by, None, op))
                    link(vec.tensor_copy(part_f, part_u))
                    link(vec.tensor_tensor(hot, part_f.rearrange("p (t k) -> p t k", t=NT).unsqueeze(3).to_broadcast(pairs),
                                           iota16.unsqueeze(1).unsqueeze(1).to_broadcast(pairs), ALU.is_equal))
                    link(vec.tensor_tensor(hot, hot, top_if[:, m].unsqueeze(2).to_broadcast(pairs), ALU.mult))
                    link(vec.tensor_reduce(pick[:, m], hot, axis=AX, op=ALU.add))
                link(vec.scalar_tensor_tensor(pair_id.rearrange("p t k -> p (t k)"), pick[:, 0].rearrange("p t k -> p (t k)"),
                                              float(NKEYS), pick[:, 1].rearrange("p t k -> p (t k)"), ALU.mult, ALU.add), alone=True)
                for m in range(2):
                    vec.tensor_copy(slot_keys[:, m, :, ds(hd * TOPK, TOPK)], pick[:, m])
                vec.tensor_copy(eidx[:, :, ds(hd * TOPK, TOPK)], pair_id)
                link(vec.tensor_tensor(gates[:, :, ds(hd * TOPK, TOPK)], best_v, best_v[:, :, 0:1].to_broadcast([P, NT, TOPK]),
                                       ALU.subtract))
            PER_ROUTE = 3 * 3 + 4 + 10 + 1 + 0

            with dve.Fori(0, PEER_HEADS // 2) as i:
                c = Chain(chain[0], i, 2 * PER_ROUTE)
                for r in range(2):
                    route_head(i, r, c)
                c.done()
            chain[0] += PEER_HEADS * PER_ROUTE
            dve.sem_inc(S["gl_in"], 1)
            dve.wait_ge(S["h2_hi"], 1)
            vec.tensor_tensor(h2_lo[:, :, :], h2_t[:, :, GATHERED * P:T], h2_hi[:, :, :].bitcast(f32), ALU.subtract).then_inc(S["h2_lo"], 1)
            dve.wait_ge(S["gl_exp"], 1)
            by_head = gates.rearrange("p t (h k) -> p (t h) k", k=TOPK)
            sums = soft_e[:, 0:NT * PEER_HEADS]
            link(vec.tensor_reduce(sums, by_head, axis=AX, op=ALU.add))
            link(vec.reciprocal(sums, sums))
            link(vec.tensor_tensor(by_head, by_head, sums.unsqueeze(2).to_broadcast([P, NT * PEER_HEADS, TOPK]), ALU.mult))
            dve.sem_inc(S["g_fin"], 1)

            for name, n in (("g_ev", 4), ("g_mm", 4), ("g_out", 1), ("gelu", 2), ("gr_used", RING), ("hid_rdy", 1), ("w_rdy", 2)):
                dve.sem_inc(S[name], n)

            dve.wait_ge(S["bs_ev"], 1)
            with dve.Fori(0, DT * P // 16) as i:
                for s in range(4):
                    wait_alone(dve, "g_mm", i * 4 + s + 1)
                    shape = [P, 2, 4, NKEYS]
                    vec.tensor_tensor(hot[:, s, :, :, :], iota[:, :].unsqueeze(1).unsqueeze(1).to_broadcast(shape),
                                      by_slot[:, 0:2, ds(i * 16 + s * 4, 4)].unsqueeze(3).to_broadcast(shape), ALU.is_equal)\
                        .then_inc(S["g_ones"], 1)

            def low_part(n, r):
                wait(dve, "raw_hi", n + 1)
                vec.tensor_tensor(raw_lo[:, r, :], raw_ring[:, r, :], raw_hi[:, r, :].bitcast(f32), ALU.subtract).then_inc(S["raw_lo"], 1)

            def up_weights(n, r, uses):
                wait(dve, "gelu", n + 3)
                wait(dve, f"rg_in{r}", 16 * (uses + 1))
                wait(dve, f"w_out{r}", 16 * uses)
                vec.tensor_tensor(w_ring[:, r, :], gelu_sb[:, r, :], g_ring[:, r, :], ALU.mult).then_inc(S["w_rdy"], 1)

            def dot(i, j):
                if j == 0:
                    wait_alone(dve, "hid_rdy", i + 1)
                wait(dve, f"gr_in{j}", 16 * (i + 1))
                vec.tensor_tensor_reduce(out=gather_ring[:, j, :], in0=gather_ring[:, j, :], in1=psum[:, 0:D], scale=1.0, scalar=0.0,
                                         op0=ALU.mult, op1=ALU.add, accum_out=hid[:, j:j + 1]).then_inc(S["gr_used"], 1)

            def dots_done(i):
                wait_alone(dve, "gr_used", (i + 2) * RING)
                vec.tensor_copy(hid_all[:, ds(i * RING, RING)], hid).then_inc(S["hid_rdy"], 1)

            dve.wait_ge(S["h2_ps"], 1)
            dve.wait_ge(S["g_quarter2"], 16)
            for r in range(2):
                low_part(r, r)
            for j in range(2):
                dot(0, j)
            for j in range(2, RING):
                low_part(j, j % 2)
                dot(0, j)
                up_weights(j - 2, j % 2, 0)
            dots_done(0)
            with dve.Fori(1, SLOTS // RING) as i:
                for j in range(RING):
                    n = i * RING + j
                    wait(dve, "up_mm", n - 1)
                    low_part(n, j % 2)
                    dot(i, j)
                    up_weights(n - 2, j % 2, i * 2 + j // 2 - 1)
                dots_done(i)
            for r in range(2):
                up_weights(NKEYS - 2 + r, r, NKEYS // 2 - 1)
            vec.memset(acc, 0.0)
            dve.wait_ge(S["hid_gelu"], 1)
            link(vec.tensor_tensor(hid_all, hid_all, gates[:, 0, :], ALU.mult))

            def down_low(n, r):
                wait(dve, "down_mm", n - 1)
                low_part(NKEYS + n, r)
                wait(dve, "whi", n + 1)
                vec.tensor_tensor(w_lo[:, r, :, :], wraw_ring[:, r, :, :], w_hi[:, r, :, :].bitcast(f32), ALU.subtract).then_inc(S["wlo"], 1)

            def accumulate(i, j):
                wait(dve, f"gr_in{j}", 16 * (SLOTS // RING + i + 1))
                wait_alone(dve, "gr_used", SLOTS + RING + i * RING + j)
                vec.scalar_tensor_tensor(acc, gather_ring[:, j, :], hid_all[:, ds(i * RING + j, 1)], acc, ALU.mult, ALU.add)\
                    .then_inc(S["gr_used"], 1)

            for j in range(RING):
                down_low(j, j % 2)
                accumulate(0, j)
            with dve.Fori(1, SLOTS // RING) as i:
                for j in range(RING):
                    down_low(i * RING + j, j % 2)
                    accumulate(i, j)

            dve.wait_ge(S["fin_in"], 16 * (1 + GROUPS))
            for g in range(GROUPS):
                link(vec.tensor_tensor(gate2_sb[g], gate2_sb[g], post2_sb, ALU.mult))
            dve.wait_ge(S["acc_sq"], NT)
            link(vec.tensor_scalar(nt_a[:, 0:NT], ss_out[:, 0:NT], 1.0 / D, EPS, ALU.mult, ALU.add))
            rsqrt(link, nt_y[:, 4:4 + NT], nt_a[:, 0:NT], nt_y[:, 0:NT], nt_b[:, 0:NT])
            for t in range(NT):
                y = acc if t == 0 else y_dense[:, t - 1, :]
                o = out2_sb if t % 2 else out_sb
                wait(dve, f"y_out{t % 2}", 16 * (t // 2))
                link(vec.scalar_tensor_tensor(o, y, nt_y[:, 4 + t:5 + t], gate2_sb[t // TPG], ALU.mult, ALU.mult))
                vec.tensor_tensor(o, o, x_sb[:, t, :], ALU.add).then_inc(S["y"], 1)

        @block.gpsimd
        def _(pool):
            def gathers(table, before, i, parity):
                nc.gpsimd.tensor_copy(stage[parity], eidx[:, 0, ds(i * RING, RING)]).then_inc(S["stage"], 1)
                wait_alone(pool, "stage", before + i + 1)
                for j in range(RING):
                    wait_alone(pool, "gr_used", (before + i) * RING + j + 1)
                    pool.indirect_dma_start(out=gather_ring[:, j, :], out_offset=None, in_=table,
                                            in_offset=bass.IndirectOffsetOnAxis(ap=stage[parity][:, j:j + 1], axis=0))\
                        .then_inc(S[f"gr_in{j}"], 16)

            with pool.Fori(0, HEADS) as h:
                for n in range(8):
                    wait(pool, "w_high", 8 * h + n + 1)
                    w = WT if n < 4 else WV
                    nc.gpsimd.tensor_tensor(w_low[:, n % 2, 0:w], w_raw[:, n % 2, 0:w], w_high[:, n % 2, 0:w].bitcast(f32), ALU.subtract)\
                        .then_inc(S["w_low"], 1)

            with pool.Fori(0, D // WOC) as b:
                for half in range(2):
                    wait(pool, "w_high", 8 * HEADS + 2 * b + half + 1)
                    nc.gpsimd.tensor_tensor(w_low[:, half, :], w_raw[:, half, :], w_high[:, half, :].bitcast(f32), ALU.subtract)\
                        .then_inc(S["w_low"], 1)

            with pool.Fori(0, DT * P // 16) as i:
                for s in range(4):
                    wait_alone(pool, "g_ones", i * 4 + s + 1)
                    gate_of = by_slot[:, 2, ds(i * 16 + s * 4, 4)].unsqueeze(2).to_broadcast([P, 4, NKEYS])
                    nc.gpsimd.tensor_tensor(hot[:, s, 1, :, :], hot[:, s, 1, :, :], gate_of, ALU.mult).then_inc(S["g_hot"], 1)

            for r in range(2):
                pool.wait_ge(S[f"ru_in{r}"], 16)
            pool.wait_ge(S["g_mm"], DT * P // 4 + 4)
            pool.wait_ge(S["g_hot"], DT * P // 4)
            for before, table in ((0, u_tab), (SLOTS // RING, v_tab)):
                with pool.Fori(0, SLOTS // RING // 2) as i:
                    for parity in range(2):
                        gathers(table, before, 2 * i + parity, parity)


_INS = ["x", "ct", "c_rows", "ada_w", "ada_wt", "ada_b", "rows", "w_t", "w_v", "w_o", "w_q", "keys_t", "decay", "lams", "post1", "pre2", "post2",
        "u_t", "u_tab", "v_tab", "ident", "dist", "alibi", "iota"]


def constants():
    s = np.arange(P)[:, None]
    rel = np.arange(384)[None, :] - P - s
    dist = np.stack([np.maximum(rel, 0), np.maximum(-rel, 0)], 1).astype(np.float32)
    slopes = 2.0 ** (-8.0 * np.arange(1, HEADS + 1) / HEADS)
    q = np.arange(SEQ).reshape(TPG, P).T
    away = np.abs(q[:, :, None] - np.arange(SEQ)[None, None, :])
    alibi = (-slopes[:, None, None, None] * DQK ** 0.5 * away[None]).astype(np.float32)
    return {"ident": np.eye(P, dtype=np.float32), "dist": dist, "alibi": alibi,
            "iota": np.tile(np.arange(NKEYS, dtype=np.float32), (P, 1))}


def lay_out(i):
    w_in = i["w_in"][0].reshape(KD, P, 7, HEADS, P)
    rq, rk, rv, rg, dq, dk, dv = (w_in[:, :, n] for n in range(7))

    def blocks(w, n):
        return w.reshape(KD, P, w.shape[1] // n, n).transpose(2, 1, 0, 3)
    a = {
        "x": np.concatenate([i["x_prompt"][0], i["x_sample"][0]], 0),
        "ct": np.concatenate([i["c_prompt"], i["c_sample"]], 0).reshape(GROUPS, KD, P).transpose(2, 1, 0).reshape(P, -1),
        "c_rows": np.concatenate([i["c_prompt"], i["c_sample"]], 0).reshape(GROUPS * KD, P),
        "ada_w": blocks(i["ada_w"][0][:, 0:2 * D], NB),
        "ada_wt": i["ada_w"][0][:, 2 * D:].T.reshape(HEADS, 8, P, 2, PIECE),
        "ada_b": i["ada_b"],
        "rows": np.concatenate([i["mix_pre_w"][0].reshape(KD, P), i["ret_gn_w"][0].reshape(HEADS, P), i["diff_subln_w"]], 0),
        "w_t": np.stack([rk, rq, dk, dq], 0).transpose(3, 0, 2, 1, 4),
        "w_v": np.stack([rv, rg, dv], 3).transpose(2, 0, 1, 3, 4).reshape(HEADS, 4, 4, P, 3 * P).transpose(0, 1, 3, 2, 4),
        "w_o": blocks(i["w_out"][0], WOC).reshape(D // WOC, P, 2, KD // 2, WOC).transpose(0, 2, 1, 3, 4),
        "w_q": blocks(i["peer_w_query"][0], 2 * P),
        "keys_t": i["peer_sub_keys"][0].transpose(3, 0, 1, 2).reshape(P, -1),
        "decay": np.stack([i["ret_decay_fwd"][0], i["ret_decay_bwd"][0]], 1).reshape(1, -1),
        "lams": np.concatenate([i["diff_lambda_q1"], i["diff_lambda_k1"], i["diff_lambda_q2"], i["diff_lambda_k2"]], 1),
        "post1": i["mix_post_w"], "pre2": i["ffn_pre_w"], "post2": i["ffn_post_w"],
        "u_t": i["peer_u"][0].reshape(NKEYS, NKEYS, KD, P).transpose(0, 3, 2, 1).reshape(NKEYS, P, -1),
        "u_tab": i["peer_u"][0], "v_tab": i["peer_v"][0],
    }
    return {**a, **constants()}


def kernel(**inputs):
    import concourse.bacc as bacc
    from concourse import mybir
    from concourse.bass_utils import run_bass_kernel_spmd

    nc = bacc.Bacc("TRN2", target_bir_lowering=False, num_devices=1)
    laid = lay_out({k: np.asarray(v) for k, v in inputs.items()})
    arrays, args = {}, []
    for name in _INS:
        a = np.ascontiguousarray(laid[name])
        arrays[f"in_{name}"] = a
        args.append(nc.dram_tensor(f"in_{name}", a.shape, mybir.dt.from_np(a.dtype), kind="ExternalInput").ap())
    out = nc.dram_tensor("out_0", (T, D), mybir.dt.float32, kind="ExternalOutput").ap()
    mod_d = nc.dram_tensor("mod_scratch", (GROUPS, MODS * D), mybir.dt.float32).ap()
    silu_d = nc.dram_tensor("silu_scratch", (GROUPS, D), mybir.dt.float32).ap()
    mix_d = nc.dram_tensor("mix_scratch", (2, HEADS, P, T), mybir.dt.float32).ap()
    g_d = nc.dram_tensor("table_scratch", (NKEYS, P, ND), mybir.dt.float32).ap()
    w_d = nc.dram_tensor("weights_scratch", (NKEYS, P, ND), mybir.dt.float32).ap()
    build_program(nc, *args, out, mod_d, silu_d, mix_d, g_d, w_d)
    got = run_bass_kernel_spmd(nc, [arrays], core_ids=[0]).results[0]["out_0"]
    return got[0:SEQ][None], got[SEQ:T][None]
```
